# Optimizing a Trainium2 kernel written in Bass

```python
import math
import jax
import jax.numpy as jnp
from jax import lax
import numpy as np

D_MODEL = 1024
BATCH = 1
SEQ = 256
DEPTH = 2

GRID_W = 64
CTX_LEN = 256
EPS = 1e-6
ROPE_BASE = 10000.0
Q_BLOCK = 128

DIFF_HEADS = 4
DIFF_DIM = 64
DIFF_VDIM = 2 * DIFF_DIM
MLA_HEADS = 4
MLA_Q_RANK = 256
MLA_KV_RANK = 128
MLA_NOPE = 64
MLA_ROPE = 32
MLA_QK = MLA_NOPE + MLA_ROPE
MLA_VDIM = 128
EV_QA = DIFF_HEADS * 2 * DIFF_DIM
EV_VA = DIFF_HEADS * DIFF_VDIM
EV_SPLITS = (EV_QA, 2 * EV_QA, 2 * EV_QA + EV_VA, 2 * EV_QA + EV_VA + MLA_Q_RANK,
             2 * EV_QA + EV_VA + MLA_Q_RANK + MLA_KV_RANK)
EV_IN = EV_SPLITS[-1] + MLA_ROPE
EV_MIX = EV_VA + MLA_HEADS * MLA_VDIM

DN_HEADS = 8
DN_DK = 128
DN_DV = 128
DN_CONV = 5
DN_CHUNK = 64
DN_QKV = 2 * DN_HEADS * DN_DK + DN_HEADS * DN_DV
DN_V = DN_HEADS * DN_DV
DN_IN = DN_QKV + DN_V + 4 * DN_HEADS
DN_MIX = DN_V

PEER_HEADS = 8
PEER_NKEYS = 128
PEER_N = PEER_NKEYS * PEER_NKEYS
PEER_DKEY = 128
PEER_TOPK = 16
PEER_BLOCK = 128

kernel_name = 'hybrid_diffusion_trunk'

def _rms(x, g=None):
    xf = x.astype(jnp.float32)
    y = xf * lax.rsqrt(jnp.mean(xf * xf, axis=-1, keepdims=True) + EPS)
    if g is not None:
        y = y * g.astype(jnp.float32)
    return y.astype(x.dtype)

def _l2n(x):
    xf = x.astype(jnp.float32)
    return (xf * lax.rsqrt(jnp.sum(xf * xf, axis=-1, keepdims=True) + EPS)).astype(x.dtype)

def _axial_rope(rows, rot_dim):
    r = jnp.broadcast_to(jnp.arange(rows, dtype=jnp.float32)[:, None], (rows, GRID_W)).reshape(-1)
    cl = jnp.broadcast_to(jnp.arange(GRID_W, dtype=jnp.float32)[None, :], (rows, GRID_W)).reshape(-1)
    nf = rot_dim // 4
    inv = ROPE_BASE ** (-jnp.arange(nf, dtype=jnp.float32) / nf)
    ang = jnp.concatenate([r[:, None] * inv, cl[:, None] * inv], axis=-1)
    return jnp.cos(ang), jnp.sin(ang)

def _rope(x, cs):
    cos, sin = cs
    h = x.shape[-1] // 2
    x1 = x[..., :h].astype(jnp.float32)
    x2 = x[..., h:].astype(jnp.float32)
    return jnp.concatenate([x1 * cos - x2 * sin, x1 * sin + x2 * cos], axis=-1).astype(x.dtype)

def _attend(q, k, v):
    b, h, s, d = q.shape
    nb = s // Q_BLOCK
    qb = jnp.moveaxis(q.reshape(b, h, nb, Q_BLOCK, d), 2, 0)
    scale = d ** -0.5

    def blk(qi):
        sc = jnp.einsum('bhqd,bhkd->bhqk', qi, k).astype(jnp.float32) * scale
        p = jax.nn.softmax(sc, axis=-1)
        return jnp.einsum('bhqk,bhkd->bhqd', p.astype(v.dtype), v)

    out = lax.map(blk, qb)
    return jnp.moveaxis(out, 0, 2).reshape(b, h, s, v.shape[-1])

def _even_heads(h, w_in, q_norm, k_norm, cq_norm, ckv_norm, w_uq, w_ukv, mq_norm, mk_norm, rope_a, rope_b):
    B, S, _ = h.shape
    qa, ka, va, cq, ckv, kr = jnp.split(h @ w_in, EV_SPLITS, axis=-1)
    qa = _rms(qa.reshape(B, S, DIFF_HEADS, 2, DIFF_DIM), q_norm).transpose(0, 2, 3, 1, 4)
    ka = _rms(ka.reshape(B, S, DIFF_HEADS, 2, DIFF_DIM), k_norm).transpose(0, 2, 3, 1, 4)
    va = va.reshape(B, S, DIFF_HEADS, DIFF_VDIM).transpose(0, 2, 1, 3)
    qb = (_rms(cq, cq_norm) @ w_uq).reshape(B, S, MLA_HEADS, MLA_QK)
    kvb = (_rms(ckv, ckv_norm) @ w_ukv).reshape(B, S, MLA_HEADS, MLA_NOPE + MLA_VDIM)
    kb = jnp.concatenate([kvb[..., :MLA_NOPE],
                          jnp.broadcast_to(kr[:, :, None, :], (B, S, MLA_HEADS, MLA_ROPE))], axis=-1)
    vb = kvb[..., MLA_NOPE:].transpose(0, 2, 1, 3)
    qb = _rms(qb, mq_norm).transpose(0, 2, 1, 3)
    kb = _rms(kb, mk_norm).transpose(0, 2, 1, 3)
    if rope_a is not None:
        qa = _rope(qa, rope_a)
        ka = _rope(ka, rope_a)
        qb = jnp.concatenate([qb[..., :MLA_NOPE], _rope(qb[..., MLA_NOPE:], rope_b)], axis=-1)
        kb = jnp.concatenate([kb[..., :MLA_NOPE], _rope(kb[..., MLA_NOPE:], rope_b)], axis=-1)
    return qa, ka, va, qb, kb, vb

def _even_out(qa, qb, k1, k2, va, kb, vb, lam, lam_init, subln, w_out):
    o1 = _attend(qa[:, :, 0], k1, va)
    o2 = _attend(qa[:, :, 1], k2, va)
    oa = _rms(o1 - lam.astype(o1.dtype) * o2, subln) * (1.0 - lam_init)
    ob = _attend(qb, kb, vb)
    o = jnp.concatenate([oa, ob], axis=1)
    B, _, S, _ = o.shape
    return o.transpose(0, 2, 1, 3).reshape(B, S, EV_MIX) @ w_out

def _even_mixer(hx, hc, w_in, w_out, q_norm, k_norm, lq1, lk1, lq2, lk2, subln,
                cq_norm, ckv_norm, w_uq, w_ukv, mq_norm, mk_norm, lam_init, rope_a, rope_b, with_ctx):
    qa_x, ka_x, va_x, qb_x, kb_x, vb_x = _even_heads(hx, w_in, q_norm, k_norm, cq_norm, ckv_norm,
                                                     w_uq, w_ukv, mq_norm, mk_norm, rope_a, rope_b)
    qa_c, ka_c, va_c, qb_c, kb_c, vb_c = _even_heads(hc, w_in, q_norm, k_norm, cq_norm, ckv_norm,
                                                     w_uq, w_ukv, mq_norm, mk_norm, None, None)
    lam = (jnp.exp(jnp.sum(lq1.astype(jnp.float32) * lk1.astype(jnp.float32)))
           - jnp.exp(jnp.sum(lq2.astype(jnp.float32) * lk2.astype(jnp.float32))) + lam_init)
    cat = lambda a, b: jnp.concatenate([a, b], axis=2)
    ox = _even_out(qa_x, qb_x, cat(ka_c[:, :, 0], ka_x[:, :, 0]), cat(ka_c[:, :, 1], ka_x[:, :, 1]),
                   cat(va_c, va_x), cat(kb_c, kb_x), cat(vb_c, vb_x), lam, lam_init, subln, w_out)
    oc = None
    if with_ctx:
        oc = _even_out(qa_c, qb_c, ka_c[:, :, 0], ka_c[:, :, 1], va_c, kb_c, vb_c, lam, lam_init, subln, w_out)
    return ox, oc

def _dwconv(x, w):
    return lax.conv_general_dilated(x, w[:, None, :].astype(x.dtype), (1,), [(DN_CONV // 2, DN_CONV // 2)],
                                    dimension_numbers=('NWC', 'WIO', 'NWC'), feature_group_count=x.shape[-1])

def _dn_project(h, w_in, conv_w, a_log, dt_bias):
    B, S, _ = h.shape
    z = h @ w_in
    qkv = jax.nn.silu(_dwconv(z[..., :DN_QKV], conv_w))
    nq = DN_HEADS * DN_DK
    q = _l2n(qkv[..., :nq].reshape(B, S, DN_HEADS, DN_DK)) * (DN_DK ** -0.5)
    k = _l2n(qkv[..., nq:2 * nq].reshape(B, S, DN_HEADS, DN_DK))
    v = qkv[..., 2 * nq:].reshape(B, S, DN_HEADS, DN_DV)
    zg = z[..., DN_QKV:DN_QKV + DN_V]
    ab = z[..., DN_QKV + DN_V:].astype(jnp.float32).reshape(B, S, 2, 2, DN_HEADS)
    g = -jnp.exp(a_log) * jax.nn.softplus(ab[:, :, 0] + dt_bias)
    beta = jax.nn.sigmoid(ab[:, :, 1])
    hd = lambda t: t.transpose(0, 2, 1, 3)
    return hd(q), hd(k), hd(v), zg, g.transpose(2, 0, 3, 1), beta.transpose(2, 0, 3, 1)

def _gated_delta_chunked(q, k, v, g, beta, s0):
    B, H, S, _ = q.shape
    dv = v.shape[-1]
    C = DN_CHUNK
    n = S // C
    q, k, v = (t.astype(jnp.float32).reshape(B, H, n, C, -1) for t in (q, k, v))
    gc = jnp.cumsum(g.astype(jnp.float32).reshape(B, H, n, C), axis=-1)
    beta = beta.astype(jnp.float32).reshape(B, H, n, C)
    idx = jnp.arange(C)
    lower = idx[:, None] >= idx[None, :]
    strict = idx[:, None] > idx[None, :]
    decay = jnp.exp(jnp.where(lower, gc[..., :, None] - gc[..., None, :], -jnp.inf))
    kb = k * beta[..., None]
    L = jnp.where(strict, jnp.einsum('bhnid,bhnjd->bhnij', kb, k) * decay, 0.0)
    rhs = jnp.concatenate([v * beta[..., None], kb * jnp.exp(gc)[..., None]], axis=-1)
    sol = lax.linalg.triangular_solve(jnp.eye(C, dtype=jnp.float32) + L, rhs,
                                      left_side=True, lower=True, unit_diagonal=True)
    u, w = sol[..., :dv], sol[..., dv:]
    a_qk = jnp.where(lower, jnp.einsum('bhnid,bhnjd->bhnij', q, k) * decay, 0.0)
    q_dec = q * jnp.exp(gc)[..., None]
    k_dec = k * jnp.exp(gc[..., -1:] - gc)[..., None]
    g_last = jnp.exp(gc[..., -1])

    def step(s, xs):
        qd, kd, uu, ww, aa, gl = xs
        v_new = uu - jnp.einsum('bhcd,bhde->bhce', ww, s)
        o = jnp.einsum('bhcd,bhde->bhce', qd, s) + jnp.einsum('bhij,bhje->bhie', aa, v_new)
        s = s * gl[..., None, None] + jnp.einsum('bhcd,bhce->bhde', kd, v_new)
        return s, o

    xs = tuple(jnp.moveaxis(t, 2, 0) for t in (q_dec, k_dec, u, w, a_qk, g_last))
    s_fin, o = lax.scan(step, s0.astype(jnp.float32), xs)
    return jnp.moveaxis(o, 0, 2).reshape(B, H, S, dv), s_fin

def _dn_direction(q, k, v, g, beta, s0, reverse):
    if reverse:
        q, k, v, g, beta = (jnp.flip(t, axis=2) for t in (q, k, v, g, beta))
    o, s = _gated_delta_chunked(q, k, v, g, beta, s0)
    if reverse:
        o = jnp.flip(o, axis=2)
    return o, s

def _dn_out(o, zg, o_norm, w_out):
    B, H, S, dv = o.shape
    y = _rms(o.transpose(0, 2, 1, 3), o_norm) * jax.nn.silu(zg.reshape(B, S, H, dv).astype(jnp.float32))
    return y.reshape(B, S, H * dv).astype(zg.dtype) @ w_out

def _odd_mixer(hx, hc, w_in, conv_w, a_log, dt_bias, o_norm, w_out, with_ctx):
    qx, kx, vx, zx, gx, bx = _dn_project(hx, w_in, conv_w, a_log, dt_bias)
    qc, kc, vc, zc, gcx, bc = _dn_project(hc, w_in, conv_w, a_log, dt_bias)
    s0 = jnp.zeros((hx.shape[0], DN_HEADS, DN_DK, DN_DV), jnp.float32)
    ox, oc = [], []
    for d, rev in enumerate((False, True)):
        o_c, s_c = _dn_direction(qc, kc, vc, gcx[d], bc[d], s0, rev)
        o_x, _ = _dn_direction(qx, kx, vx, gx[d], bx[d], s_c, rev)
        ox.append(o_x)
        oc.append(o_c)
    out_x = _dn_out(ox[0] + ox[1], zx, o_norm, w_out)
    out_c = _dn_out(oc[0] + oc[1], zc, o_norm, w_out) if with_ctx else None
    return out_x, out_c

def _peer(h, wq, k1, k2, u_tab, v_tab):
    B, S, D = h.shape
    t = h.reshape(-1, D)
    nb = t.shape[0] // PEER_BLOCK

    def blk(tb):
        qh = (tb @ wq).reshape(PEER_BLOCK, PEER_HEADS, 2, PEER_DKEY)
        s1 = jnp.einsum('thd,kd->thk', qh[:, :, 0], k1).astype(jnp.float32)
        s2 = jnp.einsum('thd,kd->thk', qh[:, :, 1], k2).astype(jnp.float32)
        v1, i1 = lax.top_k(s1, PEER_TOPK)
        v2, i2 = lax.top_k(s2, PEER_TOPK)
        cand = (v1[..., :, None] + v2[..., None, :]).reshape(PEER_BLOCK, PEER_HEADS, PEER_TOPK * PEER_TOPK)
        cidx = (i1[..., :, None] * PEER_NKEYS + i2[..., None, :]).reshape(PEER_BLOCK, PEER_HEADS, -1)
        sc, j = lax.top_k(cand, PEER_TOPK)
        e = jnp.take_along_axis(cidx, j, axis=-1)
        gate = jax.nn.softmax(sc, axis=-1)
        act = jax.nn.gelu(jnp.einsum('thkd,td->thk', u_tab[e], tb).astype(jnp.float32), approximate=False)
        return jnp.einsum('thk,thkd->td', (gate * act).astype(tb.dtype), v_tab[e])

    return lax.map(blk, t.reshape(nb, PEER_BLOCK, D)).reshape(B, S, D)

def setup_inputs(seed: int = 0) -> dict:
    key = jax.random.key(seed)
    ks = iter(jax.random.split(key, 40))
    f32 = jnp.float32
    D = D_MODEL
    ne, no = (DEPTH + 1) // 2, DEPTH // 2

    def nrm(shape, scale):
        return jax.random.normal(next(ks), shape, f32) * scale

    def gain(shape):
        return 1.0 + nrm(shape, 0.02)

    dt = jnp.exp(jax.random.uniform(next(ks), (no, 2, DN_HEADS), f32, math.log(1e-3), math.log(1e-1)))
    dt_bias = dt + jnp.log(-jnp.expm1(-dt))
    a_log = jnp.log(jax.random.uniform(next(ks), (no, 2, DN_HEADS), f32, 1.0, 16.0))
    return {
        'x': nrm((BATCH, SEQ, D), 1.0),
        'c': nrm((BATCH, D), 1.0),
        'ctx': nrm((BATCH, CTX_LEN, D), 1.0),
        'c_ctx': nrm((D,), 1.0),
        'ada_w': nrm((DEPTH, D, 6 * D), 0.5 * D ** -0.5),
        'ada_b': nrm((DEPTH, 6 * D), 0.02),
        'ev_w_in': nrm((ne, D, EV_IN), D ** -0.5),
        'ev_w_out': nrm((ne, EV_MIX, D), EV_MIX ** -0.5),
        'diff_q_norm': gain((ne, DIFF_DIM)),
        'diff_k_norm': gain((ne, DIFF_DIM)),
        'diff_lam_q1': nrm((ne, DIFF_DIM), 0.1),
        'diff_lam_k1': nrm((ne, DIFF_DIM), 0.1),
        'diff_lam_q2': nrm((ne, DIFF_DIM), 0.1),
        'diff_lam_k2': nrm((ne, DIFF_DIM), 0.1),
        'diff_subln': gain((ne, DIFF_VDIM)),
        'mla_cq_norm': gain((ne, MLA_Q_RANK)),
        'mla_ckv_norm': gain((ne, MLA_KV_RANK)),
        'mla_w_uq': nrm((ne, MLA_Q_RANK, MLA_HEADS * MLA_QK), MLA_Q_RANK ** -0.5),
        'mla_w_ukv': nrm((ne, MLA_KV_RANK, MLA_HEADS * (MLA_NOPE + MLA_VDIM)), MLA_KV_RANK ** -0.5),
        'mla_q_norm': gain((ne, MLA_QK)),
        'mla_k_norm': gain((ne, MLA_QK)),
        'dn_w_in': nrm((no, D, DN_IN), D ** -0.5),
        'dn_conv': nrm((no, DN_CONV, DN_QKV), DN_CONV ** -0.5),
        'dn_a_log': a_log,
        'dn_dt_bias': dt_bias,
        'dn_o_norm': gain((no, DN_DV)),
        'dn_w_out': nrm((no, DN_MIX, D), DN_MIX ** -0.5),
        'peer_wq': nrm((DEPTH, D, PEER_HEADS * 2 * PEER_DKEY), D ** -0.5),
        'peer_k1': nrm((DEPTH, PEER_NKEYS, PEER_DKEY), PEER_DKEY ** -0.5),
        'peer_k2': nrm((DEPTH, PEER_NKEYS, PEER_DKEY), PEER_DKEY ** -0.5),
        'peer_u': nrm((DEPTH, PEER_N, D), D ** -0.5),
        'peer_v': nrm((DEPTH, PEER_N, D), 1.0),
    }

def reference(x, c, ctx, c_ctx, ada_w, ada_b, ev_w_in, ev_w_out, diff_q_norm, diff_k_norm,
              diff_lam_q1, diff_lam_k1, diff_lam_q2, diff_lam_k2, diff_subln, mla_cq_norm, mla_ckv_norm,
              mla_w_uq, mla_w_ukv, mla_q_norm, mla_k_norm, dn_w_in, dn_conv, dn_a_log, dn_dt_bias,
              dn_o_norm, dn_w_out, peer_wq, peer_k1, peer_k2, peer_u, peer_v):
    rows = x.shape[1] // GRID_W
    rope_a = _axial_rope(rows, DIFF_DIM)
    rope_b = _axial_rope(rows, MLA_ROPE)
    for l in range(DEPTH):
        last = l == DEPTH - 1
        i = l // 2
        mx = jnp.split((jax.nn.silu(c) @ ada_w[l] + ada_b[l])[:, None, :], 6, axis=-1)
        mc = jnp.split(jax.nn.silu(c_ctx) @ ada_w[l] + ada_b[l], 6, axis=-1)
        hx = _rms(x) * (1.0 + mx[1]) + mx[0]
        hc = _rms(ctx) * (1.0 + mc[1]) + mc[0]
        if l % 2 == 0:
            lam_init = 0.8 - 0.6 * math.exp(-0.3 * l)
            ox, oc = _even_mixer(hx, hc, ev_w_in[i], ev_w_out[i], diff_q_norm[i], diff_k_norm[i],
                                 diff_lam_q1[i], diff_lam_k1[i], diff_lam_q2[i], diff_lam_k2[i], diff_subln[i],
                                 mla_cq_norm[i], mla_ckv_norm[i], mla_w_uq[i], mla_w_ukv[i],
                                 mla_q_norm[i], mla_k_norm[i], lam_init, rope_a, rope_b, not last)
        else:
            ox, oc = _odd_mixer(hx, hc, dn_w_in[i], dn_conv[i], dn_a_log[i], dn_dt_bias[i],
                                dn_o_norm[i], dn_w_out[i], not last)
        x = x + mx[2] * ox
        x = x + mx[5] * _peer(_rms(x) * (1.0 + mx[4]) + mx[3], peer_wq[l], peer_k1[l], peer_k2[l],
                              peer_u[l], peer_v[l])
        if not last:
            ctx = ctx + mc[2] * oc
            ctx = ctx + mc[5] * _peer(_rms(ctx) * (1.0 + mc[4]) + mc[3], peer_wq[l], peer_k1[l],
                                      peer_k2[l], peer_u[l], peer_v[l])
    return x


_drawn_inputs = setup_inputs


def setup_inputs(seed=0):
    import zlib

    import numpy as np

    out = dict(_drawn_inputs(seed))
    spreads = {}
    factors = {'diff_q_norm': 4.715,
     'diff_k_norm': 4.797,
     'diff_lam_q2': 16.768,
     'diff_subln': 11.35,
     'mla_cq_norm': 8.0,
     'mla_ckv_norm': 5.206,
     'mla_q_norm': 8.0,
     'mla_k_norm': 8.0,
     'dn_o_norm': 25.505}
    for name, (base, spread) in spreads.items():
        noise = np.random.default_rng([zlib.crc32(name.encode()), seed]).standard_normal(out[name].shape)
        drawn = base * np.exp(spread * noise) if base else spread * noise
        out[name] = jnp.asarray(drawn.astype(out[name].dtype))
    for name, factor in factors.items():
        out[name] = (out[name] * factor).astype(out[name].dtype)
    return out
```

```python
from contextlib import ExitStack

import concourse.bass as bass
from concourse import mybir

F32 = mybir.dt.float32
U32 = mybir.dt.uint32
ALU = mybir.AluOpType
ACT = mybir.ActivationFunctionType
AX = mybir.AxisListType

P = 128
D = 1024
KD = D // P
NT = 4
CTX_TILES = 2
TOK = NT * P
EPS = 1e-6
LAM_INIT = 0.2
DH = 4
MH = 4
ZW = 1952
QK96 = 96
HEADS = 8
NK = 128
TOPK = 16
RING = 8
NEG = -3.0e38
WCH = 512
ADA_G = 8
ADA_J = 48 // ADA_G
N_PARAM = 7
XT = range(CTX_TILES, NT)

SMALL = {}
_at = 0
for _n, _w in (("qn", 64), ("kn", 64), ("subln", 128), ("cqn", 256), ("ckvn", 128), ("mqn", 96), ("mkn", 96),
               ("onorm", 128), ("lq1", 64), ("lk1", 64), ("lq2", 64), ("lk2", 64), ("alog", 16), ("dtb", 16)):
    SMALL[_n] = (_at, _w)
    _at += _w
SMALL_W = _at
LEVELS = (1, 2, 4, 8, 16, 32)
CONST = {}
_at = 0
for _n, _w in (("ident", 128), ("ones", 128), ("blk", 128), ("incl", 256), ("strict", 256),
               ("lvl", 3 * 128 * len(LEVELS)), ("iota", 16), ("cosA", 64), ("sinA", 64), ("cosB", 32), ("sinB", 32)):
    CONST[_n] = (_at, _w)
    _at += _w
CONST_W = _at

W_EVIN, W_EVOUT, W_WQ0, W_DNIN, W_DNOUT, W_WQ1, W_END = 0, 4, 6, 10, 18, 20, 24


class Signal:

    def __init__(self, sem):
        self.sem, self.made, self.taken = sem, 0, 0

    def give(self, ins):
        self.made += 1
        ins.then_inc(self.sem, 1)

    def take(self, eng):
        self.taken += 1
        eng.wait_ge(self.sem, self.taken)


class Chain:

    def __init__(self, eng, sem):
        self.eng, self.sem, self.n, self.base = eng, sem, 0, 0

    def __call__(self, ins):
        self.n += 1
        ins.then_inc(self.sem, 1)
        self.eng.wait_ge(self.sem, self.base + self.n)

    def alone(self, mark):
        if not isinstance(self.base, int):
            self.eng.sem_inc(mark, 1)


class Pipe:

    def __init__(self, banks, full, free):
        self.banks, self.full, self.free = banks, full, free
        self.opened = self.closed = self.read = self.left = 0

    def open(self, pe):
        if self.opened >= 2:
            pe.wait_ge(self.free, self.opened - 1)
        self.opened += 1
        return self.banks[(self.opened - 1) % 2]

    def close(self, ins):
        self.closed += 1
        ins.then_inc(self.full, 1)

    def drain(self, pe):
        pe.wait_ge(self.free, self.opened)

    def take(self, eng):
        self.read += 1
        eng.wait_ge(self.full, self.read)
        return self.banks[(self.read - 1) % 2]

    def release(self, ins):
        self.left += 1
        ins.then_inc(self.free, 1)


def build(nc, x, ctx_in, cT, ada_w, ada_b, wstream, small, consts, keysT, w_uq, w_ukv, conv_w, w_ab,
          peer_u0, peer_v0, peer_u1, peer_v1, out, stop=9):
    with ExitStack() as es:
        def sb(name, shape, dt=F32):
            return es.enter_context(nc.sbuf_tensor(name, shape, dt))

        def sem(name):
            return es.enter_context(nc.semaphore(name))

        bank = [es.enter_context(nc.psum_tensor(f"bank{i}", [P, 512], F32)) for i in range(8)]

        R = sb("R", [P, NT, D])
        hT = sb("hT", [P, KD, TOK])
        htok = sb("htok", [P, NT, D])
        wbuf = sb("wbuf", [P, 2, KD, WCH])
        bc = sb("bc", [P, 4, 2, D])
        cst = sb("cst", [P, CONST_W])
        smallp = sb("smallp", [P, SMALL_W])
        keys = sb("keys", [P, 2, 2, NK])
        convw = sb("convw", [P, 24, 5])
        wab = sb("wab", [P, KD, 32])
        cs = sb("cs", [P, 3, KD * 2])
        modT = sb("modT", [P, 2, 48, 2])
        adab = sb("adab", [P, 2, 48])
        stat = sb("stat", [P, 3, 80])
        lamt = sb("lamt", [P, 72])
        negs = sb("negs", [P, 8])
        SCR = 18300
        scr = sb("scr", [P, SCR])

        def k(name):
            o, w = CONST[name]
            return cst[:, o:o + w]

        def sm(name):
            o, w = SMALL[name]
            return smallp[:, o:o + w]

        ident, ones = k("ident"), k("ones")

        c_ld, p_ld, ctx_ld = sem("consts_landed"), sem("params_landed"), sem("streams_landed")
        ada_ld = [sem(f"ada_landed{i}") for i in range(2)]
        ada_used = sem("ada_used")
        w_ld = [sem(f"w_landed{i}") for i in range(2)]
        w_used = sem("w_used")
        out_st = sem("out_stored")
        dve_sem, act_sem, pool_sem = sem("vector_step"), sem("scalar_step"), sem("pool_step")
        vec_mark = sem("vector_mark")
        pa = Pipe(bank[0:2], sem("pa_full"), sem("pa_free"))
        pv = Pipe(bank[2:4], sem("pv_full"), sem("pv_free"))
        ps = Pipe(bank[4:6], sem("scores_full"), sem("scores_free"))
        po = Pipe(bank[6:8], sem("po_full"), sem("po_free"))
        silu_in, silu_ready = Signal(sem("silu_exp")), Signal(sem("silu_ready"))
        mods_ready = Signal(sem("mods_ready"))
        diag_ready4 = Signal(sem("bdiag_ready"))
        r_ready = Signal(sem("residual_ready"))
        ss_ready, var_ready, std_ready = Signal(sem("sumsq_ready")), Signal(sem("var_ready")), Signal(sem("std_ready"))
        xn_ready = Signal(sem("xn_ready"))
        z_ready = Signal(sem("z_ready"))
        heads_ready = Signal(sem("heads_ready"))
        lam_in, lam_ready = Signal(sem("lam_in")), Signal(sem("lam_exp"))
        nmax_ready = Signal(sem("nmax_ready"))
        o_ready = Signal(sem("o_ready"))
        mla_ld = sem("mla_weights_landed")
        u_land = [sem(f"u_landed{i}") for i in range(RING)]
        v_land = [sem(f"v_landed{i}") for i in range(RING)]
        u_read, v_read = sem("u_read"), sem("v_read")
        q_staged, sc_done, idx_ready, top_ready = sem("q_staged"), sem("keyscores_done"), sem("idx_ready"), sem("top_ready")
        exp_done, gelu_done, w_ready, diag_done, y_free = (sem("exp_done"), sem("gelu_done"), sem("w_ready"),
                                                          sem("diag_done"), sem("y_free"))
        q_ready = Signal(sem("q_ready"))
        y_zero = Signal(sem("y_zero"))

        adaw = scr[:, 0:2 * ADA_J * KD * P].rearrange("p (s j k m) -> p s j k m", s=2, j=ADA_J, k=KD)
        bdiag = scr[:, 0:1024].rearrange("p (s n) -> p s n", s=2)
        xn = scr[:, 4096:8192].rearrange("p (t d) -> p t d", t=NT)
        junk = scr[:, 8192:9216]

        class Region:
            def __init__(self, whole):
                self.whole, self.at = whole, 0

            def get(self, n):
                a = self.at
                self.at += n
                assert self.at <= self.whole.shape[1], self.at
                return self.whole[:, a:a + n]

        g = Region(scr)
        z = g.get(NT * ZW).rearrange("p (t c) -> p t c", t=NT)
        qkb = g.get(NT * 8 * QK96).rearrange("p (t g c) -> p t g c", t=NT, g=8)
        kvb = g.get(NT * 768).rearrange("p (t c) -> p t c", t=NT)
        bcx = bc[:, 1:3].rearrange("p v s d -> p (v s d)")
        qbT = bcx[:, 0:2048].rearrange("p (h t) -> p h t", h=MH)
        kbT = bcx[:, 2048:4096].rearrange("p (h t) -> p h t", h=MH)
        wuq_sb = g.get(768).rearrange("p (k c) -> p k c", k=2)
        wukv_sb = g.get(768)
        tmpv = g.get(2048)
        cT3 = tmpv[:, 0:3 * TOK].rearrange("p (b t) -> p b t", b=3)
        prob = tmpv[:, 0:1024].rearrange("p (s n) -> p s n", s=2)
        probT = tmpv[:, 1024:2048].rearrange("p (s n) -> p s n", s=2)
        rope_t = kvb.rearrange("p t c -> p (t c)")
        qaT = htok[:, 0:2, :].rearrange("p a (b t) -> p (a b) t", b=2)
        kaT = htok[:, 2:4, :].rearrange("p a (b t) -> p (a b) t", b=2)
        o_tok = hT.rearrange("p k t -> p (k t)").rearrange("p (t d) -> p t d", t=NT)
        oT = htok.rearrange("p t d -> p (t d)").rearrange("p (k t) -> p k t", k=KD)
        rsum = lamt[:, 0:48]
        g = Region(scr)
        qT = g.get(NT * HEADS * 2 * P).rearrange("p (s c) -> p s c", c=2 * P)
        uring = g.get(RING * D).rearrange("p (s d) -> p s d", s=RING)
        g = Region(bcx)
        qst = g.get(2 * 256).rearrange("p (s c) -> p s c", s=2)
        sw = g.get(256)
        cand = g.get(256)
        candw = g.get(256)
        v16 = g.get(32)
        i16 = g.get(32).bitcast(U32)
        sc16 = g.get(32).rearrange("p (s c) -> p s c", s=2)
        j16 = g.get(16).bitcast(U32)
        ab16 = g.get(32).bitcast(U32)
        onehot = g.get(512)
        sel = g.get(32)
        idx = g.get(32).bitcast(U32).rearrange("p (s c) -> p s c", s=2)
        e16 = g.get(32).rearrange("p (s c) -> p s c", s=2)
        act16 = g.get(32).rearrange("p (s c) -> p s c", s=2)
        gel16 = g.get(32).rearrange("p (s c) -> p s c", s=2)
        w16 = g.get(32).rearrange("p (s c) -> p s c", s=2)
        nb = g.get(2)
        zs = g.get(4)
        diag = g.get(4 * 128).rearrange("p (s c) -> p s c", s=4)
        vring = wbuf.rearrange("p s k c -> p (s k c)").rearrange("p (s d) -> p s d", s=RING)
        Y = hT.rearrange("p k t -> p (k t)").rearrange("p (t d) -> p t d", t=NT)
        ybank = [(bank[0], bank[1]), (bank[2], bank[3])]
        scbank = bank[4:6]

        def tile_list(l):
            return range(NT)

        def peer_tiles(l):
            return range(NT) if l == 0 else range(CTX_TILES, NT)

        def act_silu(ac):
            nc.scalar.wait_ge(p_ld, 16 * N_PARAM)
            silu_in.give(nc.scalar.activation(cs[:, 1, :], cs[:, 0, :], ACT.Exp, scale=-1.0))

        def dve_silu(dv):
            silu_in.take(nc.vector)
            dv(nc.vector.tensor_scalar_add(cs[:, 1, :], cs[:, 1, :], 1.0))
            dv(nc.vector.reciprocal(cs[:, 2, :], cs[:, 1, :]))
            nc.vector.wait_ge(p_ld, 16 * N_PARAM)
            silu_ready.give(nc.vector.tensor_tensor(cs[:, 2, :], cs[:, 2, :], cs[:, 0, :], ALU.mult))

        def pe_ada(l):
            if l == 0:
                silu_ready.take(nc.tensor)
            sc = cs[:, 2, :].rearrange("p (k s) -> p k s", k=KD)
            for gi in range(ADA_G):
                n = l * ADA_G + gi
                nc.tensor.wait_ge(ada_ld[n % 2], 16 * (n // 2 + 1))
                b = pv.open(nc.tensor)
                for j in range(ADA_J):
                    for kk in range(KD):
                        last = nc.tensor.matmul(b[:, 2 * j:2 * j + 2], adaw[:, n % 2, j, kk, :], sc[:, kk, :],
                                                start=(kk == 0), stop=(kk == KD - 1))
                pv.close(last)

        def dve_ada(dv, l):
            for gi in range(ADA_G):
                b = pv.take(nc.vector)
                if l == 0 and gi == 0:
                    nc.vector.wait_ge(p_ld, 16 * N_PARAM)
                js = slice(gi * ADA_J, (gi + 1) * ADA_J)
                pv.release(nc.vector.tensor_tensor(
                    modT[:, l, js, :], b[:, 0:2 * ADA_J].rearrange("p (j s) -> p j s", s=2),
                    adab[:, l, js].unsqueeze(2).to_broadcast([P, ADA_J, 2]), ALU.add))
            nc.vector.wait_ge(pv.free, pv.left)
            for j0 in (8, 32):
                dv(nc.vector.tensor_scalar_add(modT[:, l, j0:j0 + 8, :], modT[:, l, j0:j0 + 8, :], 1.0))
            mods_ready.give(nc.vector.tensor_copy(negs[:, 6 + l:7 + l], modT[:, l, 0, 0:1]))

        def bcast_units(l, part):
            streams = (0, 1) if l == 0 else (1,)
            vectors = ((0, 16), (3, 40)) if part == 0 else ((1, 24), (2, 32))
            return [(v, j0, s, half) for v, j0 in vectors for s in streams for half in range(2)]

        def dve_bcast(dv, l, part):
            for n, (v, j0, s, half) in enumerate(bcast_units(l, part)):
                if n >= 2:
                    nc.vector.wait_ge(pa.full, bcast_base[l, part] + n - 1)
                for q in range(4):
                    ins = nc.vector.tensor_scalar(bdiag[:, n % 2, q * P:(q + 1) * P], ident,
                                                  modT[:, l, j0 + half * 4 + q, s:s + 1], None, ALU.mult)
                    dv(ins) if q < 3 else diag_ready4.give(ins)
                nc.vector.wait_ge(diag_ready4.sem, diag_ready4.made)

        def pe_bcast(l, part):
            bcast_base[l, part] = pa.opened
            for n, _ in enumerate(bcast_units(l, part)):
                b = pa.open(nc.tensor)
                diag_ready4.take(nc.tensor)
                pa.close(nc.tensor.matmul(b[:, :], ones, bdiag[:, n % 2, :], start=True, stop=True))

        def act_bcast(l, part):
            for v, j0, s, half in bcast_units(l, part):
                b = pa.take(nc.scalar)
                pa.release(nc.scalar.activation(bc[:, v, s, half * 512:(half + 1) * 512], b[:, :], ACT.Copy))
            mark[f"bc{l}{part}"] = pa.left

        def act_norm(ac, l, sub, tiles):
            if (l, sub) != (0, 0):
                r_ready.take(nc.scalar)
            for t in tiles:
                ac(nc.scalar.activation(junk, R[:, t, :], ACT.Square, accum_out=stat[:, 0, t:t + 1]))
            ss_ready.give(nc.scalar.activation(stat[:, 1, 0:NT], stat[:, 0, 0:NT], ACT.Copy))
            var_ready.take(nc.scalar)
            std_ready.give(nc.scalar.activation(stat[:, 0, 0:NT], stat[:, 1, 0:NT], ACT.Sqrt))
            if sub == 0 :
                if l == 0:
                    mods_ready.take(nc.scalar)
                for t in tiles:
                    s = 0 if t < CTX_TILES else 1
                    for half in range(2):
                        b = pa.take(nc.scalar)
                        for q in range(4):
                            kk = half * 4 + q
                            ins = nc.scalar.activation(hT[:, kk, t * P:(t + 1) * P], b[:, q * P:(q + 1) * P],
                                                       ACT.Identity, scale=modT[:, l, 8 + kk, s:s + 1],
                                                       bias=modT[:, l, kk, s:s + 1])
                        pa.release(ins)
            else:
                act_hT(tiles)

        def act_hT(tiles):
            for t in tiles:
                for half in range(2):
                    b = pa.take(nc.scalar)
                    pa.release(nc.scalar.activation(
                        hT[:, half * 4:half * 4 + 4, t * P:(t + 1) * P],
                        b[:, :].rearrange("p (q t) -> p q t", q=4), ACT.Copy))

        def dve_norm(dv, l, sub, tiles):
            t0, t1 = tiles[0], tiles[-1] + 1
            ss_ready.take(nc.vector)
            var_ready.give(nc.vector.tensor_scalar(stat[:, 1, 0:NT], stat[:, 1, 0:NT], 1.0 / D, EPS, ALU.mult, ALU.add))
            std_ready.take(nc.vector)
            dv(nc.vector.reciprocal(stat[:, 2, t0:t1], stat[:, 0, t0:t1]))
            for t in tiles:
                s = 0 if t < CTX_TILES else 1
                if sub == 0:
                    xn_ready.give(nc.vector.tensor_scalar(xn[:, t, :], R[:, t, :], stat[:, 2, t:t + 1], None, ALU.mult))
                else:
                    dv(nc.vector.scalar_tensor_tensor(out=htok[:, t, :], in0=R[:, t, :], scalar=stat[:, 2, t:t + 1],
                                                      in1=bc[:, 2, s, :], op0=ALU.mult, op1=ALU.mult))
                    xn_ready.give(nc.vector.tensor_tensor(htok[:, t, :], htok[:, t, :], bc[:, 1, s, :], ALU.add))

        def pe_turn(src, tiles, ready):
            for t in tiles:
                ready.take(nc.tensor)
                for half in range(2):
                    b = pa.open(nc.tensor)
                    for q in range(4):
                        kk = half * 4 + q
                        last = nc.tensor.transpose(b[:, q * P:(q + 1) * P], src[:, t, kk * P:(kk + 1) * P], ident)
                    pa.close(last)
            pa.drain(nc.tensor)

        def pe_lin(first, widths, lhs, tiles, pipe):
            for c, n in enumerate(widths):
                w = first + c
                nc.tensor.wait_ge(w_ld[w % 2], 16 * (w // 2 + 1))
                for t in tiles:
                    b = pipe.open(nc.tensor)
                    for kk in range(KD):
                        last = nc.tensor.matmul(b[:, 0:n], lhs[:, kk, t * P:(t + 1) * P], wbuf[:, w % 2, kk, 0:n],
                                                start=(kk == 0), stop=(kk == KD - 1))
                    pipe.close(last)
                used_chunk(w, pipe)

        def used_chunk(w, pipe):
            w_done[w] = (pipe.full, pipe.closed)

        w_done = {}
        bcast_base = {}
        def act_z():
            for c, n in enumerate((512, 512, 512, 416)):
                for t in range(NT):
                    b = pa.take(nc.scalar)
                    pa.release(nc.scalar.activation(z[:, t, c * 512:c * 512 + n], b[:, 0:n], ACT.Copy))
            mark["z"] = pa.left

        def act_sqrt(n):
            var_ready.take(nc.scalar)
            std_ready.give(nc.scalar.activation(stat[:, 0, 0:n], stat[:, 1, 0:n], ACT.Sqrt))

        def dve_rstd(dv, n):
            std_ready.take(nc.vector)
            dv(nc.vector.reciprocal(stat[:, 2, 0:n], stat[:, 0, 0:n]))

        def dve_rope(dv, v, groups, half, cos, sin, tmp):
            n = groups * half
            x1, x2 = v[:, :, 0:half], v[:, :, half:2 * half]
            c = cos.unsqueeze(1).to_broadcast([P, groups, half])
            s = sin.unsqueeze(1).to_broadcast([P, groups, half])
            t1, t2, t3 = (tmp[:, i * n:(i + 1) * n].rearrange("p (g c) -> p g c", g=groups) for i in range(3))
            dv(nc.vector.tensor_tensor(t1, x1, c, ALU.mult))
            dv(nc.vector.tensor_tensor(t2, x2, s, ALU.mult))
            dv(nc.vector.tensor_tensor(t3, x1, s, ALU.mult))
            dv(nc.vector.tensor_tensor(x1, t1, t2, ALU.subtract))
            dv(nc.vector.tensor_tensor(t1, x2, c, ALU.mult))
            return nc.vector.tensor_tensor(x2, t3, t1, ALU.add)

        def dve_lambda(dv):
            nc.vector.wait_ge(p_ld, 16 * N_PARAM)
            for i, (a, b) in enumerate((("lq1", "lk1"), ("lq2", "lk2"))):
                dv(nc.vector.tensor_tensor(tmpv[:, 0:64], sm(a), sm(b), ALU.mult))
                ins = nc.vector.tensor_reduce(lamt[:, 48 + i:49 + i], tmpv[:, 0:64], AX.X, ALU.add)
                dv(ins) if i == 0 else lam_in.give(ins)
            lam_ready.take(nc.vector)
            dv(nc.vector.tensor_tensor(lamt[:, 52:53], lamt[:, 51:52], lamt[:, 50:51], ALU.subtract))
            dv(nc.vector.tensor_scalar_add(lamt[:, 52:53], lamt[:, 52:53], -LAM_INIT))

        def act_lambda():
            lam_in.take(nc.scalar)
            lam_ready.give(nc.scalar.activation(lamt[:, 50:52], lamt[:, 48:50], ACT.Exp))

        def dve_heads(dv):
            dve_lambda(dv)
            nc.vector.wait_ge(pa.free, mark["z"])
            st = [stat[:, i, 0:72].rearrange("p (t c) -> p t c", t=NT) for i in range(3)]
            for t in range(NT):
                zq, zc = z[:, t, 0:1024], z[:, t, 1536:1920]
                dv(nc.vector.tensor_tensor(tmpv[:, 0:1024], zq, zq, ALU.mult))
                dv(nc.vector.tensor_reduce(st[0][:, t, 0:16], tmpv[:, 0:1024].rearrange("p (g c) -> p g c", g=16), AX.X, ALU.add))
                dv(nc.vector.tensor_tensor(tmpv[:, 0:384], zc, zc, ALU.mult))
                dv(nc.vector.tensor_reduce(st[0][:, t, 16:17], tmpv[:, 0:256], AX.X, ALU.add))
                dv(nc.vector.tensor_reduce(st[0][:, t, 17:18], tmpv[:, 256:384], AX.X, ALU.add))
            dv(nc.vector.tensor_scalar(st[1][:, :, 0:16], st[0][:, :, 0:16], 1.0 / 64, EPS, ALU.mult, ALU.add))
            dv(nc.vector.tensor_scalar(st[1][:, :, 16:17], st[0][:, :, 16:17], 1.0 / 256, EPS, ALU.mult, ALU.add))
            var_ready.give(nc.vector.tensor_scalar(st[1][:, :, 17:18], st[0][:, :, 17:18], 1.0 / 128, EPS, ALU.mult, ALU.add))
            dve_rstd(dv, 72)
            for t in range(NT):
                zq = z[:, t, 0:1024].rearrange("p (g c) -> p g c", g=16)
                dv(nc.vector.tensor_tensor(zq, zq, st[2][:, t, 0:16].unsqueeze(2).to_broadcast([P, 16, 64]), ALU.mult))
                for a, name in ((0, "qn"), (8, "kn")):
                    v = zq[:, a:a + 8, :]
                    dv(nc.vector.tensor_tensor(v, v, sm(name).unsqueeze(1).to_broadcast([P, 8, 64]), ALU.mult))
                if t >= CTX_TILES:
                    o = (t - CTX_TILES) * 32
                    dv(dve_rope(dv, zq, 16, 32, k("cosA")[:, o:o + 32], k("sinA")[:, o:o + 32], rope_t))
                for a, n, c, name in ((1536, 256, 16, "cqn"), (1792, 128, 17, "ckvn")):
                    v = z[:, t, a:a + n]
                    ins = nc.vector.scalar_tensor_tensor(out=v, in0=v, scalar=st[2][:, t, c:c + 1], in1=sm(name),
                                                         op0=ALU.mult, op1=ALU.mult)
                    dv(ins) if c == 16 else heads_ready.give(ins)
            nc.vector.wait_ge(pa.free, mark["mla"])
            for t in range(NT):
                dv(nc.vector.tensor_copy(qkb[:, t, 4:8, 0:64], kvb[:, t, :].rearrange("p (h c) -> p h c", h=MH)[:, :, 0:64]))
                dv(nc.vector.tensor_copy(qkb[:, t, 4:8, 64:96], z[:, t, 1920:1952].unsqueeze(1).to_broadcast([P, 4, 32])))
                v = qkb[:, t, :, :].rearrange("p g c -> p (g c)")
                dv(nc.vector.tensor_tensor(tmpv[:, 0:768], v, v, ALU.mult))
                dv(nc.vector.tensor_reduce(stat[:, 0, t * 8:t * 8 + 8], tmpv[:, 0:768].rearrange("p (g c) -> p g c", g=8), AX.X, ALU.add))
            var_ready.give(nc.vector.tensor_scalar(stat[:, 1, 0:32], stat[:, 0, 0:32], 1.0 / QK96, EPS, ALU.mult, ALU.add))
            dve_rstd(dv, 32)
            for t in range(NT):
                v = qkb[:, t, :, :]
                dv(nc.vector.tensor_tensor(v, v, stat[:, 2, t * 8:t * 8 + 8].unsqueeze(2).to_broadcast([P, 8, QK96]), ALU.mult))
                dv(nc.vector.tensor_tensor(v[:, 0:4], v[:, 0:4], sm("mqn").unsqueeze(1).to_broadcast([P, 4, QK96]), ALU.mult))
                ins = nc.vector.tensor_tensor(v[:, 4:8], v[:, 4:8], sm("mkn").unsqueeze(1).to_broadcast([P, 4, QK96]), ALU.mult)
                if t >= CTX_TILES:
                    dv(ins)
                    o = (t - CTX_TILES) * 16
                    ins = dve_rope(dv, v[:, :, 64:96], 8, 16, k("cosB")[:, o:o + 16], k("sinB")[:, o:o + 16], tmpv)
                heads_ready.give(ins)

        def pe_heads():
            for t in range(NT):
                heads_ready.take(nc.tensor)
                for base in (0, 512):
                    b = pa.open(nc.tensor)
                    for h in range(DH):
                        last = nc.tensor.transpose(b[:, h * P:(h + 1) * P], z[:, t, base + h * P:base + (h + 1) * P], ident)
                    pa.close(last)
                b = pa.open(nc.tensor)
                for q in range(3):
                    last = nc.tensor.transpose(b[:, q * P:(q + 1) * P], z[:, t, 1536 + q * P:1536 + (q + 1) * P], ident)
                pa.close(last)
            pa.drain(nc.tensor)
            nc.tensor.wait_ge(p_ld, 16 * N_PARAM)
            nc.tensor.wait_ge(mla_ld, 32)
            for t in range(NT):
                tt = slice(t * P, (t + 1) * P)
                b = pa.open(nc.tensor)
                nc.tensor.matmul(b[:, 0:384], cT3[:, 0, tt], wuq_sb[:, 0, :], start=True, stop=False)
                pa.close(nc.tensor.matmul(b[:, 0:384], cT3[:, 1, tt], wuq_sb[:, 1, :], start=False, stop=True))
                for half in range(2):
                    b = pa.open(nc.tensor)
                    pa.close(nc.tensor.matmul(b[:, 0:384], cT3[:, 2, tt], wukv_sb[:, half * 384:(half + 1) * 384],
                                              start=True, stop=True))
            for t in range(NT):
                heads_ready.take(nc.tensor)
                for base in (0, 4):
                    b = pa.open(nc.tensor)
                    for h in range(MH):
                        last = nc.tensor.transpose(b[0:QK96, h * P:(h + 1) * P], qkb[:, t, base + h, :], ident)
                    pa.close(last)
            pa.drain(nc.tensor)

        def act_heads():
            act_lambda()
            act_sqrt(72)
            for t in range(NT):
                tt = slice(t * P, (t + 1) * P)
                for dst, n in ((qaT, 4), (kaT, 4), (cT3, 3)):
                    b = pa.take(nc.scalar)
                    pa.release(nc.scalar.activation(dst[:, 0:n, tt], b[:, 0:n * P].rearrange("p (h t) -> p h t", h=n), ACT.Copy))
            for t in range(NT):
                b = pa.take(nc.scalar)
                pa.release(nc.scalar.activation(qkb[:, t, 0:4, :], b[:, 0:384].rearrange("p (h c) -> p h c", h=4), ACT.Copy))
                for half in range(2):
                    b = pa.take(nc.scalar)
                    pa.release(nc.scalar.activation(kvb[:, t, half * 384:(half + 1) * 384], b[:, 0:384], ACT.Copy))
            mark["mla"] = pa.left
            act_sqrt(32)
            for t in range(NT):
                for dst in (qbT, kbT):
                    b = pa.take(nc.scalar)
                    pa.release(nc.scalar.activation(dst[0:QK96, :, t * P:(t + 1) * P],
                                                    b[0:QK96, :].rearrange("p (h t) -> p h t", h=MH), ACT.Copy))

        UNITS = [(t, m) for t in range(NT) for m in range(12)]

        def unit(u):
            t, m = UNITS[u]
            return t, m, (CTX_TILES if t < CTX_TILES else NT), (64 ** -0.5 if m < 8 else QK96 ** -0.5)

        def pe_attn():
            def scores(u):
                t, m, nk, _ = unit(u)
                b = ps.open(nc.tensor)
                if m < 8:
                    r = slice((m % 2) * 64, (m % 2) * 64 + 64)
                    q, kt = qaT[r, m // 2, t * P:(t + 1) * P], kaT[r, m // 2, 0:nk * P]
                else:
                    q, kt = qbT[0:QK96, m - 8, t * P:(t + 1) * P], kbT[0:QK96, m - 8, 0:nk * P]
                ps.close(nc.tensor.matmul(b[:, 0:nk * P], q, kt, start=True, stop=True))

            scores(0)
            for u in range(len(UNITS)):
                t, m, nk, _ = unit(u)
                if u + 1 < len(UNITS):
                    scores(u + 1)
                b = pv.open(nc.tensor)
                nc.tensor.wait_ge(ps.free, u + 1)
                for c in range(nk):
                    last = nc.tensor.transpose(b[:, c * P:(c + 1) * P], prob[:, u % 2, c * P:(c + 1) * P], ident)
                pv.close(last)
                b = po.open(nc.tensor)
                pv.drain(nc.tensor)
                for c in range(nk):
                    v = z[:, c, 1024 + (m // 2) * P:1024 + (m // 2 + 1) * P] if m < 8 else \
                        kvb[:, c, (m - 8) * 192 + 64:(m - 8) * 192 + 192]
                    last = nc.tensor.matmul(b[:, 0:P], probT[:, u % 2, c * P:(c + 1) * P], v, start=(c == 0), stop=(c == nk - 1))
                po.close(last)

        def act_attn():
            for u in range(len(UNITS)):
                _, _, nk, scale = unit(u)
                nmax_ready.take(nc.scalar)
                ps.release(nc.scalar.activation(prob[:, u % 2, 0:nk * P], ps.banks[u % 2][:, 0:nk * P], ACT.Exp,
                                                bias=negs[:, 2 + u % 2:3 + u % 2], scale=scale, accum_out=rsum[:, u:u + 1]))

        def dve_attn(dv):
            def nmax(u):
                _, _, nk, scale = unit(u)
                b = ps.take(nc.vector)
                dv(nc.vector.tensor_reduce(negs[:, u % 2:u % 2 + 1], b[:, 0:nk * P], AX.X, ALU.max))
                nmax_ready.give(nc.vector.tensor_scalar(negs[:, 2 + u % 2:3 + u % 2], negs[:, u % 2:u % 2 + 1],
                                                        -scale, None, ALU.mult))

            nmax(0)
            for u in range(len(UNITS)):
                t, m, nk, _ = unit(u)
                if u + 1 < len(UNITS):
                    nmax(u + 1)
                b = pv.take(nc.vector)
                pv.release(nc.vector.tensor_copy(probT[:, u % 2, 0:nk * P], b[:, 0:nk * P]))
                dv(nc.vector.reciprocal(negs[:, 4 + u % 2:5 + u % 2], rsum[:, u:u + 1]))
                b = po.take(nc.vector)
                nc.vector.wait_ge(po.free, po.left)
                if m < 8:
                    dst = o_tok[:, t, (m // 2) * P:(m // 2 + 1) * P]
                else:
                    dst = o_tok[:, t, (m - 4) * P:(m - 3) * P]
                if m < 8 and m % 2:
                    dv(nc.vector.tensor_tensor(negs[:, 4 + u % 2:5 + u % 2], negs[:, 4 + u % 2:5 + u % 2], lamt[:, 52:53], ALU.mult))
                    po.release(nc.vector.scalar_tensor_tensor(out=dst, in0=b[:, 0:P], scalar=negs[:, 4 + u % 2:5 + u % 2], in1=dst,
                                                              op0=ALU.mult, op1=ALU.add))
                else:
                    po.release(nc.vector.tensor_scalar(dst, b[:, 0:P], negs[:, 4 + u % 2:5 + u % 2], None, ALU.mult))
            nc.vector.wait_ge(po.free, po.left)
            for t in range(NT):
                v = o_tok[:, t, 0:512]
                dv(nc.vector.tensor_tensor(tmpv[:, 0:512], v, v, ALU.mult))
                dv(nc.vector.tensor_reduce(stat[:, 0, t * 4:t * 4 + 4], tmpv[:, 0:512].rearrange("p (g c) -> p g c", g=4), AX.X, ALU.add))
            var_ready.give(nc.vector.tensor_scalar(stat[:, 1, 0:16], stat[:, 0, 0:16], 1.0 / P, EPS, ALU.mult, ALU.add))
            dve_rstd(dv, 16)
            for t in range(NT):
                v = o_tok[:, t, 0:512].rearrange("p (g c) -> p g c", g=4)
                dv(nc.vector.tensor_tensor(v, v, stat[:, 2, t * 4:t * 4 + 4].unsqueeze(2).to_broadcast([P, 4, P]), ALU.mult))
                o_ready.give(nc.vector.scalar_tensor_tensor(out=v, in0=v, scalar=1.0 - LAM_INIT,
                                                            in1=sm("subln").unsqueeze(1).to_broadcast([P, 4, P]),
                                                            op0=ALU.mult, op1=ALU.mult))

        def act_turn(dst, tiles):
            for t in tiles:
                for half in range(2):
                    b = pa.take(nc.scalar)
                    pa.release(nc.scalar.activation(dst[:, half * 4:half * 4 + 4, t * P:(t + 1) * P],
                                                    b[:, :].rearrange("p (q t) -> p q t", q=4), ACT.Copy))

        def dve_residual(dv, tiles, tmp):
            n = 0
            for c in range(2):
                for t in tiles:
                    n += 1
                    s = 0 if t < CTX_TILES else 1
                    b = pv.take(nc.vector)
                    cc = slice(c * 512, (c + 1) * 512)
                    pv.release(nc.vector.tensor_tensor(tmp, b[:, :], bc[:, 0, s, cc], ALU.mult))
                    nc.vector.wait_ge(pv.free, pv.left)
                    ins = nc.vector.tensor_tensor(R[:, t, cc], R[:, t, cc], tmp, ALU.add)
                    r_ready.give(ins) if n == 2 * len(tiles) else dv(ins)
            nc.vector.wait_ge(r_ready.sem, r_ready.made)

        qT4 = qT.rearrange("p (t h) c -> p t h c", h=HEADS)
        qTf = qT.rearrange("p s c -> p (s c)")
        htf = htok.rearrange("p t d -> p (t d)")
        Yf = Y.rearrange("p t d -> p (t d)")

        def pe_query(l):
            tiles = peer_tiles(l)
            a, n = tiles[0] * P, len(tiles) * P
            for c in range(4):
                w = (W_WQ0 if l == 0 else W_WQ1) + c
                nc.tensor.wait_ge(w_ld[w % 2], 16 * (w // 2 + 1))
                for cb in range(4):
                    b = pa.open(nc.tensor)
                    for kk in range(KD):
                        last = nc.tensor.matmul(b[:, 0:n], wbuf[:, w % 2, kk, cb * P:(cb + 1) * P], hT[:, kk, a:a + n],
                                                start=(kk == 0), stop=(kk == KD - 1))
                    pa.close(last)
                used_chunk(w, pa)
            mark[f"q{l}"] = pa.closed
            pa.drain(nc.tensor)

        def act_query(l):
            nt = len(peer_tiles(l))
            for c in range(4):
                for cb in range(4):
                    b = pa.take(nc.scalar)
                    pa.release(nc.scalar.activation(qT4[:, 0:nt, 2 * c + cb // 2, (cb % 2) * P:(cb % 2 + 1) * P],
                                                    b[:, 0:nt * P].rearrange("p (t c) -> p t c", t=nt), ACT.Copy))
            nc.scalar.wait_ge(pa.free, pa.left)

        def steps(eng, l, body, chain=None):
            n = len(peer_tiles(l)) * HEADS
            base = 0 if l == 0 else NT * HEADS
            start = chain.n if chain else 0
            for p in range(2):
                body(p, base + p, p, 0, True, n)
            per = chain.n - start if chain else 0
            start += per
            with eng.Fori(1, n // 2 - 1) as i:
                if chain:
                    chain.base, chain.n = (i - 1) * per + start, 0
                for p in range(2):
                    body(i * 2 + p, i * 2 + (base + p), p, i, False, n)
                if chain:
                    assert chain.n == per, (chain.n, per)
            if chain:
                chain.base, chain.n = 0, start + per * (n // 2 - 2)
            for p in range(2):
                body(n - 2 + p, base + n - 2 + p, p, None, False, n)

        def tab(l, which):
            return ((peer_u0, peer_v0), (peer_u1, peer_v1))[l][which]

        def pool_peer(l):
            def body(s, gs, par, i, first, n):
                dyn = not isinstance(s, int)

                def hold(sm_, v):
                    if isinstance(v, int) and v <= 0:
                        return
                    nc.gpsimd.wait_ge(sm_, v)
                    if dyn:
                        nc.gpsimd.sem_inc(pool_sem, 1)

                hold(idx_ready, gs + 1)
                for which, ring, land, read in ((0, uring, u_land, u_read), (1, vring, v_land, v_read)):
                    for kk in range(TOPK):
                        hold(read, gs * 16 + (kk - RING + 1))
                        nc.gpsimd.indirect_dma_start(
                            ring[:, kk % RING, :], None, tab(l, which),
                            bass.IndirectOffsetOnAxis(idx[:, par, kk:kk + 1], 0)).then_inc(land[kk % RING], 16)
            steps(nc.gpsimd, l, body)

        def dve_route(dv, s, gs, par):
            b = scbank[par]
            nc.vector.wait_ge(sc_done, gs + 1)
            for half in range(2):
                src = b[:, half * NK:(half + 1) * NK]
                o = half * TOPK
                dv.alone(vec_mark)
                dv(nc.vector.max(v16[:, o:o + 8], src))
                dv.alone(vec_mark)
                dv(nc.vector.max_index(i16[:, o:o + 8], v16[:, o:o + 8], src))
                dv.alone(vec_mark)
                dv(nc.vector.match_replace(sw[:, 0:NK], v16[:, o:o + 8], src, NEG))
                dv.alone(vec_mark)
                dv(nc.vector.max(v16[:, o + 8:o + 16], sw[:, 0:NK]))
                dv.alone(vec_mark)
                dv(nc.vector.max_index(i16[:, o + 8:o + 16], v16[:, o + 8:o + 16], sw[:, 0:NK]))
            c2 = cand.rearrange("p (a b) -> p a b", a=TOPK)
            dv(nc.vector.tensor_tensor(c2, v16[:, 0:16].unsqueeze(2).to_broadcast([P, TOPK, TOPK]),
                                       v16[:, 16:32].unsqueeze(1).to_broadcast([P, TOPK, TOPK]), ALU.add))
            dv.alone(vec_mark)
            dv(nc.vector.max(sc16[:, par, 0:8], cand))
            dv.alone(vec_mark)
            dv(nc.vector.max_index(j16[:, 0:8], sc16[:, par, 0:8], cand))
            dv.alone(vec_mark)
            dv(nc.vector.match_replace(candw, sc16[:, par, 0:8], cand, NEG))
            dv.alone(vec_mark)
            dv(nc.vector.max(sc16[:, par, 8:16], candw))
            dv.alone(vec_mark)
            dv(nc.vector.max_index(j16[:, 8:16], sc16[:, par, 8:16], candw))
            nc.vector.tensor_scalar(nb[:, par:par + 1], sc16[:, par, 0:1], -1.0, None, ALU.mult).then_inc(top_ready, 1)
            dv(nc.vector.tensor_scalar(ab16[:, 0:16], j16, 4, None, ALU.logical_shift_right))
            dv(nc.vector.tensor_scalar(ab16[:, 16:32], j16, 15, None, ALU.bitwise_and))
            oh = onehot.rearrange("p (k i) -> p k i", k=32)
            dv(nc.vector.tensor_tensor(oh, ab16.unsqueeze(2).to_broadcast([P, 32, TOPK]),
                                       k("iota").unsqueeze(1).to_broadcast([P, 32, TOPK]), ALU.is_equal))
            for half in range(2):
                o = half * TOPK
                dv(nc.vector.tensor_tensor(oh[:, o:o + 16, :], oh[:, o:o + 16, :],
                                           i16[:, o:o + 16].unsqueeze(1).to_broadcast([P, TOPK, TOPK]), ALU.mult))
            dv(nc.vector.tensor_reduce(sel, oh, AX.X, ALU.add))
            nc.vector.scalar_tensor_tensor(out=idx[:, par, :], in0=sel[:, 0:16], scalar=float(NK), in1=sel[:, 16:32],
                                           op0=ALU.mult, op1=ALU.add).then_inc(idx_ready, 1)

        def tile_of(s, par, i, t0, back=0):
            if isinstance(s, int):
                return t0 + (s - back) // HEADS
            return (i - 1) // 4 + t0 if (back and par == 0) else i // 4 + t0

        def dve_peer(dv, l):
            t0 = peer_tiles(l)[0]

            def yacc(s, gs, par, t):
                nc.vector.wait_ge(v_read, gs * 16 + 16)
                nc.vector.wait_ge(y_free, gs * 2) if not (isinstance(gs, int) and gs == 0) else None
                for half in range(2):
                    dst = Yf[:, bass.ds(t * D + half * 512, 512)]
                    nc.vector.tensor_tensor(dst, dst, ybank[par][half][:, :], ALU.add).then_inc(y_free, 1)

            def body(s, gs, par, i, first, n):
                t = tile_of(s, par, i, t0)
                for kk in range(TOPK):
                    nc.vector.wait_ge(u_land[kk % RING], gs * 32 + 16 * (kk // RING + 1))
                    nc.vector.scalar_tensor_tensor(out=uring[:, kk % RING, :], in0=uring[:, kk % RING, :], scalar=1.0,
                                                   in1=htf[:, bass.ds(t * D, D)], op0=ALU.mult, op1=ALU.mult,
                                                   accum_out=act16[:, par, kk:kk + 1]).then_inc(u_read, 1)
                if not (first and par == 0):
                    yacc(None, gs - 1, 1 - par, tile_of(s, par, i, t0, 1))
                if not (isinstance(s, int) and s == n - 1):
                    dve_route(dv, s, gs + 1, 1 - par)
                nc.vector.wait_ge(exp_done, gs + 1)
                dv(nc.vector.reciprocal(zs[:, 2 + par:3 + par], zs[:, par:par + 1]))
                nc.vector.wait_ge(gelu_done, gs + 1)
                nc.vector.scalar_tensor_tensor(out=w16[:, par, :], in0=gel16[:, par, :], scalar=zs[:, 2 + par:3 + par],
                                               in1=e16[:, par, :], op0=ALU.mult, op1=ALU.mult).then_inc(w_ready, 1)
                if isinstance(s, int) and s == n - 1:
                    yacc(None, gs, par, tile_of(s, par, i, t0))

            base = 0 if l == 0 else NT * HEADS
            nc.vector.wait_ge(pa.full, mark[f"q{l}"])
            dv(nc.vector.memset(Yf, 0.0))
            dve_route(dv, 0, base, 0)
            steps(nc.vector, l, body, dv)
            end = base + len(peer_tiles(l)) * HEADS
            nc.vector.wait_ge(y_free, 2 * end)
            for t in peer_tiles(l):
                s = 0 if t < CTX_TILES else 1
                dv(nc.vector.tensor_tensor(Y[:, t, :], Y[:, t, :], bc[:, 3, s, :], ALU.mult))
                ins = nc.vector.tensor_tensor(R[:, t, :], R[:, t, :], Y[:, t, :], ALU.add)
                dv(ins) if t < NT - 1 else r_ready.give(ins)
            nc.vector.wait_ge(r_ready.sem, r_ready.made)

        def act_peer(l):
            base = 0 if l == 0 else NT * HEADS

            def stage(s, gs, par):
                if not (isinstance(gs, int) and gs < 2):
                    nc.scalar.wait_ge(sc_done, gs - 1)
                nc.scalar.activation(qst[:, par, :], qTf[:, bass.ds(s * 256, 256)], ACT.Copy).then_inc(q_staged, 1)

            def softmax(gs, par):
                nc.scalar.wait_ge(top_ready, gs + 1)
                nc.scalar.activation(e16[:, par, :], sc16[:, par, :], ACT.Exp, bias=nb[:, par:par + 1],
                                     accum_out=zs[:, par:par + 1]).then_inc(exp_done, 1)

            def body(s, gs, par, i, first, n):
                last = isinstance(s, int) and s == n - 1
                if not last:
                    stage(s + 1, gs + 1, 1 - par)
                nc.scalar.wait_ge(u_read, gs * 16 + 16)
                nc.scalar.activation(gel16[:, par, :], act16[:, par, :], ACT.Gelu).then_inc(gelu_done, 1)
                if not last:
                    softmax(gs + 1, 1 - par)
                nc.scalar.wait_ge(w_ready, gs + 1)
                for kk in range(TOPK):
                    if not (isinstance(gs, int) and gs * 16 + kk < 4):
                        nc.scalar.wait_ge(v_read, gs * 16 + (kk - 3))
                    nc.scalar.activation(diag[:, kk % 4, :], ident, ACT.Copy, scale=w16[:, par, kk:kk + 1]).then_inc(diag_done, 1)

            stage(0, base, 0)
            softmax(base, 0)
            steps(nc.scalar, l, body)

        def pe_peer(l):
            base = 0 if l == 0 else NT * HEADS

            def keyscores(gs, par):
                nc.tensor.wait_ge(q_staged, gs + 1)
                if not (isinstance(gs, int) and gs < 2):
                    nc.tensor.wait_ge(idx_ready, gs - 1)
                nc.tensor.matmul(scbank[par][:, 0:NK], qst[:, par, 0:P], keys[:, l, 0, :], start=True, stop=True)
                nc.tensor.matmul(scbank[par][:, NK:2 * NK], qst[:, par, P:2 * P], keys[:, l, 1, :],
                                 start=True, stop=True).then_inc(sc_done, 1)

            def body(s, gs, par, i, first, n):
                if not (isinstance(s, int) and s == n - 1):
                    keyscores(gs + 1, 1 - par)
                if not (isinstance(gs, int) and gs < 2):
                    nc.tensor.wait_ge(y_free, gs * 2 - 2)
                for kk in range(TOPK):
                    nc.tensor.wait_ge(v_land[kk % RING], gs * 32 + 16 * (kk // RING + 1))
                    nc.tensor.wait_ge(diag_done, gs * 16 + (kk + 1))
                    for half in range(2):
                        ins = nc.tensor.matmul(ybank[par][half][:, :], diag[:, kk % 4, :],
                                               vring[:, kk % RING, half * 512:(half + 1) * 512],
                                               start=(kk == 0), stop=(kk == TOPK - 1))
                    ins.then_inc(v_read, 1)

            keyscores(base, 0)
            steps(nc.tensor, l, body)
            nc.tensor.wait_ge(y_free, 2 * (base + len(peer_tiles(l)) * HEADS))
        NG, CH, CONV, XW = 4, 64, 5, 256
        g = Region(scr)
        ktok = g.get(NT * D).rearrange("p (t d) -> p t d", t=NT)
        vtok = g.get(NT * D).rearrange("p (t d) -> p t d", t=NT)
        qtok = g.get(2 * D).rearrange("p (t d) -> p t d", t=2)
        zgs = g.get(2 * D).rearrange("p (t d) -> p t d", t=2)
        kTg = g.get(2 * TOK).rearrange("p (h t) -> p h t", h=2)
        qTg = g.get(2 * XW).rearrange("p (h t) -> p h t", h=2)
        ug = g.get(NT * 512).rearrange("p (t u c) -> p t u c", t=NT, u=4)
        wTg = g.get(NT * 512).rearrange("p (t u c) -> p t u c", t=NT, u=4)
        g = Region(htok.rearrange("p t d -> p (t d)"))
        kdg = g.get(NT * 512).rearrange("p (t u c) -> p t u c", t=NT, u=4)
        ATg = g.get(2 * 512).rearrange("p (t u c) -> p t u c", t=2, u=4)
        qdTg = g.get(2 * 512).rearrange("p (t u c) -> p t u c", t=2, u=4)
        g = Region(bcx)
        cpad = g.get(2 * 2 * (XW + CONV - 1)).rearrange("p (r s c) -> p r s c", r=2, s=2)
        cout = g.get(2 * TOK).rearrange("p (r c) -> p r c", r=2)
        csil = g.get(2 * TOK).rearrange("p (r c) -> p r c", r=2)
        g = Region(bcx)
        Xm, XTm, LTm, Pm = (g.get(1024).rearrange("p (r u c) -> p r u c", r=2, u=4) for _ in range(4))
        g = Region(hT.rearrange("p k t -> p (k t)"))
        S = g.get(512).rearrange("p (u c) -> p u c", u=4)
        vn = g.get(512).rearrange("p (u c) -> p u c", u=4)
        dec, CTm = (g.get(1024).rearrange("p (r u c) -> p r u c", r=2, u=4) for _ in range(2))
        dgc = g.get(1024).rearrange("p (r u c) -> p r u c", r=2, u=4)
        g = Region(wbuf[:, 1].rearrange("p k c -> p (k c)"))
        vbm, kbm, Lm, qem = (g.get(1024).rearrange("p (r u c) -> p r u c", r=2, u=4) for _ in range(4))
        Am = CTm
        sqb = wTg.rearrange("p t u c -> p (t u c)")
        g = Region(bc[:, 0, 0, :])
        abt = g.get(128).rearrange("p (t c) -> p t c", t=NT)
        ga, gm, gn, gg, beta, eg, ed, bek = (g.get(64) for _ in range(8))
        gct = g.get(256)
        g = Region(bc[:, 3, 0, :])
        glb = g.get(128)
        ealog = g.get(16)

        pad_ready = Signal(sem("conv_padding_ready"))
        conv_ready, csil_ready = Signal(sem("conv_ready")), Signal(sem("conv_silu_ready"))
        gate_in, gate_out = Signal(sem("gate_in")), Signal(sem("gate_exp"))
        g_ready = Signal(sem("log_decay_ready"))
        norm_ready = Signal(sem("qk_normed"))
        operand_ready = Signal(sem("dn_operand_ready"))
        dec_in, dec_exp = Signal(sem("decay_in")), Signal(sem("decay_exp"))
        vn_ready = Signal(sem("vnew_ready"))
        DT = [(0, 1), (2, 3)]

        def dth(v):
            return v.rearrange("p (d t h) -> p d t h", d=2, t=NT)

        def unit_scalars(v, gp, t):
            s = dth(v)[:, :, t, 2 * gp:2 * gp + 2].rearrange("p d h -> p h d")
            return s.unsqueeze(3).to_broadcast([P, 2, 2, P])

        def u4(v):
            return v.rearrange("p (h d) c -> p h d c", h=2)

        def over_dirs(v):
            return v.unsqueeze(2).to_broadcast([P, 2, 2, P])

        def over_heads(v):
            return v.unsqueeze(1).to_broadcast([P, 2, 2, P])

        incl = k("incl").rearrange("p (d c) -> p d c", d=2)
        strict = k("strict").rearrange("p (d c) -> p d c", d=2)
        lvl = k("lvl").rearrange("p (l d c) -> p l d c", l=len(LEVELS), d=3)
        identu = ident.unsqueeze(1).to_broadcast([P, 4, P])

        def pe_dn_project():
            def turn(i):
                csil_ready.take(nc.tensor)
                b = pa.open(nc.tensor)
                for t in (XT if i < 8 else AT):
                    last = nc.tensor.transpose(b[:, t * P:(t + 1) * P], csil[:, i % 2, t * P:(t + 1) * P], ident)
                pa.close(last)

            for i in range(26):
                if i < 24:
                    w, cb = W_DNIN + i // 4, i % 4
                    if cb == 0:
                        nc.tensor.wait_ge(w_ld[w % 2], 16 * (w // 2 + 1))
                    a = XW if i < 8 else 0
                    b = pa.open(nc.tensor)
                    for kk in range(KD):
                        last = nc.tensor.matmul(b[:, a:TOK], wbuf[:, w % 2, kk, cb * P:(cb + 1) * P], hT[:, kk, a:TOK],
                                                start=(kk == 0), stop=(kk == KD - 1))
                    pa.close(last)
                    if cb == 3:
                        used_chunk(w, pa)
                if i >= 2:
                    turn(i - 2)
            b = pa.open(nc.tensor)
            for t in AT:
                for kk in range(KD):
                    last = nc.tensor.matmul(b[:, t * 32:(t + 1) * 32], hT[:, kk, t * P:(t + 1) * P], wab[:, kk, :],
                                            start=(kk == 0), stop=(kk == KD - 1))
            pa.close(last)
            pe_lin(W_DNIN + 6, (512, 512), hT, XT, pa)
            mark["dn_hT"] = pa.closed
            g_ready.take(nc.tensor)
            b = pv.open(nc.tensor)
            gd = dth(gg).rearrange("p d t h -> p d (t h)")
            for d, m in ((0, k("incl")[:, P:2 * P]), (1, k("incl")[:, 0:P])):
                nc.tensor.matmul(b[:, d * 32:(d + 1) * 32], m, gd[:, d], start=True, stop=True)
                nc.tensor.matmul(b[:, 64 + d * 32:96 + d * 32], k("blk"), gd[:, d], start=True, stop=True)
            for c in range(2):
                rows_c = k("blk")[:, c * CH:c * CH + 1].to_broadcast([P, P])
                for d in range(2):
                    o = 128 + c * 64 + d * 32
                    last = nc.tensor.matmul(b[:, o:o + 32], rows_c, gd[:, d], start=True, stop=True)
            pv.close(last)

        def act_dn_project(ac):
            def silu(i):
                conv_ready.take(nc.scalar)
                a = XW if i < 8 else 0
                csil_ready.give(nc.scalar.activation(csil[:, i % 2, a:TOK], cout[:, i % 2, a:TOK], ACT.Silu))

            def turned(i):
                b = pa.take(nc.scalar)
                o = (i % 8) * P
                dst, a, n = ((qtok, XW, 2), (ktok, 0, NT), (vtok, 0, NT))[i // 8]
                pa.release(nc.scalar.activation(dst[:, 0:n, o:o + P], b[:, a:TOK].rearrange("p (t c) -> p t c", t=n), ACT.Copy))

            pad_ready.take(nc.scalar)
            for i in range(26):
                if i < 24:
                    b = pa.take(nc.scalar)
                    s = 1 if i < 8 else 0
                    pa.release(nc.scalar.activation(cpad[:, i % 2, s:2, 2:2 + XW],
                                                    b[:, s * XW:TOK].rearrange("p (s c) -> p s c", s=2 - s), ACT.Copy))
                    mark["cv", i] = pa.left
                if 1 <= i < 25:
                    silu(i - 1)
                if i >= 2:
                    turned(i - 2)
            b = pa.take(nc.scalar)
            pa.release(nc.scalar.activation(abt, b[:, 0:128].rearrange("p (t c) -> p t c", t=NT), ACT.Copy))
            mark["ab"] = pa.left
            for c in range(2):
                for t in range(2):
                    b = pa.take(nc.scalar)
                    pa.release(nc.scalar.activation(zgs[:, t, c * 512:(c + 1) * 512], b[:, :], ACT.Silu))
            mark["zg"] = pa.left
            gate_in.take(nc.scalar)
            ac(nc.scalar.activation(gn, gn, ACT.Exp))
            ac(nc.scalar.activation(beta, beta, ACT.Exp))
            gate_out.give(nc.scalar.activation(ealog, sm("alog"), ACT.Exp))
            gate_in.take(nc.scalar)
            gate_out.give(nc.scalar.activation(gn, gn, ACT.Ln))
            gate_in.take(nc.scalar)
            ac(nc.scalar.activation(eg, gct[:, 0:64], ACT.Exp))
            ac(nc.scalar.activation(ed, ed, ACT.Exp))
            gate_out.give(nc.scalar.activation(glb, gct[:, 128:256], ACT.Exp))
            act_sqrt(48)

        def dve_dn_project(dv):
            pad_ready.give(nc.vector.memset(cpad, 0.0))
            for i in range(24):
                nc.vector.wait_ge(pa.free, mark["cv", i])
                s = 1 if i < 8 else 0
                o = cout[:, i % 2, s * XW:TOK].rearrange("p (s c) -> p s c", s=2 - s)
                for j in range(CONV):
                    v = cpad[:, i % 2, s:2, j:j + XW]
                    if j == 0:
                        dv(nc.vector.tensor_scalar(o, v, convw[:, i, 0:1], None, ALU.mult))
                    else:
                        ins = nc.vector.scalar_tensor_tensor(out=o, in0=v, scalar=convw[:, i, j:j + 1], in1=o,
                                                             op0=ALU.mult, op1=ALU.add)
                        conv_ready.give(ins) if j == CONV - 1 else dv(ins)
            nc.vector.wait_ge(pa.free, mark["ab"])
            a_in = abt[:, :, 0:16].rearrange("p t (d h) -> p t d h", d=2)
            b_in = abt[:, :, 16:32].rearrange("p t (d h) -> p t d h", d=2)
            tdh = lambda v: dth(v).rearrange("p d t h -> p t d h")
            dtb = sm("dtb").rearrange("p (d h) -> p d h", d=2).unsqueeze(1).to_broadcast([P, NT, 2, 8])
            dv(nc.vector.tensor_tensor(tdh(ga), a_in, dtb, ALU.add))
            dv(nc.vector.tensor_scalar(gn, ga, -1.0, None, ALU.mult))
            dv(nc.vector.tensor_tensor(gn, gn, ga, ALU.min))
            dv(nc.vector.tensor_scalar(gm, ga, 0.0, None, ALU.max))
            gate_in.give(nc.vector.tensor_scalar(tdh(beta), b_in, -1.0, None, ALU.mult))
            gate_out.take(nc.vector)
            dv(nc.vector.tensor_scalar_add(beta, beta, 1.0))
            dv(nc.vector.reciprocal(beta, beta))
            gate_in.give(nc.vector.tensor_scalar_add(gn, gn, 1.0))
            gate_out.take(nc.vector)
            dv(nc.vector.tensor_tensor(gm, gm, gn, ALU.add))
            ea = ealog.rearrange("p (d h) -> p d h", d=2).unsqueeze(2).to_broadcast([P, 2, NT, 8])
            g_ready.give(nc.vector.tensor_tensor(dth(gg), dth(gm), ea, ALU.mult))
            b = pv.take(nc.vector)
            pv.release(nc.vector.tensor_scalar(gct, b[:, 0:256], -1.0, None, ALU.mult))
            nc.vector.wait_ge(pv.free, pv.left)
            gate_in.give(nc.vector.tensor_tensor(ed, gct[:, 64:128], gct[:, 0:64], ALU.subtract))
            gate_out.take(nc.vector)
            dv(nc.vector.tensor_tensor(bek, beta, eg, ALU.mult))
            nc.vector.wait_ge(pa.free, mark["zg"])
            rows = [(ktok, t) for t in range(NT)] + [(qtok, t) for t in range(2)]
            for n, (v, t) in enumerate(rows):
                dv(nc.vector.tensor_tensor(sqb[:, 0:D], v[:, t, :], v[:, t, :], ALU.mult))
                dv(nc.vector.tensor_reduce(stat[:, 0, n * 8:n * 8 + 8], sqb[:, 0:D].rearrange("p (h c) -> p h c", h=8), AX.X, ALU.add))
            var_ready.give(nc.vector.tensor_scalar(stat[:, 1, 0:48], stat[:, 0, 0:48], EPS, None, ALU.add))
            dve_rstd(dv, 48)
            dv(nc.vector.tensor_scalar(stat[:, 2, 32:48], stat[:, 2, 32:48], float(P) ** -0.5, None, ALU.mult))
            for n, (v, t) in enumerate(rows):
                w = v[:, t, :].rearrange("p (h c) -> p h c", h=8)
                ins = nc.vector.tensor_tensor(w, w, stat[:, 2, n * 8:n * 8 + 8].unsqueeze(2).to_broadcast([P, 8, P]), ALU.mult)
                norm_ready.give(ins) if n == len(rows) - 1 else dv(ins)
            nc.vector.wait_ge(norm_ready.sem, norm_ready.made)
            nc.vector.wait_ge(pa.full, mark["dn_hT"])

        def pe_dn_group(gp):
            for hh in range(2):
                b = pa.open(nc.tensor)
                for t in AT:
                    o = (2 * gp + hh) * P
                    last = nc.tensor.transpose(b[:, t * P:(t + 1) * P], ktok[:, t, o:o + P], ident)
                pa.close(last)
            b = pa.open(nc.tensor)
            for hh in range(2):
                for t in range(2):
                    o = (2 * gp + hh) * P
                    last = nc.tensor.transpose(b[:, (hh * 2 + t) * P:(hh * 2 + t + 1) * P], qtok[:, t, o:o + P], ident)
            pa.close(last)
            pa.drain(nc.tensor)
            for pair in DT:
                x_pair = pair[0] >= CTX_TILES
                for r, t in enumerate(pair):
                    tt = slice(t * P, (t + 1) * P)
                    operand_ready.take(nc.tensor)
                    b = pv.open(nc.tensor)
                    pv.close(nc.tensor.matmul(b[:, :], ones, dgc[:, r].rearrange("p u c -> p (u c)"), start=True, stop=True))
                    b = ps.open(nc.tensor)
                    for hh in range(2):
                        last = nc.tensor.matmul(b[:, hh * P:(hh + 1) * P], kTg[:, hh, tt], kTg[:, hh, tt], start=True, stop=True)
                        if x_pair:
                            a = (t - CTX_TILES) * P
                            last = nc.tensor.matmul(b[:, 256 + hh * P:256 + (hh + 1) * P], qTg[:, hh, a:a + P], kTg[:, hh, tt],
                                                    start=True, stop=True)
                    ps.close(last)
                for r, t in enumerate(pair):
                    operand_ready.take(nc.tensor)
                    b = pv.open(nc.tensor)
                    for u in range(4):
                        last = nc.tensor.transpose(b[:, u * P:(u + 1) * P], Lm[:, r, u, :], ident)
                    pv.close(last)
                    if x_pair:
                        b = pa.open(nc.tensor)
                        for u in range(4):
                            last = nc.tensor.transpose(b[:, u * P:(u + 1) * P], Am[:, r, u, :], ident)
                        pa.close(last)
                for li in range(1, len(LEVELS)):
                    for r, t in enumerate(pair):
                        operand_ready.take(nc.tensor)
                        b = pa.open(nc.tensor)
                        for u in range(4):
                            last = nc.tensor.matmul(b[:, u * P:(u + 1) * P], CTm[:, r, u, :], Xm[:, r, u, :], start=True, stop=True)
                        pa.close(last)
                        level_job[r] = pa.opened
                    for r, t in enumerate(pair):
                        nc.tensor.wait_ge(pa.free, level_job[r])
                        if li < len(LEVELS) - 1:
                            b = ps.open(nc.tensor)
                            for u in range(4):
                                last = nc.tensor.matmul(b[:, u * P:(u + 1) * P], XTm[:, r, u, :], Pm[:, r, u, :], start=True, stop=True)
                            ps.close(last)
                        b = pv.open(nc.tensor)
                        for u in range(4):
                            last = nc.tensor.matmul(b[:, u * P:(u + 1) * P], Pm[:, r, u, :], XTm[:, r, u, :], start=True, stop=True)
                        pv.close(last)
                for r, t in enumerate(pair):
                    operand_ready.take(nc.tensor)
                    b = pa.open(nc.tensor)
                    for u in range(4):
                        last = nc.tensor.matmul(b[:, u * P:(u + 1) * P], XTm[:, r, u, :], vbm[:, r, u, :], start=True, stop=True)
                    pa.close(last)
                    b = pa.open(nc.tensor)
                    for u in range(4):
                        last = nc.tensor.matmul(b[:, u * P:(u + 1) * P], kbm[:, r, u, :], XTm[:, r, u, :], start=True, stop=True)
                    pa.close(last)
                    if x_pair:
                        b = pa.open(nc.tensor)
                        for u in range(4):
                            last = nc.tensor.transpose(b[:, u * P:(u + 1) * P], qem[:, r, u, :], ident)
                        pa.close(last)
            pa.drain(nc.tensor)
            for n in range(8):
                if n == 0:
                    operand_ready.take(nc.tensor)
                else:
                    ps.drain(nc.tensor)
                b = pv.open(nc.tensor)
                for u in range(4):
                    t, c = chunk_of(n, u % 2)
                    r = slice(c * CH, (c + 1) * CH)
                    last = nc.tensor.matmul(b[r, u * P:(u + 1) * P], wTg[:, t, u, r], S[:, u, :], start=True, stop=True)
                pv.close(last)
                vn_ready.take(nc.tensor)
                if n >= 4:
                    b = po.open(nc.tensor)
                    for u in range(4):
                        t, c = chunk_of(n, u % 2)
                        r = slice(c * CH, (c + 1) * CH)
                        nc.tensor.matmul(b[r, u * P:(u + 1) * P], qdTg[:, t - CTX_TILES, u, r], S[:, u, :], start=True, stop=False)
                        last = nc.tensor.matmul(b[r, u * P:(u + 1) * P], ATg[:, t - CTX_TILES, u, r], vn[:, u, :],
                                                start=False, stop=True)
                    po.close(last)
                b = ps.open(nc.tensor)
                for u in range(4):
                    t, c = chunk_of(n, u % 2)
                    last = nc.tensor.matmul(b[:, u * P:(u + 1) * P], kdg[:, t, u, :], vn[:, u, :], start=True, stop=True)
                ps.close(last)

        level_job = [0, 0]

        def chunk_of(n, d):
            c = n if d == 0 else (3 - n if n < 4 else 11 - n)
            return c // 2, c % 2

        def act_dn_group(gp):
            def copy4(dst):
                b = pa.take(nc.scalar)
                pa.release(nc.scalar.activation(dst, b[:, :].rearrange("p (u c) -> p u c", u=4), ACT.Copy))

            for hh in range(2):
                b = pa.take(nc.scalar)
                pa.release(nc.scalar.activation(kTg[:, hh, :], b[:, :], ACT.Copy))
            b = pa.take(nc.scalar)
            pa.release(nc.scalar.activation(qTg, b[:, :].rearrange("p (h t) -> p h t", h=2), ACT.Copy))
            for pair in DT:
                x_pair = pair[0] >= CTX_TILES
                for r, t in enumerate(pair):
                    dec_in.take(nc.scalar)
                    dec_exp.give(nc.scalar.activation(dec[:, r], dec[:, r], ACT.Exp, scale=-1.0))
                if x_pair:
                    for r, t in enumerate(pair):
                        copy4(ATg[:, r])
                    mark["at", gp] = pa.left
                for li in range(1, len(LEVELS)):
                    for r, t in enumerate(pair):
                        copy4(Pm[:, r])
                for r, t in enumerate(pair):
                    copy4(ug[:, t])
                    copy4(wTg[:, t])
                    if x_pair:
                        copy4(qdTg[:, r])
            mark["pre", gp] = pa.left

        def dve_dn_group(dv, gp):
            heads = slice(2 * gp * P, 2 * (gp + 1) * P)
            for pair in DT:
                x_pair = pair[0] >= CTX_TILES
                for r, t in enumerate(pair):
                    operand_ready.give(nc.vector.tensor_tensor(u4(dgc[:, r]), u4(identu), unit_scalars(gct[:, 0:64], gp, t), ALU.mult))
                    b = pv.take(nc.vector)
                    pv.release(nc.vector.tensor_tensor(u4(dec[:, r]), b[:, :].rearrange("p (h d c) -> p h d c", h=2, d=2),
                                                       unit_scalars(gct[:, 0:64], gp, t), ALU.subtract))
                    nc.vector.wait_ge(pv.free, pv.left)
                    dec_in.give(nc.vector.tensor_scalar(dec[:, r], dec[:, r], 0.0, None, ALU.max))
                for r, t in enumerate(pair):
                    dec_exp.take(nc.vector)
                    dv(nc.vector.tensor_tensor(u4(dec[:, r]), u4(dec[:, r]), over_heads(incl), ALU.mult))
                    b = ps.take(nc.vector)
                    ins = nc.vector.tensor_tensor(u4(Lm[:, r]), u4(dec[:, r]),
                                                  over_dirs(b[:, 0:256].rearrange("p (h c) -> p h c", h=2)), ALU.mult)
                    if x_pair:
                        dv(ins)
                        ins = nc.vector.tensor_tensor(u4(Am[:, r]), u4(dec[:, r]),
                                                      over_dirs(b[:, 256:512].rearrange("p (h c) -> p h c", h=2)), ALU.mult)
                    ps.release(ins)
                    nc.vector.wait_ge(ps.free, ps.left)
                    dv(nc.vector.tensor_tensor(u4(Lm[:, r]), u4(Lm[:, r]), unit_scalars(beta, gp, t), ALU.mult))
                    operand_ready.give(nc.vector.tensor_tensor(u4(Lm[:, r]), u4(Lm[:, r]), over_heads(strict), ALU.mult))
                for r, t in enumerate(pair):
                    b = pv.take(nc.vector)
                    pv.release(nc.vector.tensor_copy(LTm[:, r], b[:, :].rearrange("p (u c) -> p u c", u=4)))
                    nc.vector.wait_ge(pv.free, pv.left)
                    for dst, src, m in ((Xm, Lm, lvl[:, 0, 0:2]), (XTm, LTm, lvl[:, 0, 1:3])):
                        dv(nc.vector.tensor_tensor(u4(dst[:, r]), u4(src[:, r]), over_heads(m), ALU.mult))
                        dv(nc.vector.tensor_tensor(dst[:, r], identu, dst[:, r], ALU.subtract))
                if x_pair:
                    nc.vector.wait_ge(pa.full, mark["at", gp])
                for li in range(1, len(LEVELS)):
                    for r, t in enumerate(pair):
                        operand_ready.give(nc.vector.tensor_tensor(u4(CTm[:, r]), u4(LTm[:, r]), over_heads(lvl[:, li, 1:3]), ALU.mult))
                    for r, t in enumerate(pair):
                        if li < len(LEVELS) - 1:
                            b = ps.take(nc.vector)
                            ps.release(nc.vector.tensor_tensor(Xm[:, r], Xm[:, r], b[:, :].rearrange("p (u c) -> p u c", u=4), ALU.subtract))
                        b = pv.take(nc.vector)
                        pv.release(nc.vector.tensor_tensor(XTm[:, r], XTm[:, r], b[:, :].rearrange("p (u c) -> p u c", u=4), ALU.subtract))
                    nc.vector.wait_ge(pv.free, pv.left)
                    nc.vector.wait_ge(ps.free, ps.left)
                for r, t in enumerate(pair):
                    kh = over_dirs(ktok[:, t, heads].rearrange("p (h c) -> p h c", h=2))
                    vh = over_dirs(vtok[:, t, heads].rearrange("p (h c) -> p h c", h=2))
                    dv(nc.vector.tensor_tensor(u4(vbm[:, r]), vh, unit_scalars(beta, gp, t), ALU.mult))
                    dv(nc.vector.tensor_tensor(u4(kdg[:, t]), kh, unit_scalars(ed, gp, t), ALU.mult))
                    if x_pair:
                        qh = over_dirs(qtok[:, t - CTX_TILES, heads].rearrange("p (h c) -> p h c", h=2))
                        dv(nc.vector.tensor_tensor(u4(qem[:, r]), qh, unit_scalars(eg, gp, t), ALU.mult))
                    operand_ready.give(nc.vector.tensor_tensor(u4(kbm[:, r]), kh, unit_scalars(bek, gp, t), ALU.mult))
            nc.vector.wait_ge(pa.free, mark["pre", gp])
            dv(nc.vector.memset(vn, 0.0))
            operand_ready.give(nc.vector.memset(S, 0.0))
            nc.vector.wait_ge(operand_ready.sem, operand_ready.made)
            for n in range(8):
                b = pv.take(nc.vector)
                for d in range(2):
                    t, c = chunk_of(n, d)
                    r = slice(c * CH, (c + 1) * CH)
                    by_dir = lambda v: v.rearrange("p (h d) c -> p h d c", h=2)[r, :, d, :]
                    ins = nc.vector.tensor_tensor(by_dir(vn), by_dir(ug[:, t]),
                                                  by_dir(b[:, :].rearrange("p (u c) -> p u c", u=4)), ALU.subtract)
                    dv(ins) if d == 0 else pv.release(ins)
                nc.vector.wait_ge(pv.free, pv.left)
                vn_ready.give(nc.vector.tensor_copy(negs[:, 0:1], vn[:, 0, 0:1]))
                b = ps.take(nc.vector)
                for u in range(4):
                    t, c = chunk_of(n, u % 2)
                    o = (c * 2 + u % 2) * 32 + t * 8 + 2 * gp + u // 2
                    ins = nc.vector.scalar_tensor_tensor(out=S[:, u, :], in0=S[:, u, :], scalar=glb[:, o:o + 1],
                                                         in1=b[:, u * P:(u + 1) * P], op0=ALU.mult, op1=ALU.add)
                    dv(ins) if u < 3 else ps.release(ins)
                nc.vector.wait_ge(ps.free, ps.left)
                if n < 7:
                    dv(nc.vector.memset(vn, 0.0))
                if n >= 4:
                    b = po.take(nc.vector)
                    for d in range(2):
                        t, c = chunk_of(n, d)
                        r = slice(c * CH, (c + 1) * CH)
                        dst = qtok[r, t - CTX_TILES, heads].rearrange("p (h c) -> p h c", h=2)
                        src = b[r, :].rearrange("p (h d c) -> p h d c", h=2, d=2)[:, :, d, :]
                        if n < 6:
                            ins = nc.vector.tensor_copy(dst, src)
                        else:
                            ins = nc.vector.tensor_tensor(dst, dst, src, ALU.add)
                        dv(ins) if d == 0 else po.release(ins)
                    nc.vector.wait_ge(po.free, po.left)

        def dve_dn_out(dv):
            for t in range(2):
                dv(nc.vector.tensor_tensor(sqb[:, 0:D], qtok[:, t, :], qtok[:, t, :], ALU.mult))
                dv(nc.vector.tensor_reduce(stat[:, 0, t * 8:t * 8 + 8], sqb[:, 0:D].rearrange("p (h c) -> p h c", h=8), AX.X, ALU.add))
            var_ready.give(nc.vector.tensor_scalar(stat[:, 1, 0:16], stat[:, 0, 0:16], 1.0 / P, EPS, ALU.mult, ALU.add))
            dve_rstd(dv, 16)
            for t in range(2):
                v = qtok[:, t, :].rearrange("p (h c) -> p h c", h=8)
                dv(nc.vector.tensor_tensor(v, v, stat[:, 2, t * 8:t * 8 + 8].unsqueeze(2).to_broadcast([P, 8, P]), ALU.mult))
                dv(nc.vector.tensor_tensor(v, v, sm("onorm").unsqueeze(1).to_broadcast([P, 8, P]), ALU.mult))
                o_ready.give(nc.vector.tensor_tensor(qtok[:, t, :], qtok[:, t, :], zgs[:, t, :], ALU.mult))

        def pe_dn():
            pe_dn_project()
            norm_ready.take(nc.tensor)
            for gp in range(NG):
                pe_dn_group(gp)
            mark["dn_done"] = (ps.full, ps.closed)
            for t in range(2):
                o_ready.take(nc.tensor)
                for half in range(2):
                    b = pa.open(nc.tensor)
                    for q in range(4):
                        kk = half * 4 + q
                        last = nc.tensor.transpose(b[:, q * P:(q + 1) * P], qtok[:, t, kk * P:(kk + 1) * P], ident)
                    pa.close(last)
            pa.drain(nc.tensor)

        def act_dn(ac):
            act_dn_project(ac)
            for gp in range(NG):
                act_dn_group(gp)
            act_sqrt(16)

        def dve_dn(dv):
            dve_dn_project(dv)
            for gp in range(NG):
                dve_dn_group(dv, gp)
            dve_dn_out(dv)

        mark = {}
        AT = range(NT)
        block = es.enter_context(nc.Block())

        @block.tensor
        def _(pe):
            pe.wait_ge(p_ld, 16 * N_PARAM)
            pe_ada(0)
            pe_ada(1)
            mark["ada"] = pv.closed
            pe_bcast(0, 0)
            pe_turn(xn, AT, xn_ready)
            pe_lin(W_EVIN, (512, 512, 512, 416), hT, AT, pa)
            pe_heads()
            pe_attn()
            pe_turn(o_tok, AT, o_ready)
            pe_lin(W_EVOUT, (512, 512), oT, AT, pv)
            if stop >= 2:
                pe_bcast(0, 1)
                pe_turn(htok, AT, xn_ready)
                pe_query(0)
                pv.drain(pe)
                pe_peer(0)
            if stop >= 3:
                pe_bcast(1, 0)
                pe_turn(xn, AT, xn_ready)
                pe_dn()
                pe_lin(W_DNOUT, (512, 512), oT, XT, pv)
            if stop >= 4:
                pe_bcast(1, 1)
                pe_turn(htok, XT, xn_ready)
                pe_query(1)
                pv.drain(pe)
                pe_peer(1)

        @block.scalar
        def _(act):
            ac = Chain(act, act_sem)
            act_silu(ac)
            act_bcast(0, 0)
            act.wait_ge(ctx_ld, 32)
            act_norm(ac, 0, 0, AT)
            act_z()
            act_heads()
            act_attn()
            act_sqrt(4 * NT)
            act_turn(oT, AT)
            if stop >= 2:
                act_bcast(0, 1)
                act_norm(ac, 0, 1, AT)
                act_query(0)
                act_peer(0)
            if stop >= 3:
                act_bcast(1, 0)
                act_norm(ac, 1, 0, AT)
                act_dn(ac)
                act_turn(oT, XT)
            if stop >= 4:
                act_bcast(1, 1)
                act_norm(ac, 1, 1, XT)
                act_query(1)
                act_peer(1)

        @block.vector
        def _(dve):
            dv = Chain(dve, dve_sem)
            dve.wait_ge(p_ld, 16 * N_PARAM)
            dve_silu(dv)
            dve_ada(dv, 0)
            dve_ada(dv, 1)
            dve_bcast(dv, 0, 0)
            dve_norm(dv, 0, 0, AT)
            dve_heads(dv)
            dve_attn(dv)
            dve_residual(dv, AT, tmpv[:, 0:512])
            if stop >= 2:
                dve_bcast(dv, 0, 1)
                dve.wait_ge(pa.free, mark["bc01"])
                dve_norm(dv, 0, 1, AT)
                dve_peer(dv, 0)
            if stop >= 3:
                dve_bcast(dv, 1, 0)
                dve_norm(dv, 1, 0, AT)
                dve_dn(dv)
                dve_residual(dv, XT, junk[:, 0:512])
            if stop >= 4:
                dve_bcast(dv, 1, 1)
                dve.wait_ge(pa.free, mark["bc11"])
                dve_norm(dv, 1, 1, XT)
                dve_peer(dv, 1)

        @block.gpsimd
        def _(pool):
            if stop >= 2:
                pool_peer(0)
            if stop >= 4:
                pool_peer(1)

        @block.sync
        def _(sp):
            for dst, src in ((cs[:, 0, :], cT), (cst[:], consts), (adab[:], ada_b), (smallp[:], small),
                             (keys[:], keysT), (convw[:], conv_w), (wab[:], w_ab)):
                sp.dma_start(dst, src).then_inc(p_ld, 16)
            for n in range(2 * ADA_G):
                if n >= 2:
                    sp.wait_ge(pv.full, n - 1)
                sp.dma_start(adaw[:, n % 2], ada_w[n // ADA_G, n % ADA_G]).then_inc(ada_ld[n % 2], 16)
                if n == 3:
                    sp.dma_start(R[:, 0:CTX_TILES, :], ctx_in[0].rearrange("(t p) d -> p t d", p=P)).then_inc(ctx_ld, 16)
                    sp.dma_start(R[:, CTX_TILES:NT, :], x[0].rearrange("(t p) d -> p t d", p=P)).then_inc(ctx_ld, 16)
            sp.dma_start(wuq_sb, w_uq).then_inc(mla_ld, 16)
            sp.dma_start(wukv_sb, w_ukv).then_inc(mla_ld, 16)
            for w in range(W_END if stop >= 4 else (W_WQ0, W_DNIN, W_WQ1)[stop - 1]):
                if w >= 2:
                    sp.wait_ge(*w_done[w - 2]) if w - 2 in w_done else None
                if w == W_DNOUT + 1:
                    sp.wait_ge(*mark["dn_done"])
                if w in (W_DNIN, W_DNIN + 1):
                    sp.wait_ge(v_read, NT * HEADS * TOPK)
                sp.dma_start(wbuf[:, w % 2], wstream[w]).then_inc(w_ld[w % 2], 16)
            sp.wait_ge(r_ready.sem, r_ready.made)
            if stop >= 4:
                sp.dma_start(out[0].rearrange("(t p) d -> p t d", p=P), R[:, CTX_TILES:NT, :]).then_inc(out_st, 16)
            else:
                sp.dma_start(out.rearrange("t p d -> p t d"), R[:, :, :]).then_inc(out_st, 16)
            sp.wait_ge(out_st, 16)


STOP = 9


def _shape_constants():
    import numpy as np
    c = {}
    i = np.arange(P)[:, None]
    j = np.arange(P)[None, :]
    same = (i // 64) == (j // 64)
    c["ident"] = (i == j)
    c["ones"] = np.ones((P, P))
    c["blk"] = same
    c["incl"] = np.concatenate([same & (i >= j), same & (i <= j)], 1)
    c["strict"] = np.concatenate([same & (i > j), same & (i < j)], 1)
    lv = []
    for m in LEVELS:
        f = (i // m % 2 == 1) & (j // m == i // m - 1)
        lv += [f, f.T, f]
    c["lvl"] = np.concatenate(lv, 1)
    c["iota"] = np.broadcast_to(np.arange(16), (P, 16))
    tok = np.arange(256)
    for name, rot in (("A", 64), ("B", 32)):
        nf = rot // 4
        inv = (np.float32(10000.0) ** (-np.arange(nf, dtype=np.float32) / np.float32(nf))).astype(np.float32)
        ang = np.concatenate([(tok // 64)[:, None].astype(np.float32) * inv,
                              (tok % 64)[:, None].astype(np.float32) * inv], 1)
        for f, n in ((np.cos, "cos"), (np.sin, "sin")):
            c[n + name] = f(ang).reshape(2, P, rot // 2).transpose(1, 0, 2).reshape(P, -1)
    return np.ascontiguousarray(np.concatenate([c[n].astype(np.float32) for n in CONST], 1))


def kernel(x, c, ctx, c_ctx, ada_w, ada_b, ev_w_in, ev_w_out, diff_q_norm, diff_k_norm,
           diff_lam_q1, diff_lam_k1, diff_lam_q2, diff_lam_k2, diff_subln, mla_cq_norm, mla_ckv_norm,
           mla_w_uq, mla_w_ukv, mla_q_norm, mla_k_norm, dn_w_in, dn_conv, dn_a_log, dn_dt_bias,
           dn_o_norm, dn_w_out, peer_wq, peer_k1, peer_k2, peer_u, peer_v):
    import numpy as np
    import concourse.bacc as _bacc
    from concourse import mybir as _mybir
    from concourse.bass_utils import run_bass_kernel_spmd as _run

    cc = np.ascontiguousarray

    def chunks(w):
        n = -(-w.shape[1] // WCH)
        full = np.zeros((D, n * WCH), w.dtype)
        full[:, :w.shape[1]] = w
        return full.reshape(KD, P, n, WCH).transpose(2, 1, 0, 3)

    c2 = np.stack([np.asarray(c_ctx), np.asarray(c)[0]], 0)
    rows = [np.asarray(v).reshape(-1) for v in (
        diff_q_norm, diff_k_norm, diff_subln, mla_cq_norm, mla_ckv_norm, mla_q_norm, mla_k_norm, dn_o_norm,
        diff_lam_q1, diff_lam_k1, diff_lam_q2, diff_lam_k2, dn_a_log, dn_dt_bias)]
    keysT = np.stack([np.asarray(peer_k1), np.asarray(peer_k2)], 1)
    dn = np.asarray(dn_w_in)[0]
    wq = np.asarray(peer_wq)
    arrays = {
        "x": cc(x), "ctx_in": cc(ctx),
        "cT": cc(c2.reshape(2, KD, P).transpose(2, 1, 0).reshape(P, 2 * KD)),
        "ada_w": cc(np.asarray(ada_w).reshape(2, KD, P, ADA_G, ADA_J, P).transpose(0, 3, 2, 4, 1, 5)),
        "ada_b": cc(np.asarray(ada_b).reshape(2, 48, P).transpose(2, 0, 1)),
        "wstream": cc(np.concatenate([chunks(np.asarray(ev_w_in)[0]), chunks(np.asarray(ev_w_out)[0]), chunks(wq[0]),
                                      chunks(dn[:, :4096]), chunks(np.asarray(dn_w_out)[0]), chunks(wq[1])], 0)),
        "small": cc(np.broadcast_to(np.concatenate(rows)[None, :], (P, SMALL_W))),
        "consts": _shape_constants(),
        "keysT": cc(keysT.transpose(3, 0, 1, 2)),
        "w_uq": cc(np.asarray(mla_w_uq)[0].reshape(2, P, 384).transpose(1, 0, 2).reshape(P, 768)),
        "w_ukv": cc(np.asarray(mla_w_ukv)[0]),
        "conv_w": cc(np.asarray(dn_conv)[0].reshape(5, 24, P).transpose(2, 1, 0)),
        "w_ab": cc(dn[:, 4096:].reshape(KD, P, 32).transpose(1, 0, 2)),
        "peer_u0": np.asarray(peer_u)[0], "peer_v0": np.asarray(peer_v)[0],
        "peer_u1": np.asarray(peer_u)[1], "peer_v1": np.asarray(peer_v)[1],
    }
    nc = _bacc.Bacc("TRN2", target_bir_lowering=False, num_devices=1)
    args = {n: nc.dram_tensor(f"in_{n}_dram", a.shape, _mybir.dt.from_np(a.dtype), kind="ExternalInput").ap()
            for n, a in arrays.items()}
    shape = (1, 256, D) if STOP >= 4 else (NT, P, D)
    out = nc.dram_tensor("out_0_dram", shape, _mybir.dt.float32, kind="ExternalOutput").ap()
    build(nc, out=out, stop=STOP, **args)
    r = _run(nc, [{f"in_{n}_dram": a for n, a in arrays.items()}], core_ids=[0])
    return r.results[0]["out_0_dram"]
```

```python
from contextlib import ExitStack

import concourse.bass as bass
from concourse import mybir

F32 = mybir.dt.float32
U32 = mybir.dt.uint32
ALU = mybir.AluOpType
ACT = mybir.ActivationFunctionType
AX = mybir.AxisListType

P = 128
D = 1024
KD = D // P
NT = 4
CTX_TILES = 2
TOK = NT * P
EPS = 1e-6
LAM_INIT = 0.2
DH = 4
MH = 4
ZW = 1952
QK96 = 96
HEADS = 8
NK = 128
TOPK = 16
RING = 8
NEG = -3.0e38
WCH = 512
ADA_C = 12
N_PARAM = 6
XT = range(CTX_TILES, NT)

SMALL = {}
_at = 0
for _n, _w in (("qn", 64), ("kn", 64), ("subln", 128), ("cqn", 256), ("ckvn", 128), ("mqn", 96), ("mkn", 96),
               ("onorm", 128), ("lq1", 64), ("lk1", 64), ("lq2", 64), ("lk2", 64), ("alog", 16), ("dtb", 16)):
    SMALL[_n] = (_at, _w)
    _at += _w
SMALL_W = _at
LEVELS = (1, 2, 4, 8, 16, 32)
CONST = {}
_at = 0
for _n, _w in (("ident", 128), ("ones", 128), ("blk", 128), ("incl", 256), ("strict", 256),
               ("lvl", 3 * 128 * len(LEVELS)), ("iota", 16), ("cosA", 64), ("sinA", 64), ("cosB", 32), ("sinB", 32)):
    CONST[_n] = (_at, _w)
    _at += _w
CONST_W = _at

W_ADA0, W_EVIN, W_ADA1, W_EVOUT, W_WQ0, W_DNIN, W_DNOUT, W_WQ1, W_END = 0, 12, 16, 28, 30, 34, 42, 44, 48


class Signal:

    def __init__(self, sem):
        self.sem, self.made, self.taken = sem, 0, 0

    def give(self, ins):
        self.made += 1
        ins.then_inc(self.sem, 1)

    def take(self, eng):
        self.taken += 1
        eng.wait_ge(self.sem, self.taken)


class Chain:

    def __init__(self, eng, sem):
        self.eng, self.sem, self.n, self.base = eng, sem, 0, 0

    def __call__(self, ins):
        self.n += 1
        ins.then_inc(self.sem, 1)
        self.eng.wait_ge(self.sem, self.base + self.n)

    def alone(self, mark):
        if not isinstance(self.base, int):
            self.eng.sem_inc(mark, 1)


class Pipe:

    def __init__(self, banks, full, free):
        self.banks, self.full, self.free = banks, full, free
        self.opened = self.closed = self.read = self.left = 0

    def open(self, pe):
        if self.opened >= 2:
            pe.wait_ge(self.free, self.opened - 1)
        self.opened += 1
        return self.banks[(self.opened - 1) % 2]

    def close(self, ins):
        self.closed += 1
        ins.then_inc(self.full, 1)

    def drain(self, pe):
        pe.wait_ge(self.free, self.opened)

    def take(self, eng):
        self.read += 1
        eng.wait_ge(self.full, self.read)
        return self.banks[(self.read - 1) % 2]

    def release(self, ins):
        self.left += 1
        ins.then_inc(self.free, 1)


def build(nc, x, ctx_in, cT, ada_b, wstream, small, consts, keysT, w_uq, w_ukv, conv_w, w_ab,
          peer_u0, peer_v0, peer_u1, peer_v1, out, stop=9):
    with ExitStack() as es:
        def sb(name, shape, dt=F32):
            return es.enter_context(nc.sbuf_tensor(name, shape, dt))

        def sem(name):
            return es.enter_context(nc.semaphore(name))

        bank = [es.enter_context(nc.psum_tensor(f"bank{i}", [P, 512], F32)) for i in range(8)]

        R = sb("R", [P, NT, D])
        hT = sb("hT", [P, KD, TOK])
        htok = sb("htok", [P, NT, D])
        wbuf = sb("wbuf", [P, 2, KD, WCH])
        bc = sb("bc", [P, 4, 2, D])
        cst = sb("cst", [P, CONST_W])
        smallp = sb("smallp", [P, SMALL_W])
        keys = sb("keys", [P, 2, 2, NK])
        convw = sb("convw", [P, 24, 5])
        wab = sb("wab", [P, KD, 32])
        cs = sb("cs", [P, 3, KD * 2])
        modT = sb("modT", [P, 2, 16, 2])
        stat = sb("stat", [P, 3, 80])
        lamt = sb("lamt", [P, 72])
        negs = sb("negs", [P, 8])
        SCR = 18432
        scr = sb("scr", [P, SCR])

        def k(name):
            o, w = CONST[name]
            return cst[:, o:o + w]

        def sm(name):
            o, w = SMALL[name]
            return smallp[:, o:o + w]

        ident, ones = k("ident"), k("ones")

        c_ld, p_ld, ctx_ld = sem("consts_landed"), sem("params_landed"), sem("streams_landed")
        ab_ld = [sem(f"ada_bias_landed{i}") for i in range(2)]
        row_ready = Signal(sem("mod_row_ready"))
        row_st = [sem(f"mod_row_stored{i}") for i in range(2)]
        bc_ld = sem("mod_vectors_landed")
        vec_free = Signal(sem("mod_vectors_free"))
        w_ld = [sem(f"w_landed{i}") for i in range(2)]
        out_st = sem("out_stored")
        dve_sem, act_sem, pool_sem = sem("vector_step"), sem("scalar_step"), sem("pool_step")
        vec_mark = sem("vector_mark")
        pa = Pipe(bank[0:2], sem("pa_full"), sem("pa_free"))
        pv = Pipe(bank[2:4], sem("pv_full"), sem("pv_free"))
        ps = Pipe(bank[4:6], sem("scores_full"), sem("scores_free"))
        po = Pipe(bank[6:8], sem("po_full"), sem("po_free"))
        silu_in, silu_ready = Signal(sem("silu_exp")), Signal(sem("silu_ready"))
        mods_ready = Signal(sem("mods_ready"))
        r_ready = Signal(sem("residual_ready"))
        ss_ready, var_ready, std_ready = Signal(sem("sumsq_ready")), Signal(sem("var_ready")), Signal(sem("std_ready"))
        xn_ready = Signal(sem("xn_ready"))
        z_ready = Signal(sem("z_ready"))
        heads_ready = Signal(sem("heads_ready"))
        lam_in, lam_ready = Signal(sem("lam_in")), Signal(sem("lam_exp"))
        nmax_ready = Signal(sem("nmax_ready"))
        o_ready = Signal(sem("o_ready"))
        mla_ld = sem("mla_weights_landed")
        u_land = [sem(f"u_landed{i}") for i in range(RING)]
        v_land = [sem(f"v_landed{i}") for i in range(RING)]
        u_read, v_read = sem("u_read"), sem("v_read")
        q_staged, sc_done, idx_ready, top_ready = sem("q_staged"), sem("keyscores_done"), sem("idx_ready"), sem("top_ready")
        exp_done, gelu_done, w_ready, diag_done, y_free = (sem("exp_done"), sem("gelu_done"), sem("w_ready"),
                                                          sem("diag_done"), sem("y_free"))
        q_ready = Signal(sem("q_ready"))
        y_zero = Signal(sem("y_zero"))

        mark = {}
        mods = nc.dram_tensor("mods_scratch", (2, 2, 6 * D), F32, kind="Internal").ap()

        xn = scr[:, 4096:8192].rearrange("p (t d) -> p t d", t=NT)
        junk = scr[:, 8192:9216]

        class Region:
            def __init__(self, whole):
                self.whole, self.at = whole, 0

            def get(self, n):
                a = self.at
                self.at += n
                assert self.at <= self.whole.shape[1], self.at
                return self.whole[:, a:a + n]

        g = Region(scr)
        z = g.get(NT * ZW).rearrange("p (t c) -> p t c", t=NT)
        qkb = g.get(NT * 8 * QK96).rearrange("p (t g c) -> p t g c", t=NT, g=8)
        kvb = g.get(NT * 768).rearrange("p (t c) -> p t c", t=NT)
        bcx = bc[:, 1:3].rearrange("p v s d -> p (v s d)")
        qbT = bcx[:, 0:2048].rearrange("p (h t) -> p h t", h=MH)
        kbT = bcx[:, 2048:4096].rearrange("p (h t) -> p h t", h=MH)
        tmpv = g.get(2048)
        modbuf = scr[:, g.at:g.at + 2048].rearrange("p (s r c) -> p s r c", s=2, r=2)
        mrow, mbias = modbuf[:, 0], modbuf[:, 1]
        wuq_sb = g.get(768).rearrange("p (k c) -> p k c", k=2)
        wukv_sb = g.get(768)
        cT3 = tmpv[:, 0:3 * TOK].rearrange("p (b t) -> p b t", b=3)
        prob = tmpv[:, 0:1024].rearrange("p (s n) -> p s n", s=2)
        probT = tmpv[:, 1024:2048].rearrange("p (s n) -> p s n", s=2)
        rope_t = kvb.rearrange("p t c -> p (t c)")
        qaT = htok[:, 0:2, :].rearrange("p a (b t) -> p (a b) t", b=2)
        kaT = htok[:, 2:4, :].rearrange("p a (b t) -> p (a b) t", b=2)
        o_tok = hT.rearrange("p k t -> p (k t)").rearrange("p (t d) -> p t d", t=NT)
        oT = htok.rearrange("p t d -> p (t d)").rearrange("p (k t) -> p k t", k=KD)
        rsum = lamt[:, 0:48]
        g = Region(scr)
        qT = g.get(NT * HEADS * 2 * P).rearrange("p (s c) -> p s c", c=2 * P)
        uring = g.get(RING * D).rearrange("p (s d) -> p s d", s=RING)
        g = Region(bcx)
        qst = g.get(2 * 256).rearrange("p (s c) -> p s c", s=2)
        sw = g.get(256)
        cand = g.get(256)
        candw = g.get(256)
        v16 = g.get(32)
        i16 = g.get(32).bitcast(U32)
        sc16 = g.get(32).rearrange("p (s c) -> p s c", s=2)
        j16 = g.get(16).bitcast(U32)
        ab16 = g.get(32).bitcast(U32)
        onehot = g.get(512)
        sel = g.get(32)
        idx = g.get(32).bitcast(U32).rearrange("p (s c) -> p s c", s=2)
        e16 = g.get(32).rearrange("p (s c) -> p s c", s=2)
        act16 = g.get(32).rearrange("p (s c) -> p s c", s=2)
        gel16 = g.get(32).rearrange("p (s c) -> p s c", s=2)
        w16 = g.get(32).rearrange("p (s c) -> p s c", s=2)
        nb = g.get(2)
        zs = g.get(4)
        diag = g.get(4 * 128).rearrange("p (s c) -> p s c", s=4)
        vring = wbuf.rearrange("p s k c -> p (s k c)").rearrange("p (s d) -> p s d", s=RING)
        Y = hT.rearrange("p k t -> p (k t)").rearrange("p (t d) -> p t d", t=NT)
        ybank = [(bank[0], bank[1]), (bank[2], bank[3])]
        scbank = bank[4:6]

        def tile_list(l):
            return range(NT)

        def peer_tiles(l):
            return range(NT) if l == 0 else range(CTX_TILES, NT)

        def act_silu(ac):
            nc.scalar.wait_ge(p_ld, 16 * N_PARAM)
            silu_in.give(nc.scalar.activation(cs[:, 1, :], cs[:, 0, :], ACT.Exp, scale=-1.0))

        def dve_silu(dv):
            silu_in.take(nc.vector)
            dv(nc.vector.tensor_scalar_add(cs[:, 1, :], cs[:, 1, :], 1.0))
            dv(nc.vector.reciprocal(cs[:, 2, :], cs[:, 1, :]))
            nc.vector.wait_ge(p_ld, 16 * N_PARAM)
            silu_ready.give(nc.vector.tensor_tensor(cs[:, 2, :], cs[:, 2, :], cs[:, 0, :], ALU.mult))

        def pe_ada(l, c):
            if (l, c) == (0, 0):
                silu_ready.take(nc.tensor)
            w = (W_ADA0, W_ADA1)[l] + c
            nc.tensor.wait_ge(w_ld[w % 2], 16 * (w // 2 + 1))
            b = pa.open(nc.tensor)
            sc = cs[:, 2, :].rearrange("p (k s) -> p k s", k=KD)
            for kk in range(KD):
                last = nc.tensor.matmul(b[0:2, :], sc[:, kk, :], wbuf[:, w % 2, kk, :], start=(kk == 0), stop=(kk == KD - 1))
            pa.close(last)
            used_chunk(w, pa)
            mark["ada", l, c] = pa.closed
            if c < 4:
                b = pa.open(nc.tensor)
                nc.tensor.wait_ge(pa.free, pa.opened - 1)
                for q in range(4):
                    last = nc.tensor.transpose(b[:, 2 * q:2 * q + 2], mrow[0:2, c % 2, q * P:(q + 1) * P], ident[0:2, 0:2])
                pa.close(last)

        def dve_ada(l, c):
            n = l * ADA_C + c
            nc.vector.wait_ge(ab_ld[n % 2], 16 * (n // 2 + 1))
            if n >= 2:
                nc.vector.wait_ge(row_st[n % 2], 16 * (n // 2))
            nc.vector.wait_ge(pa.full, mark["ada", l, c])
            one = 1.0 if c in (2, 3, 8, 9) else 0.0
            nc.vector.scalar_tensor_tensor(out=mrow[0:2, n % 2, :], in0=bank[(mark["ada", l, c] - 1) % 2][0:2, :], scalar=one,
                                           in1=mbias[0:2, n % 2, :], op0=ALU.add, op1=ALU.add).then_inc(pa.free, 1)
            nc.vector.wait_ge(pa.free, mark["ada", l, c])
            row_ready.give(nc.vector.tensor_copy(negs[0:2, 6 + n % 2:7 + n % 2], mrow[0:2, n % 2, 0:1]))
            if c < 4:
                nc.vector.wait_ge(pa.full, mark["ada", l, c] + 1)
                nc.vector.tensor_copy(modT[:, l, 4 * c:4 * c + 4, :],
                                      bank[mark["ada", l, c] % 2][:, 0:8].rearrange("p (q s) -> p q s", q=4)).then_inc(pa.free, 1)
            if c == 3:
                nc.vector.wait_ge(pa.free, mark["ada", l, c] + 1)
                mods_ready.give(nc.vector.tensor_copy(negs[:, 2 + l:3 + l], modT[:, l, 0, 0:1]))

        def act_ada():
            pa.read += ADA_C + 4
            pa.left += ADA_C + 4

        def pool_ada(l):
            for n in range(l * ADA_C, (l + 1) * ADA_C + 2):
                if n < (l + 1) * ADA_C:
                    if l == 1 and n == ADA_C:
                        nc.gpsimd.wait_ge(pa.full, mark["heads"])
                    if n >= 2:
                        nc.gpsimd.wait_ge(row_ready.sem, n - 1)
                    o = (n % ADA_C) * 512
                    nc.gpsimd.dma_start(mbias[0:2, n % 2, :], ada_b[l:l + 1, o:o + 512].to_broadcast([2, 512]))\
                        .then_inc(ab_ld[n % 2], 16)
                m = n - 2
                if m >= l * ADA_C:
                    nc.gpsimd.wait_ge(row_ready.sem, m + 1)
                    o = (m % ADA_C) * 512
                    nc.gpsimd.dma_start(mods[l, :, o:o + 512], mrow[0:2, m % 2, :]).then_inc(row_st[m % 2], 16)

        def pool_vectors(l, part):
            if part == 0:
                for r in range(2):
                    nc.gpsimd.wait_ge(row_st[r], 16 * (l + 1) * ADA_C // 2)
            if (l, part) != (0, 0):
                vec_free.take(nc.gpsimd)
            for v, at in (((0, 2), (3, 5)) if part == 0 else ((1, 3), (2, 4))):
                for s in ((0, 1) if l == 0 else (1,)):
                    nc.gpsimd.dma_start(bc[:, v, s, :], mods[l, s:s + 1, at * D:(at + 1) * D].to_broadcast([P, D]))\
                        .then_inc(bc_ld, 16)

        BC_COUNT = {(0, 0): 4, (0, 1): 8, (1, 0): 10, (1, 1): 12}

        def act_norm(ac, l, sub, tiles):
            if (l, sub) != (0, 0):
                r_ready.take(nc.scalar)
            for t in tiles:
                ac(nc.scalar.activation(junk, R[:, t, :], ACT.Square, accum_out=stat[:, 0, t:t + 1]))
            ss_ready.give(nc.scalar.activation(stat[:, 1, 0:NT], stat[:, 0, 0:NT], ACT.Copy))
            var_ready.take(nc.scalar)
            std_ready.give(nc.scalar.activation(stat[:, 0, 0:NT], stat[:, 1, 0:NT], ACT.Sqrt))
            if sub == 0:
                mods_ready.take(nc.scalar)
                for t in tiles:
                    s = 0 if t < CTX_TILES else 1
                    for half in range(2):
                        b = pa.take(nc.scalar)
                        for q in range(4):
                            kk = half * 4 + q
                            ins = nc.scalar.activation(hT[:, kk, t * P:(t + 1) * P], b[:, q * P:(q + 1) * P],
                                                       ACT.Identity, scale=modT[:, l, 8 + kk, s:s + 1],
                                                       bias=modT[:, l, kk, s:s + 1])
                        pa.release(ins)
            else:
                act_hT(tiles)

        def act_hT(tiles):
            for t in tiles:
                for half in range(2):
                    b = pa.take(nc.scalar)
                    pa.release(nc.scalar.activation(
                        hT[:, half * 4:half * 4 + 4, t * P:(t + 1) * P],
                        b[:, :].rearrange("p (q t) -> p q t", q=4), ACT.Copy))

        def dve_norm(dv, l, sub, tiles):
            t0, t1 = tiles[0], tiles[-1] + 1
            ss_ready.take(nc.vector)
            var_ready.give(nc.vector.tensor_scalar(stat[:, 1, 0:NT], stat[:, 1, 0:NT], 1.0 / D, EPS, ALU.mult, ALU.add))
            std_ready.take(nc.vector)
            dv(nc.vector.reciprocal(stat[:, 2, t0:t1], stat[:, 0, t0:t1]))
            for t in tiles:
                s = 0 if t < CTX_TILES else 1
                if sub == 0:
                    xn_ready.give(nc.vector.tensor_scalar(xn[:, t, :], R[:, t, :], stat[:, 2, t:t + 1], None, ALU.mult))
                else:
                    dv(nc.vector.scalar_tensor_tensor(out=htok[:, t, :], in0=R[:, t, :], scalar=stat[:, 2, t:t + 1],
                                                      in1=bc[:, 2, s, :], op0=ALU.mult, op1=ALU.mult))
                    xn_ready.give(nc.vector.tensor_tensor(htok[:, t, :], htok[:, t, :], bc[:, 1, s, :], ALU.add))

        def pe_turn(src, tiles, ready):
            for t in tiles:
                ready.take(nc.tensor)
                for half in range(2):
                    b = pa.open(nc.tensor)
                    for q in range(4):
                        kk = half * 4 + q
                        last = nc.tensor.transpose(b[:, q * P:(q + 1) * P], src[:, t, kk * P:(kk + 1) * P], ident)
                    pa.close(last)
            pa.drain(nc.tensor)

        def pe_lin(first, widths, lhs, tiles, pipe):
            for c, n in enumerate(widths):
                w = first + c
                nc.tensor.wait_ge(w_ld[w % 2], 16 * (w // 2 + 1))
                for t in tiles:
                    b = pipe.open(nc.tensor)
                    for kk in range(KD):
                        last = nc.tensor.matmul(b[:, 0:n], lhs[:, kk, t * P:(t + 1) * P], wbuf[:, w % 2, kk, 0:n],
                                                start=(kk == 0), stop=(kk == KD - 1))
                    pipe.close(last)
                used_chunk(w, pipe)

        def used_chunk(w, pipe):
            w_done[w] = (pipe.full, pipe.closed)

        w_done = {}
        def act_z():
            for c, n in enumerate((512, 512, 512, 416)):
                for t in range(NT):
                    b = pa.take(nc.scalar)
                    pa.release(nc.scalar.activation(z[:, t, c * 512:c * 512 + n], b[:, 0:n], ACT.Copy))
            mark["z"] = pa.left

        def act_sqrt(n):
            var_ready.take(nc.scalar)
            std_ready.give(nc.scalar.activation(stat[:, 0, 0:n], stat[:, 1, 0:n], ACT.Sqrt))

        def dve_rstd(dv, n):
            std_ready.take(nc.vector)
            dv(nc.vector.reciprocal(stat[:, 2, 0:n], stat[:, 0, 0:n]))

        def dve_rope(dv, v, groups, half, cos, sin, tmp):
            n = groups * half
            x1, x2 = v[:, :, 0:half], v[:, :, half:2 * half]
            c = cos.unsqueeze(1).to_broadcast([P, groups, half])
            s = sin.unsqueeze(1).to_broadcast([P, groups, half])
            t1, t2, t3 = (tmp[:, i * n:(i + 1) * n].rearrange("p (g c) -> p g c", g=groups) for i in range(3))
            dv(nc.vector.tensor_tensor(t1, x1, c, ALU.mult))
            dv(nc.vector.tensor_tensor(t2, x2, s, ALU.mult))
            dv(nc.vector.tensor_tensor(t3, x1, s, ALU.mult))
            dv(nc.vector.tensor_tensor(x1, t1, t2, ALU.subtract))
            dv(nc.vector.tensor_tensor(t1, x2, c, ALU.mult))
            return nc.vector.tensor_tensor(x2, t3, t1, ALU.add)

        def dve_lambda(dv):
            nc.vector.wait_ge(p_ld, 16 * N_PARAM)
            for i, (a, b) in enumerate((("lq1", "lk1"), ("lq2", "lk2"))):
                dv(nc.vector.tensor_tensor(tmpv[:, 0:64], sm(a), sm(b), ALU.mult))
                ins = nc.vector.tensor_reduce(lamt[:, 48 + i:49 + i], tmpv[:, 0:64], AX.X, ALU.add)
                dv(ins) if i == 0 else lam_in.give(ins)
            lam_ready.take(nc.vector)
            dv(nc.vector.tensor_tensor(lamt[:, 52:53], lamt[:, 51:52], lamt[:, 50:51], ALU.subtract))
            dv(nc.vector.tensor_scalar_add(lamt[:, 52:53], lamt[:, 52:53], -LAM_INIT))

        def act_lambda():
            lam_in.take(nc.scalar)
            lam_ready.give(nc.scalar.activation(lamt[:, 50:52], lamt[:, 48:50], ACT.Exp))

        def dve_heads(dv):
            dve_lambda(dv)
            nc.vector.wait_ge(pa.free, mark["z"])
            st = [stat[:, i, 0:72].rearrange("p (t c) -> p t c", t=NT) for i in range(3)]
            for t in range(NT):
                zq, zc = z[:, t, 0:1024], z[:, t, 1536:1920]
                dv(nc.vector.tensor_tensor(tmpv[:, 0:1024], zq, zq, ALU.mult))
                dv(nc.vector.tensor_reduce(st[0][:, t, 0:16], tmpv[:, 0:1024].rearrange("p (g c) -> p g c", g=16), AX.X, ALU.add))
                dv(nc.vector.tensor_tensor(tmpv[:, 0:384], zc, zc, ALU.mult))
                dv(nc.vector.tensor_reduce(st[0][:, t, 16:17], tmpv[:, 0:256], AX.X, ALU.add))
                dv(nc.vector.tensor_reduce(st[0][:, t, 17:18], tmpv[:, 256:384], AX.X, ALU.add))
            dv(nc.vector.tensor_scalar(st[1][:, :, 0:16], st[0][:, :, 0:16], 1.0 / 64, EPS, ALU.mult, ALU.add))
            dv(nc.vector.tensor_scalar(st[1][:, :, 16:17], st[0][:, :, 16:17], 1.0 / 256, EPS, ALU.mult, ALU.add))
            var_ready.give(nc.vector.tensor_scalar(st[1][:, :, 17:18], st[0][:, :, 17:18], 1.0 / 128, EPS, ALU.mult, ALU.add))
            dve_rstd(dv, 72)
            for t in range(NT):
                zq = z[:, t, 0:1024].rearrange("p (g c) -> p g c", g=16)
                dv(nc.vector.tensor_tensor(zq, zq, st[2][:, t, 0:16].unsqueeze(2).to_broadcast([P, 16, 64]), ALU.mult))
                for a, name in ((0, "qn"), (8, "kn")):
                    v = zq[:, a:a + 8, :]
                    dv(nc.vector.tensor_tensor(v, v, sm(name).unsqueeze(1).to_broadcast([P, 8, 64]), ALU.mult))
                if t >= CTX_TILES:
                    o = (t - CTX_TILES) * 32
                    dv(dve_rope(dv, zq, 16, 32, k("cosA")[:, o:o + 32], k("sinA")[:, o:o + 32], rope_t))
                for a, n, c, name in ((1536, 256, 16, "cqn"), (1792, 128, 17, "ckvn")):
                    v = z[:, t, a:a + n]
                    ins = nc.vector.scalar_tensor_tensor(out=v, in0=v, scalar=st[2][:, t, c:c + 1], in1=sm(name),
                                                         op0=ALU.mult, op1=ALU.mult)
                    dv(ins) if c == 16 else heads_ready.give(ins)
            nc.vector.wait_ge(pa.free, mark["mla"])
            for t in range(NT):
                dv(nc.vector.tensor_copy(qkb[:, t, 4:8, 0:64], kvb[:, t, :].rearrange("p (h c) -> p h c", h=MH)[:, :, 0:64]))
                dv(nc.vector.tensor_copy(qkb[:, t, 4:8, 64:96], z[:, t, 1920:1952].unsqueeze(1).to_broadcast([P, 4, 32])))
                v = qkb[:, t, :, :].rearrange("p g c -> p (g c)")
                dv(nc.vector.tensor_tensor(tmpv[:, 0:768], v, v, ALU.mult))
                dv(nc.vector.tensor_reduce(stat[:, 0, t * 8:t * 8 + 8], tmpv[:, 0:768].rearrange("p (g c) -> p g c", g=8), AX.X, ALU.add))
            var_ready.give(nc.vector.tensor_scalar(stat[:, 1, 0:32], stat[:, 0, 0:32], 1.0 / QK96, EPS, ALU.mult, ALU.add))
            dve_rstd(dv, 32)
            for t in range(NT):
                v = qkb[:, t, :, :]
                dv(nc.vector.tensor_tensor(v, v, stat[:, 2, t * 8:t * 8 + 8].unsqueeze(2).to_broadcast([P, 8, QK96]), ALU.mult))
                dv(nc.vector.tensor_tensor(v[:, 0:4], v[:, 0:4], sm("mqn").unsqueeze(1).to_broadcast([P, 4, QK96]), ALU.mult))
                ins = nc.vector.tensor_tensor(v[:, 4:8], v[:, 4:8], sm("mkn").unsqueeze(1).to_broadcast([P, 4, QK96]), ALU.mult)
                if t >= CTX_TILES:
                    dv(ins)
                    o = (t - CTX_TILES) * 16
                    ins = dve_rope(dv, v[:, :, 64:96], 8, 16, k("cosB")[:, o:o + 16], k("sinB")[:, o:o + 16], tmpv)
                heads_ready.give(ins)

        def pe_heads():
            for t in range(NT):
                heads_ready.take(nc.tensor)
                for base in (0, 512):
                    b = pa.open(nc.tensor)
                    for h in range(DH):
                        last = nc.tensor.transpose(b[:, h * P:(h + 1) * P], z[:, t, base + h * P:base + (h + 1) * P], ident)
                    pa.close(last)
                b = pa.open(nc.tensor)
                for q in range(3):
                    last = nc.tensor.transpose(b[:, q * P:(q + 1) * P], z[:, t, 1536 + q * P:1536 + (q + 1) * P], ident)
                pa.close(last)
            pa.drain(nc.tensor)
            nc.tensor.wait_ge(p_ld, 16 * N_PARAM)
            nc.tensor.wait_ge(mla_ld, 32)
            for t in range(NT):
                tt = slice(t * P, (t + 1) * P)
                b = pa.open(nc.tensor)
                nc.tensor.matmul(b[:, 0:384], cT3[:, 0, tt], wuq_sb[:, 0, :], start=True, stop=False)
                pa.close(nc.tensor.matmul(b[:, 0:384], cT3[:, 1, tt], wuq_sb[:, 1, :], start=False, stop=True))
                for half in range(2):
                    b = pa.open(nc.tensor)
                    pa.close(nc.tensor.matmul(b[:, 0:384], cT3[:, 2, tt], wukv_sb[:, half * 384:(half + 1) * 384],
                                              start=True, stop=True))
            for t in range(NT):
                heads_ready.take(nc.tensor)
                for base in (0, 4):
                    b = pa.open(nc.tensor)
                    for h in range(MH):
                        last = nc.tensor.transpose(b[0:QK96, h * P:(h + 1) * P], qkb[:, t, base + h, :], ident)
                    pa.close(last)
            pa.drain(nc.tensor)
            mark["heads"] = pa.closed

        def act_heads():
            act_lambda()
            act_sqrt(72)
            for t in range(NT):
                tt = slice(t * P, (t + 1) * P)
                for dst, n in ((qaT, 4), (kaT, 4), (cT3, 3)):
                    b = pa.take(nc.scalar)
                    pa.release(nc.scalar.activation(dst[:, 0:n, tt], b[:, 0:n * P].rearrange("p (h t) -> p h t", h=n), ACT.Copy))
            for t in range(NT):
                b = pa.take(nc.scalar)
                pa.release(nc.scalar.activation(qkb[:, t, 0:4, :], b[:, 0:384].rearrange("p (h c) -> p h c", h=4), ACT.Copy))
                for half in range(2):
                    b = pa.take(nc.scalar)
                    pa.release(nc.scalar.activation(kvb[:, t, half * 384:(half + 1) * 384], b[:, 0:384], ACT.Copy))
            mark["mla"] = pa.left
            act_sqrt(32)
            for t in range(NT):
                for dst in (qbT, kbT):
                    b = pa.take(nc.scalar)
                    pa.release(nc.scalar.activation(dst[0:QK96, :, t * P:(t + 1) * P],
                                                    b[0:QK96, :].rearrange("p (h t) -> p h t", h=MH), ACT.Copy))

        UNITS = [(t, m) for t in range(NT) for m in range(12)]

        def unit(u):
            t, m = UNITS[u]
            return t, m, (CTX_TILES if t < CTX_TILES else NT), (64 ** -0.5 if m < 8 else QK96 ** -0.5)

        def pe_attn():
            def scores(u):
                t, m, nk, _ = unit(u)
                b = ps.open(nc.tensor)
                if m < 8:
                    r = slice((m % 2) * 64, (m % 2) * 64 + 64)
                    q, kt = qaT[r, m // 2, t * P:(t + 1) * P], kaT[r, m // 2, 0:nk * P]
                else:
                    q, kt = qbT[0:QK96, m - 8, t * P:(t + 1) * P], kbT[0:QK96, m - 8, 0:nk * P]
                ps.close(nc.tensor.matmul(b[:, 0:nk * P], q, kt, start=True, stop=True))

            scores(0)
            for u in range(len(UNITS)):
                t, m, nk, _ = unit(u)
                if u + 1 < len(UNITS):
                    scores(u + 1)
                b = pv.open(nc.tensor)
                nc.tensor.wait_ge(ps.free, u + 1)
                for c in range(nk):
                    last = nc.tensor.transpose(b[:, c * P:(c + 1) * P], prob[:, u % 2, c * P:(c + 1) * P], ident)
                pv.close(last)
                b = po.open(nc.tensor)
                pv.drain(nc.tensor)
                for c in range(nk):
                    v = z[:, c, 1024 + (m // 2) * P:1024 + (m // 2 + 1) * P] if m < 8 else \
                        kvb[:, c, (m - 8) * 192 + 64:(m - 8) * 192 + 192]
                    last = nc.tensor.matmul(b[:, 0:P], probT[:, u % 2, c * P:(c + 1) * P], v, start=(c == 0), stop=(c == nk - 1))
                po.close(last)
                if u % 4 == 3:
                    pe_ada(1, u // 4)
            pa.drain(nc.tensor)

        def act_attn():
            act_ada()
            for u in range(len(UNITS)):
                _, _, nk, scale = unit(u)
                nmax_ready.take(nc.scalar)
                ps.release(nc.scalar.activation(prob[:, u % 2, 0:nk * P], ps.banks[u % 2][:, 0:nk * P], ACT.Exp,
                                                bias=negs[:, 2 + u % 2:3 + u % 2], scale=scale, accum_out=rsum[:, u:u + 1]))

        def dve_attn(dv):
            def nmax(u):
                _, _, nk, scale = unit(u)
                b = ps.take(nc.vector)
                dv(nc.vector.tensor_reduce(negs[:, u % 2:u % 2 + 1], b[:, 0:nk * P], AX.X, ALU.max))
                nmax_ready.give(nc.vector.tensor_scalar(negs[:, 2 + u % 2:3 + u % 2], negs[:, u % 2:u % 2 + 1],
                                                        -scale, None, ALU.mult))

            nmax(0)
            for u in range(len(UNITS)):
                t, m, nk, _ = unit(u)
                if u + 1 < len(UNITS):
                    nmax(u + 1)
                b = pv.take(nc.vector)
                pv.release(nc.vector.tensor_copy(probT[:, u % 2, 0:nk * P], b[:, 0:nk * P]))
                dv(nc.vector.reciprocal(negs[:, 4 + u % 2:5 + u % 2], rsum[:, u:u + 1]))
                b = po.take(nc.vector)
                nc.vector.wait_ge(po.free, po.left)
                if m < 8:
                    dst = o_tok[:, t, (m // 2) * P:(m // 2 + 1) * P]
                else:
                    dst = o_tok[:, t, (m - 4) * P:(m - 3) * P]
                if m < 8 and m % 2:
                    dv(nc.vector.tensor_tensor(negs[:, 4 + u % 2:5 + u % 2], negs[:, 4 + u % 2:5 + u % 2], lamt[:, 52:53], ALU.mult))
                    po.release(nc.vector.scalar_tensor_tensor(out=dst, in0=b[:, 0:P], scalar=negs[:, 4 + u % 2:5 + u % 2], in1=dst,
                                                              op0=ALU.mult, op1=ALU.add))
                else:
                    po.release(nc.vector.tensor_scalar(dst, b[:, 0:P], negs[:, 4 + u % 2:5 + u % 2], None, ALU.mult))
                if u % 4 == 3:
                    dve_ada(1, u // 4)
            nc.vector.wait_ge(po.free, po.left)
            for t in range(NT):
                v = o_tok[:, t, 0:512]
                dv(nc.vector.tensor_tensor(tmpv[:, 0:512], v, v, ALU.mult))
                dv(nc.vector.tensor_reduce(stat[:, 0, t * 4:t * 4 + 4], tmpv[:, 0:512].rearrange("p (g c) -> p g c", g=4), AX.X, ALU.add))
            var_ready.give(nc.vector.tensor_scalar(stat[:, 1, 0:16], stat[:, 0, 0:16], 1.0 / P, EPS, ALU.mult, ALU.add))
            dve_rstd(dv, 16)
            for t in range(NT):
                v = o_tok[:, t, 0:512].rearrange("p (g c) -> p g c", g=4)
                dv(nc.vector.tensor_tensor(v, v, stat[:, 2, t * 4:t * 4 + 4].unsqueeze(2).to_broadcast([P, 4, P]), ALU.mult))
                o_ready.give(nc.vector.scalar_tensor_tensor(out=v, in0=v, scalar=1.0 - LAM_INIT,
                                                            in1=sm("subln").unsqueeze(1).to_broadcast([P, 4, P]),
                                                            op0=ALU.mult, op1=ALU.mult))

        def act_turn(dst, tiles):
            for t in tiles:
                for half in range(2):
                    b = pa.take(nc.scalar)
                    pa.release(nc.scalar.activation(dst[:, half * 4:half * 4 + 4, t * P:(t + 1) * P],
                                                    b[:, :].rearrange("p (q t) -> p q t", q=4), ACT.Copy))

        def dve_residual(dv, l, tiles, tmp):
            n = 0
            nc.vector.wait_ge(bc_ld, 16 * BC_COUNT[l, 0])
            for c in range(2):
                for t in tiles:
                    n += 1
                    s = 0 if t < CTX_TILES else 1
                    b = pv.take(nc.vector)
                    cc = slice(c * 512, (c + 1) * 512)
                    pv.release(nc.vector.tensor_tensor(tmp, b[:, :], bc[:, 0, s, cc], ALU.mult))
                    nc.vector.wait_ge(pv.free, pv.left)
                    ins = nc.vector.tensor_tensor(R[:, t, cc], R[:, t, cc], tmp, ALU.add)
                    r_ready.give(ins) if n == 2 * len(tiles) else dv(ins)
            nc.vector.wait_ge(r_ready.sem, r_ready.made)
            if l == 1:
                vec_free.give(nc.vector.tensor_copy(negs[:, 0:1], ident[:, 0:1]))

        qT4 = qT.rearrange("p (t h) c -> p t h c", h=HEADS)
        qTf = qT.rearrange("p s c -> p (s c)")
        htf = htok.rearrange("p t d -> p (t d)")
        Yf = Y.rearrange("p t d -> p (t d)")

        def pe_query(l):
            tiles = peer_tiles(l)
            a, n = tiles[0] * P, len(tiles) * P
            for c in range(4):
                w = (W_WQ0 if l == 0 else W_WQ1) + c
                nc.tensor.wait_ge(w_ld[w % 2], 16 * (w // 2 + 1))
                for cb in range(4):
                    b = pa.open(nc.tensor)
                    for kk in range(KD):
                        last = nc.tensor.matmul(b[:, 0:n], wbuf[:, w % 2, kk, cb * P:(cb + 1) * P], hT[:, kk, a:a + n],
                                                start=(kk == 0), stop=(kk == KD - 1))
                    pa.close(last)
                used_chunk(w, pa)
            mark[f"q{l}"] = pa.closed
            pa.drain(nc.tensor)

        def act_query(l):
            nt = len(peer_tiles(l))
            for c in range(4):
                for cb in range(4):
                    b = pa.take(nc.scalar)
                    pa.release(nc.scalar.activation(qT4[:, 0:nt, 2 * c + cb // 2, (cb % 2) * P:(cb % 2 + 1) * P],
                                                    b[:, 0:nt * P].rearrange("p (t c) -> p t c", t=nt), ACT.Copy))
            nc.scalar.wait_ge(pa.free, pa.left)

        def steps(eng, l, body, chain=None):
            n = len(peer_tiles(l)) * HEADS
            base = 0 if l == 0 else NT * HEADS
            start = chain.n if chain else 0
            for p in range(2):
                body(p, base + p, p, 0, True, n)
            per = chain.n - start if chain else 0
            start += per
            with eng.Fori(1, n // 2 - 1) as i:
                if chain:
                    chain.base, chain.n = (i - 1) * per + start, 0
                for p in range(2):
                    body(i * 2 + p, i * 2 + (base + p), p, i, False, n)
                if chain:
                    assert chain.n == per, (chain.n, per)
            if chain:
                chain.base, chain.n = 0, start + per * (n // 2 - 2)
            for p in range(2):
                body(n - 2 + p, base + n - 2 + p, p, None, False, n)

        def tab(l, which):
            return ((peer_u0, peer_v0), (peer_u1, peer_v1))[l][which]

        def pool_peer(l):
            def body(s, gs, par, i, first, n):
                dyn = not isinstance(s, int)

                def hold(sm_, v):
                    if isinstance(v, int) and v <= 0:
                        return
                    nc.gpsimd.wait_ge(sm_, v)
                    if dyn:
                        nc.gpsimd.sem_inc(pool_sem, 1)

                hold(idx_ready, gs + 1)
                for which, ring, land, read in ((0, uring, u_land, u_read), (1, vring, v_land, v_read)):
                    for kk in range(TOPK):
                        hold(read, gs * 16 + (kk - RING + 1))
                        nc.gpsimd.indirect_dma_start(
                            ring[:, kk % RING, :], None, tab(l, which),
                            bass.IndirectOffsetOnAxis(idx[:, par, kk:kk + 1], 0)).then_inc(land[kk % RING], 16)
            steps(nc.gpsimd, l, body)

        def dve_route(dv, s, gs, par):
            b = scbank[par]
            nc.vector.wait_ge(sc_done, gs + 1)
            for half in range(2):
                src = b[:, half * NK:(half + 1) * NK]
                o = half * TOPK
                dv.alone(vec_mark)
                dv(nc.vector.max(v16[:, o:o + 8], src))
                dv.alone(vec_mark)
                dv(nc.vector.max_index(i16[:, o:o + 8], v16[:, o:o + 8], src))
                dv.alone(vec_mark)
                dv(nc.vector.match_replace(sw[:, 0:NK], v16[:, o:o + 8], src, NEG))
                dv.alone(vec_mark)
                dv(nc.vector.max(v16[:, o + 8:o + 16], sw[:, 0:NK]))
                dv.alone(vec_mark)
                dv(nc.vector.max_index(i16[:, o + 8:o + 16], v16[:, o + 8:o + 16], sw[:, 0:NK]))
            c2 = cand.rearrange("p (a b) -> p a b", a=TOPK)
            dv(nc.vector.tensor_tensor(c2, v16[:, 0:16].unsqueeze(2).to_broadcast([P, TOPK, TOPK]),
                                       v16[:, 16:32].unsqueeze(1).to_broadcast([P, TOPK, TOPK]), ALU.add))
            dv.alone(vec_mark)
            dv(nc.vector.max(sc16[:, par, 0:8], cand))
            dv.alone(vec_mark)
            dv(nc.vector.max_index(j16[:, 0:8], sc16[:, par, 0:8], cand))
            dv.alone(vec_mark)
            dv(nc.vector.match_replace(candw, sc16[:, par, 0:8], cand, NEG))
            dv.alone(vec_mark)
            dv(nc.vector.max(sc16[:, par, 8:16], candw))
            dv.alone(vec_mark)
            dv(nc.vector.max_index(j16[:, 8:16], sc16[:, par, 8:16], candw))
            nc.vector.tensor_scalar(nb[:, par:par + 1], sc16[:, par, 0:1], -1.0, None, ALU.mult).then_inc(top_ready, 1)
            dv(nc.vector.tensor_scalar(ab16[:, 0:16], j16, 4, None, ALU.logical_shift_right))
            dv(nc.vector.tensor_scalar(ab16[:, 16:32], j16, 15, None, ALU.bitwise_and))
            oh = onehot.rearrange("p (k i) -> p k i", k=32)
            dv(nc.vector.tensor_tensor(oh, ab16.unsqueeze(2).to_broadcast([P, 32, TOPK]),
                                       k("iota").unsqueeze(1).to_broadcast([P, 32, TOPK]), ALU.is_equal))
            for half in range(2):
                o = half * TOPK
                dv(nc.vector.tensor_tensor(oh[:, o:o + 16, :], oh[:, o:o + 16, :],
                                           i16[:, o:o + 16].unsqueeze(1).to_broadcast([P, TOPK, TOPK]), ALU.mult))
            dv(nc.vector.tensor_reduce(sel, oh, AX.X, ALU.add))
            nc.vector.scalar_tensor_tensor(out=idx[:, par, :], in0=sel[:, 0:16], scalar=float(NK), in1=sel[:, 16:32],
                                           op0=ALU.mult, op1=ALU.add).then_inc(idx_ready, 1)

        def tile_of(s, par, i, t0, back=0):
            if isinstance(s, int):
                return t0 + (s - back) // HEADS
            return (i - 1) // 4 + t0 if (back and par == 0) else i // 4 + t0

        def dve_peer(dv, l):
            t0 = peer_tiles(l)[0]

            def yacc(s, gs, par, t):
                nc.vector.wait_ge(v_read, gs * 16 + 16)
                nc.vector.wait_ge(y_free, gs * 2) if not (isinstance(gs, int) and gs == 0) else None
                for half in range(2):
                    dst = Yf[:, bass.ds(t * D + half * 512, 512)]
                    nc.vector.tensor_tensor(dst, dst, ybank[par][half][:, :], ALU.add).then_inc(y_free, 1)

            def body(s, gs, par, i, first, n):
                t = tile_of(s, par, i, t0)
                for kk in range(TOPK):
                    nc.vector.wait_ge(u_land[kk % RING], gs * 32 + 16 * (kk // RING + 1))
                    nc.vector.scalar_tensor_tensor(out=uring[:, kk % RING, :], in0=uring[:, kk % RING, :], scalar=1.0,
                                                   in1=htf[:, bass.ds(t * D, D)], op0=ALU.mult, op1=ALU.mult,
                                                   accum_out=act16[:, par, kk:kk + 1]).then_inc(u_read, 1)
                nc.vector.wait_ge(exp_done, gs + 1)
                dv(nc.vector.reciprocal(zs[:, 2 + par:3 + par], zs[:, par:par + 1]))
                nc.vector.wait_ge(gelu_done, gs + 1)
                nc.vector.scalar_tensor_tensor(out=w16[:, par, :], in0=gel16[:, par, :], scalar=zs[:, 2 + par:3 + par],
                                               in1=e16[:, par, :], op0=ALU.mult, op1=ALU.mult).then_inc(w_ready, 1)
                if not (first and par == 0):
                    yacc(None, gs - 1, 1 - par, tile_of(s, par, i, t0, 1))
                if not (isinstance(s, int) and s == n - 1):
                    dve_route(dv, s, gs + 1, 1 - par)
                if isinstance(s, int) and s == n - 1:
                    yacc(None, gs, par, tile_of(s, par, i, t0))

            base = 0 if l == 0 else NT * HEADS
            nc.vector.wait_ge(pa.full, mark[f"q{l}"])
            dv(nc.vector.memset(Yf, 0.0))
            dve_route(dv, 0, base, 0)
            steps(nc.vector, l, body, dv)
            end = base + len(peer_tiles(l)) * HEADS
            nc.vector.wait_ge(y_free, 2 * end)
            for t in peer_tiles(l):
                s = 0 if t < CTX_TILES else 1
                dv(nc.vector.tensor_tensor(Y[:, t, :], Y[:, t, :], bc[:, 3, s, :], ALU.mult))
                ins = nc.vector.tensor_tensor(R[:, t, :], R[:, t, :], Y[:, t, :], ALU.add)
                dv(ins) if t < NT - 1 else r_ready.give(ins)
            nc.vector.wait_ge(r_ready.sem, r_ready.made)

        def act_peer(l):
            base = 0 if l == 0 else NT * HEADS

            def stage(s, gs, par):
                if not (isinstance(gs, int) and gs < 2):
                    nc.scalar.wait_ge(sc_done, gs - 1)
                nc.scalar.activation(qst[:, par, :], qTf[:, bass.ds(s * 256, 256)], ACT.Copy).then_inc(q_staged, 1)

            def softmax(gs, par):
                nc.scalar.wait_ge(top_ready, gs + 1)
                nc.scalar.activation(e16[:, par, :], sc16[:, par, :], ACT.Exp, bias=nb[:, par:par + 1],
                                     accum_out=zs[:, par:par + 1]).then_inc(exp_done, 1)

            def body(s, gs, par, i, first, n):
                last = isinstance(s, int) and s == n - 1
                if not last:
                    stage(s + 1, gs + 1, 1 - par)
                nc.scalar.wait_ge(u_read, gs * 16 + 16)
                nc.scalar.activation(gel16[:, par, :], act16[:, par, :], ACT.Gelu).then_inc(gelu_done, 1)
                nc.scalar.wait_ge(w_ready, gs + 1)
                for kk in range(TOPK):
                    if not (isinstance(gs, int) and gs * 16 + kk < 4):
                        nc.scalar.wait_ge(v_read, gs * 16 + (kk - 3))
                    nc.scalar.activation(diag[:, kk % 4, :], ident, ACT.Copy, scale=w16[:, par, kk:kk + 1]).then_inc(diag_done, 1)
                if not last:
                    softmax(gs + 1, 1 - par)

            stage(0, base, 0)
            softmax(base, 0)
            steps(nc.scalar, l, body)

        def pe_peer(l):
            base = 0 if l == 0 else NT * HEADS

            def keyscores(gs, par):
                nc.tensor.wait_ge(q_staged, gs + 1)
                if not (isinstance(gs, int) and gs < 2):
                    nc.tensor.wait_ge(idx_ready, gs - 1)
                nc.tensor.matmul(scbank[par][:, 0:NK], qst[:, par, 0:P], keys[:, l, 0, :], start=True, stop=True)
                nc.tensor.matmul(scbank[par][:, NK:2 * NK], qst[:, par, P:2 * P], keys[:, l, 1, :],
                                 start=True, stop=True).then_inc(sc_done, 1)

            def body(s, gs, par, i, first, n):
                if not (isinstance(s, int) and s == n - 1):
                    keyscores(gs + 1, 1 - par)
                if not (isinstance(gs, int) and gs < 2):
                    nc.tensor.wait_ge(y_free, gs * 2 - 2)
                for kk in range(TOPK):
                    nc.tensor.wait_ge(v_land[kk % RING], gs * 32 + 16 * (kk // RING + 1))
                    nc.tensor.wait_ge(diag_done, gs * 16 + (kk + 1))
                    for half in range(2):
                        ins = nc.tensor.matmul(ybank[par][half][:, :], diag[:, kk % 4, :],
                                               vring[:, kk % RING, half * 512:(half + 1) * 512],
                                               start=(kk == 0), stop=(kk == TOPK - 1))
                    ins.then_inc(v_read, 1)

            keyscores(base, 0)
            steps(nc.tensor, l, body)
            nc.tensor.wait_ge(y_free, 2 * (base + len(peer_tiles(l)) * HEADS))
        NG, CH, CONV, XW = 4, 64, 5, 256
        g = Region(scr)
        ktok = g.get(NT * D).rearrange("p (t d) -> p t d", t=NT)
        vtok = g.get(NT * D).rearrange("p (t d) -> p t d", t=NT)
        qtok = g.get(2 * D).rearrange("p (t d) -> p t d", t=2)
        zgs = g.get(2 * D).rearrange("p (t d) -> p t d", t=2)
        kTg = g.get(2 * TOK).rearrange("p (h t) -> p h t", h=2)
        qTg = g.get(2 * XW).rearrange("p (h t) -> p h t", h=2)
        vns = g.get(512).rearrange("p (u c) -> p u c", u=4)
        g2, g3 = Region(htok.rearrange("p t d -> p (t d)")), Region(wbuf[:, 0].rearrange("p k c -> p (k c)"))
        ug, wTg, ATg, qdTg = [], [], [], []
        for r1, r2, r3 in ((g, g, g2), (g2, g3, g3)):
            ug.append(r1.get(NT * 512).rearrange("p (t u c) -> p t u c", t=NT, u=4))
            wTg.append(r2.get(NT * 512).rearrange("p (t u c) -> p t u c", t=NT, u=4))
            ATg.append(r3.get(2 * 512).rearrange("p (t u c) -> p t u c", t=2, u=4))
            qdTg.append(r3.get(2 * 512).rearrange("p (t u c) -> p t u c", t=2, u=4))
        g = Region(bcx)
        cpad = g.get(2 * 2 * (XW + CONV - 1)).rearrange("p (r s c) -> p r s c", r=2, s=2)
        cout = g.get(2 * TOK).rearrange("p (r c) -> p r c", r=2)
        csil = g.get(2 * TOK).rearrange("p (r c) -> p r c", r=2)
        g = Region(bcx)
        Xm, XTm, LTm, Pm = (g.get(1024).rearrange("p (r u c) -> p r u c", r=2, u=4) for _ in range(4))
        g = Region(hT.rearrange("p k t -> p (k t)"))
        S = g.get(512).rearrange("p (u c) -> p u c", u=4)
        vn = g.get(512).rearrange("p (u c) -> p u c", u=4)
        dec, CTm = (g.get(1024).rearrange("p (r u c) -> p r u c", r=2, u=4) for _ in range(2))
        dgc = g.get(1024).rearrange("p (r u c) -> p r u c", r=2, u=4)
        g = Region(wbuf[:, 1].rearrange("p k c -> p (k c)"))
        vbm, kbm, Lm, qem = (g.get(1024).rearrange("p (r u c) -> p r u c", r=2, u=4) for _ in range(4))
        Am = CTm
        sqb = wTg[0].rearrange("p t u c -> p (t u c)")
        g = Region(bc[:, 0, 0, :])
        abt = g.get(128).rearrange("p (t c) -> p t c", t=NT)
        ga, gm, gn, gg, beta, eg, ed, bek = (g.get(64) for _ in range(8))
        gct = g.get(256)
        g = Region(bc[:, 3, 0, :])
        glb = g.get(128)
        ealog = g.get(16)

        pad_ready = Signal(sem("conv_padding_ready"))
        conv_ready, csil_ready = Signal(sem("conv_ready")), Signal(sem("conv_silu_ready"))
        gate_in, gate_out = Signal(sem("gate_in")), Signal(sem("gate_exp"))
        g_ready = Signal(sem("log_decay_ready"))
        norm_ready = Signal(sem("qk_normed"))
        operand_ready = Signal(sem("dn_operand_ready"))
        dec_in, dec_exp = Signal(sem("decay_in")), Signal(sem("decay_exp"))
        vn_ready = Signal(sem("vnew_ready"))
        DT = [(0, 1), (2, 3)]

        def dth(v):
            return v.rearrange("p (d t h) -> p d t h", d=2, t=NT)

        def unit_scalars(v, gp, t):
            s = dth(v)[:, :, t, 2 * gp:2 * gp + 2].rearrange("p d h -> p h d")
            return s.unsqueeze(3).to_broadcast([P, 2, 2, P])

        def u4(v):
            return v.rearrange("p (h d) c -> p h d c", h=2)

        def over_dirs(v):
            return v.unsqueeze(2).to_broadcast([P, 2, 2, P])

        def over_heads(v):
            return v.unsqueeze(1).to_broadcast([P, 2, 2, P])

        incl = k("incl").rearrange("p (d c) -> p d c", d=2)
        strict = k("strict").rearrange("p (d c) -> p d c", d=2)
        lvl = k("lvl").rearrange("p (l d c) -> p l d c", l=len(LEVELS), d=3)
        identu = ident.unsqueeze(1).to_broadcast([P, 4, P])

        def pe_dn_project():
            def turn(i):
                csil_ready.take(nc.tensor)
                b = pa.open(nc.tensor)
                for t in (XT if i < 8 else AT):
                    last = nc.tensor.transpose(b[:, t * P:(t + 1) * P], csil[:, i % 2, t * P:(t + 1) * P], ident)
                pa.close(last)

            for i in range(26):
                if i < 24:
                    w, cb = W_DNIN + i // 4, i % 4
                    if cb == 0:
                        nc.tensor.wait_ge(w_ld[w % 2], 16 * (w // 2 + 1))
                    a = XW if i < 8 else 0
                    b = pa.open(nc.tensor)
                    for kk in range(KD):
                        last = nc.tensor.matmul(b[:, a:TOK], wbuf[:, w % 2, kk, cb * P:(cb + 1) * P], hT[:, kk, a:TOK],
                                                start=(kk == 0), stop=(kk == KD - 1))
                    pa.close(last)
                    if cb == 3:
                        used_chunk(w, pa)
                if i >= 2:
                    turn(i - 2)
            b = pa.open(nc.tensor)
            for t in AT:
                for kk in range(KD):
                    last = nc.tensor.matmul(b[:, t * 32:(t + 1) * 32], hT[:, kk, t * P:(t + 1) * P], wab[:, kk, :],
                                            start=(kk == 0), stop=(kk == KD - 1))
            pa.close(last)
            pe_lin(W_DNIN + 6, (512, 512), hT, XT, pa)
            mark["dn_hT"] = pa.closed
            g_ready.take(nc.tensor)
            b = pv.open(nc.tensor)
            gd = dth(gg).rearrange("p d t h -> p d (t h)")
            for d, m in ((0, k("incl")[:, P:2 * P]), (1, k("incl")[:, 0:P])):
                nc.tensor.matmul(b[:, d * 32:(d + 1) * 32], m, gd[:, d], start=True, stop=True)
                nc.tensor.matmul(b[:, 64 + d * 32:96 + d * 32], k("blk"), gd[:, d], start=True, stop=True)
            for c in range(2):
                rows_c = k("blk")[:, c * CH:c * CH + 1].to_broadcast([P, P])
                for d in range(2):
                    o = 128 + c * 64 + d * 32
                    last = nc.tensor.matmul(b[:, o:o + 32], rows_c, gd[:, d], start=True, stop=True)
            pv.close(last)

        def act_dn_project(ac):
            def silu(i):
                conv_ready.take(nc.scalar)
                a = XW if i < 8 else 0
                csil_ready.give(nc.scalar.activation(csil[:, i % 2, a:TOK], cout[:, i % 2, a:TOK], ACT.Silu))

            def turned(i):
                b = pa.take(nc.scalar)
                o = (i % 8) * P
                dst, a, n = ((qtok, XW, 2), (ktok, 0, NT), (vtok, 0, NT))[i // 8]
                pa.release(nc.scalar.activation(dst[:, 0:n, o:o + P], b[:, a:TOK].rearrange("p (t c) -> p t c", t=n), ACT.Copy))

            pad_ready.take(nc.scalar)
            for i in range(26):
                if i < 24:
                    b = pa.take(nc.scalar)
                    s = 1 if i < 8 else 0
                    pa.release(nc.scalar.activation(cpad[:, i % 2, s:2, 2:2 + XW],
                                                    b[:, s * XW:TOK].rearrange("p (s c) -> p s c", s=2 - s), ACT.Copy))
                    mark["cv", i] = pa.left
                if 1 <= i < 25:
                    silu(i - 1)
                if i >= 2:
                    turned(i - 2)
            b = pa.take(nc.scalar)
            pa.release(nc.scalar.activation(abt, b[:, 0:128].rearrange("p (t c) -> p t c", t=NT), ACT.Copy))
            mark["ab"] = pa.left
            for c in range(2):
                for t in range(2):
                    b = pa.take(nc.scalar)
                    pa.release(nc.scalar.activation(zgs[:, t, c * 512:(c + 1) * 512], b[:, :], ACT.Silu))
            mark["zg"] = pa.left
            gate_in.take(nc.scalar)
            ac(nc.scalar.activation(gn, gn, ACT.Exp))
            ac(nc.scalar.activation(beta, beta, ACT.Exp))
            gate_out.give(nc.scalar.activation(ealog, sm("alog"), ACT.Exp))
            gate_in.take(nc.scalar)
            gate_out.give(nc.scalar.activation(gn, gn, ACT.Ln))
            gate_in.take(nc.scalar)
            ac(nc.scalar.activation(eg, gct[:, 0:64], ACT.Exp))
            ac(nc.scalar.activation(ed, ed, ACT.Exp))
            gate_out.give(nc.scalar.activation(glb, gct[:, 128:256], ACT.Exp))
            act_sqrt(48)

        def dve_dn_project(dv):
            pad_ready.give(nc.vector.memset(cpad, 0.0))
            for i in range(24):
                nc.vector.wait_ge(pa.free, mark["cv", i])
                s = 1 if i < 8 else 0
                o = cout[:, i % 2, s * XW:TOK].rearrange("p (s c) -> p s c", s=2 - s)
                for j in range(CONV):
                    v = cpad[:, i % 2, s:2, j:j + XW]
                    if j == 0:
                        dv(nc.vector.tensor_scalar(o, v, convw[:, i, 0:1], None, ALU.mult))
                    else:
                        ins = nc.vector.scalar_tensor_tensor(out=o, in0=v, scalar=convw[:, i, j:j + 1], in1=o,
                                                             op0=ALU.mult, op1=ALU.add)
                        conv_ready.give(ins) if j == CONV - 1 else dv(ins)
            nc.vector.wait_ge(pa.free, mark["ab"])
            a_in = abt[:, :, 0:16].rearrange("p t (d h) -> p t d h", d=2)
            b_in = abt[:, :, 16:32].rearrange("p t (d h) -> p t d h", d=2)
            tdh = lambda v: dth(v).rearrange("p d t h -> p t d h")
            dtb = sm("dtb").rearrange("p (d h) -> p d h", d=2).unsqueeze(1).to_broadcast([P, NT, 2, 8])
            dv(nc.vector.tensor_tensor(tdh(ga), a_in, dtb, ALU.add))
            dv(nc.vector.tensor_scalar(gn, ga, -1.0, None, ALU.mult))
            dv(nc.vector.tensor_tensor(gn, gn, ga, ALU.min))
            dv(nc.vector.tensor_scalar(gm, ga, 0.0, None, ALU.max))
            gate_in.give(nc.vector.tensor_scalar(tdh(beta), b_in, -1.0, None, ALU.mult))
            gate_out.take(nc.vector)
            dv(nc.vector.tensor_scalar_add(beta, beta, 1.0))
            dv(nc.vector.reciprocal(beta, beta))
            gate_in.give(nc.vector.tensor_scalar_add(gn, gn, 1.0))
            gate_out.take(nc.vector)
            dv(nc.vector.tensor_tensor(gm, gm, gn, ALU.add))
            ea = ealog.rearrange("p (d h) -> p d h", d=2).unsqueeze(2).to_broadcast([P, 2, NT, 8])
            g_ready.give(nc.vector.tensor_tensor(dth(gg), dth(gm), ea, ALU.mult))
            b = pv.take(nc.vector)
            pv.release(nc.vector.tensor_scalar(gct, b[:, 0:256], -1.0, None, ALU.mult))
            nc.vector.wait_ge(pv.free, pv.left)
            gate_in.give(nc.vector.tensor_tensor(ed, gct[:, 64:128], gct[:, 0:64], ALU.subtract))
            gate_out.take(nc.vector)
            dv(nc.vector.tensor_tensor(bek, beta, eg, ALU.mult))
            nc.vector.wait_ge(pa.free, mark["zg"])
            rows = [(ktok, t) for t in range(NT)] + [(qtok, t) for t in range(2)]
            for n, (v, t) in enumerate(rows):
                dv(nc.vector.tensor_tensor(sqb[:, 0:D], v[:, t, :], v[:, t, :], ALU.mult))
                dv(nc.vector.tensor_reduce(stat[:, 0, n * 8:n * 8 + 8], sqb[:, 0:D].rearrange("p (h c) -> p h c", h=8), AX.X, ALU.add))
            var_ready.give(nc.vector.tensor_scalar(stat[:, 1, 0:48], stat[:, 0, 0:48], EPS, None, ALU.add))
            dve_rstd(dv, 48)
            dv(nc.vector.tensor_scalar(stat[:, 2, 32:48], stat[:, 2, 32:48], float(P) ** -0.5, None, ALU.mult))
            for n, (v, t) in enumerate(rows):
                w = v[:, t, :].rearrange("p (h c) -> p h c", h=8)
                ins = nc.vector.tensor_tensor(w, w, stat[:, 2, n * 8:n * 8 + 8].unsqueeze(2).to_broadcast([P, 8, P]), ALU.mult)
                norm_ready.give(ins) if n == len(rows) - 1 else dv(ins)
            nc.vector.wait_ge(norm_ready.sem, norm_ready.made)
            nc.vector.wait_ge(pa.full, mark["dn_hT"])

        def pe_dn_inverse(gp):
            for hh in range(2):
                b = pa.open(nc.tensor)
                for t in AT:
                    o = (2 * gp + hh) * P
                    last = nc.tensor.transpose(b[:, t * P:(t + 1) * P], ktok[:, t, o:o + P], ident)
                pa.close(last)
            b = pa.open(nc.tensor)
            for hh in range(2):
                for t in range(2):
                    o = (2 * gp + hh) * P
                    last = nc.tensor.transpose(b[:, (hh * 2 + t) * P:(hh * 2 + t + 1) * P], qtok[:, t, o:o + P], ident)
            pa.close(last)
            pa.drain(nc.tensor)
            for pair in DT:
                x_pair = pair[0] >= CTX_TILES
                for r, t in enumerate(pair):
                    tt = slice(t * P, (t + 1) * P)
                    b = pv.open(nc.tensor)
                    operand_ready.take(nc.tensor)
                    pv.close(nc.tensor.matmul(b[:, :], ones, dgc[:, r].rearrange("p u c -> p (u c)"), start=True, stop=True))
                    b = ps.open(nc.tensor)
                    for hh in range(2):
                        last = nc.tensor.matmul(b[:, hh * P:(hh + 1) * P], kTg[:, hh, tt], kTg[:, hh, tt], start=True, stop=True)
                        if x_pair:
                            a = (t - CTX_TILES) * P
                            last = nc.tensor.matmul(b[:, 256 + hh * P:256 + (hh + 1) * P], qTg[:, hh, a:a + P], kTg[:, hh, tt],
                                                    start=True, stop=True)
                    ps.close(last)
                yield
                for r, t in enumerate(pair):
                    b = pa.open(nc.tensor)
                    operand_ready.take(nc.tensor)
                    for u in range(4):
                        last = nc.tensor.transpose(b[:, u * P:(u + 1) * P], Lm[:, r, u, :], ident)
                    pa.close(last)
                    if x_pair:
                        b = pa.open(nc.tensor)
                        for u in range(4):
                            last = nc.tensor.transpose(b[:, u * P:(u + 1) * P], Am[:, r, u, :], ident)
                        pa.close(last)
                yield
                for li in range(1, len(LEVELS)):
                    for r, t in enumerate(pair):
                        b = pa.open(nc.tensor)
                        operand_ready.take(nc.tensor)
                        for u in range(4):
                            last = nc.tensor.matmul(b[:, u * P:(u + 1) * P], CTm[:, r, u, :], Xm[:, r, u, :], start=True, stop=True)
                        pa.close(last)
                        level_job[r] = pa.opened
                    for r, t in enumerate(pair):
                        nc.tensor.wait_ge(pa.free, level_job[r])
                        if li < len(LEVELS) - 1:
                            b = ps.open(nc.tensor)
                            for u in range(4):
                                last = nc.tensor.matmul(b[:, u * P:(u + 1) * P], XTm[:, r, u, :], Pm[:, r, u, :], start=True, stop=True)
                            ps.close(last)
                        b = pv.open(nc.tensor)
                        for u in range(4):
                            last = nc.tensor.matmul(b[:, u * P:(u + 1) * P], Pm[:, r, u, :], XTm[:, r, u, :], start=True, stop=True)
                        pv.close(last)
                    yield
                for r, t in enumerate(pair):
                    b = pa.open(nc.tensor)
                    operand_ready.take(nc.tensor)
                    for u in range(4):
                        last = nc.tensor.matmul(b[:, u * P:(u + 1) * P], XTm[:, r, u, :], vbm[:, r, u, :], start=True, stop=True)
                    pa.close(last)
                    b = pa.open(nc.tensor)
                    for u in range(4):
                        last = nc.tensor.matmul(b[:, u * P:(u + 1) * P], kbm[:, r, u, :], XTm[:, r, u, :], start=True, stop=True)
                    pa.close(last)
                    if x_pair:
                        b = pa.open(nc.tensor)
                        for u in range(4):
                            last = nc.tensor.transpose(b[:, u * P:(u + 1) * P], qem[:, r, u, :], ident)
                        pa.close(last)
                mark["rhs", gp] = pa.opened
                yield

        def pe_dn_scan(gp):
            s2 = gp % 2
            nc.tensor.wait_ge(pa.free, mark["rhs", gp])
            for n in range(8):
                b = pv.open(nc.tensor)
                if n == 0:
                    operand_ready.take(nc.tensor)
                else:
                    nc.tensor.wait_ge(ps.free, state_job)
                for u in range(4):
                    t, c = chunk_of(n, u % 2)
                    r = slice(c * CH, (c + 1) * CH)
                    last = nc.tensor.matmul(b[r, u * P:(u + 1) * P], wTg[s2][:, t, u, r], S[:, u, :], start=True, stop=True)
                pv.close(last)
                yield
                if n >= 4:
                    b = po.open(nc.tensor)
                    vn_ready.take(nc.tensor)
                    for u in range(4):
                        t, c = chunk_of(n, u % 2)
                        r = slice(c * CH, (c + 1) * CH)
                        nc.tensor.matmul(b[r, u * P:(u + 1) * P], qdTg[s2][:, t - CTX_TILES, u, r], S[:, u, :], start=True, stop=False)
                        last = nc.tensor.matmul(b[r, u * P:(u + 1) * P], ATg[s2][:, t - CTX_TILES, u, r], vn[:, u, :],
                                                start=False, stop=True)
                    po.close(last)
                else:
                    vn_ready.take(nc.tensor)
                b = ps.open(nc.tensor)
                for u in range(4):
                    t, c = chunk_of(n, u % 2)
                    o = (2 * gp + u // 2) * P
                    last = nc.tensor.matmul(b[:, u * P:(u + 1) * P], ktok[:, t, o:o + P], vns[:, u, :], start=True, stop=True)
                ps.close(last)
                state_job = ps.opened
                yield

        def beside(first, second):
            for _ in range(16):
                next(first)
                next(second)

        def dn_groups(inverse, scan):
            for _ in inverse(0):
                pass
            for gp in range(NG - 1):
                beside(inverse(gp + 1), scan(gp))
            for _ in scan(NG - 1):
                pass

        level_job = [0, 0]

        def chunk_of(n, d):
            c = n if d == 0 else (3 - n if n < 4 else 11 - n)
            return c // 2, c % 2

        def act_dn_inverse(gp):
            s2 = gp % 2

            def copy4(dst):
                b = pa.take(nc.scalar)
                pa.release(nc.scalar.activation(dst, b[:, :].rearrange("p (u c) -> p u c", u=4), ACT.Copy))

            for hh in range(2):
                b = pa.take(nc.scalar)
                pa.release(nc.scalar.activation(kTg[:, hh, :], b[:, :], ACT.Copy))
            b = pa.take(nc.scalar)
            pa.release(nc.scalar.activation(qTg, b[:, :].rearrange("p (h t) -> p h t", h=2), ACT.Copy))
            for pair in DT:
                x_pair = pair[0] >= CTX_TILES
                for r, t in enumerate(pair):
                    dec_in.take(nc.scalar)
                    dec_exp.give(nc.scalar.activation(dec[:, r], dec[:, r], ACT.Exp, scale=-1.0))
                yield
                for r, t in enumerate(pair):
                    copy4(LTm[:, r])
                    mark["lt", gp, t] = pa.left
                    if x_pair:
                        copy4(ATg[s2][:, r])
                if x_pair:
                    mark["at", gp] = pa.left
                yield
                for li in range(1, len(LEVELS)):
                    for r, t in enumerate(pair):
                        copy4(Pm[:, r])
                    yield
                for r, t in enumerate(pair):
                    copy4(ug[s2][:, t])
                    copy4(wTg[s2][:, t])
                    if x_pair:
                        copy4(qdTg[s2][:, r])
                mark["pre", gp] = pa.left
                yield

        def act_dn_scan(gp):
            for n in range(16):
                yield

        def dve_dn_inverse(dv, gp):
            heads = slice(2 * gp * P, 2 * (gp + 1) * P)
            for pair in DT:
                x_pair = pair[0] >= CTX_TILES
                for r, t in enumerate(pair):
                    operand_ready.give(nc.vector.tensor_tensor(u4(dgc[:, r]), u4(identu), unit_scalars(gct[:, 0:64], gp, t), ALU.mult))
                for r, t in enumerate(pair):
                    b = pv.take(nc.vector)
                    pv.release(nc.vector.tensor_tensor(u4(dec[:, r]), b[:, :].rearrange("p (h d c) -> p h d c", h=2, d=2),
                                                       unit_scalars(gct[:, 0:64], gp, t), ALU.subtract))
                    nc.vector.wait_ge(pv.free, pv.left)
                    dec_in.give(nc.vector.tensor_scalar(dec[:, r], dec[:, r], 0.0, None, ALU.max))
                yield
                for r, t in enumerate(pair):
                    dec_exp.take(nc.vector)
                    b = ps.take(nc.vector)
                    ins = nc.vector.tensor_tensor(u4(Lm[:, r]), u4(dec[:, r]),
                                                  over_dirs(b[:, 0:256].rearrange("p (h c) -> p h c", h=2)), ALU.mult)
                    if x_pair:
                        dv(ins)
                        ins = nc.vector.tensor_tensor(u4(Am[:, r]), u4(dec[:, r]),
                                                      over_dirs(b[:, 256:512].rearrange("p (h c) -> p h c", h=2)), ALU.mult)
                    ps.release(ins)
                    nc.vector.wait_ge(ps.free, ps.left)
                    if x_pair:
                        dv(nc.vector.tensor_tensor(u4(Am[:, r]), u4(Am[:, r]), over_heads(incl), ALU.mult))
                    operand_ready.give(nc.vector.tensor_tensor(u4(Lm[:, r]), u4(Lm[:, r]), unit_scalars(beta, gp, t), ALU.mult))
                nc.vector.wait_ge(operand_ready.sem, operand_ready.made)
                for r, t in enumerate(pair):
                    dv(nc.vector.tensor_tensor(u4(Xm[:, r]), u4(Lm[:, r]), over_heads(lvl[:, 0, 0:2]), ALU.mult))
                    dv(nc.vector.tensor_tensor(Xm[:, r], identu, Xm[:, r], ALU.subtract))
                for r, t in enumerate(pair):
                    nc.vector.wait_ge(pa.free, mark["lt", gp, t])
                    dv(nc.vector.tensor_tensor(u4(XTm[:, r]), u4(LTm[:, r]), over_heads(lvl[:, 0, 1:3]), ALU.mult))
                    dv(nc.vector.tensor_tensor(XTm[:, r], identu, XTm[:, r], ALU.subtract))
                if x_pair:
                    nc.vector.wait_ge(pa.full, mark["at", gp])
                yield
                for li in range(1, len(LEVELS)):
                    for r, t in enumerate(pair):
                        operand_ready.give(nc.vector.tensor_tensor(u4(CTm[:, r]), u4(LTm[:, r]), over_heads(lvl[:, li, 1:3]), ALU.mult))
                    for r, t in enumerate(pair):
                        if li < len(LEVELS) - 1:
                            b = ps.take(nc.vector)
                            ps.release(nc.vector.tensor_tensor(Xm[:, r], Xm[:, r], b[:, :].rearrange("p (u c) -> p u c", u=4), ALU.subtract))
                        b = pv.take(nc.vector)
                        pv.release(nc.vector.tensor_tensor(XTm[:, r], XTm[:, r], b[:, :].rearrange("p (u c) -> p u c", u=4), ALU.subtract))
                    nc.vector.wait_ge(pv.free, pv.left)
                    nc.vector.wait_ge(ps.free, ps.left)
                    yield
                for r, t in enumerate(pair):
                    kh = over_dirs(ktok[:, t, heads].rearrange("p (h c) -> p h c", h=2))
                    vh = over_dirs(vtok[:, t, heads].rearrange("p (h c) -> p h c", h=2))
                    dv(nc.vector.tensor_tensor(u4(vbm[:, r]), vh, unit_scalars(beta, gp, t), ALU.mult))
                    if x_pair:
                        qh = over_dirs(qtok[:, t - CTX_TILES, heads].rearrange("p (h c) -> p h c", h=2))
                        dv(nc.vector.tensor_tensor(u4(qem[:, r]), qh, unit_scalars(eg, gp, t), ALU.mult))
                    operand_ready.give(nc.vector.tensor_tensor(u4(kbm[:, r]), kh, unit_scalars(bek, gp, t), ALU.mult))
                yield

        def dve_dn_scan(dv, gp):
            s2 = gp % 2
            heads = slice(2 * gp * P, 2 * (gp + 1) * P)
            nc.vector.wait_ge(pa.free, mark["pre", gp])
            dv(nc.vector.memset(vn, 0.0))
            dv(nc.vector.memset(vns, 0.0))
            operand_ready.give(nc.vector.memset(S, 0.0))
            nc.vector.wait_ge(operand_ready.sem, operand_ready.made)
            for n in range(8):
                b = pv.take(nc.vector)
                for d in range(2):
                    t, c = chunk_of(n, d)
                    r = slice(c * CH, (c + 1) * CH)
                    by_dir = lambda v: v.rearrange("p (h d) c -> p h d c", h=2)[r, :, d, :]
                    ins = nc.vector.tensor_tensor(by_dir(vn), by_dir(ug[s2][:, t]),
                                                  by_dir(b[:, :].rearrange("p (u c) -> p u c", u=4)), ALU.subtract)
                    dv(ins) if d == 0 else pv.release(ins)
                nc.vector.wait_ge(pv.free, pv.left)
                for d in range(2):
                    t, c = chunk_of(n, d)
                    r = slice(c * CH, (c + 1) * CH)
                    by_dir = lambda v: v.rearrange("p (h d) c -> p h d c", h=2)[r, :, d, :]
                    last_decay = dth(ed)[r, d, t, 2 * gp:2 * gp + 2].unsqueeze(2).to_broadcast([CH, 2, P])
                    ins = nc.vector.tensor_tensor(by_dir(vns), by_dir(vn), last_decay, ALU.mult)
                    dv(ins) if d == 0 else vn_ready.give(ins)
                yield
                b = ps.take(nc.vector)
                for u in range(4):
                    t, c = chunk_of(n, u % 2)
                    o = (c * 2 + u % 2) * 32 + t * 8 + 2 * gp + u // 2
                    ins = nc.vector.scalar_tensor_tensor(out=S[:, u, :], in0=S[:, u, :], scalar=glb[:, o:o + 1],
                                                         in1=b[:, u * P:(u + 1) * P], op0=ALU.mult, op1=ALU.add)
                    nc.vector.wait_ge(vn_ready.sem, vn_ready.made) if u == 0 else None
                    dv(ins) if u < 3 else ps.release(ins)
                nc.vector.wait_ge(ps.free, ps.left)
                if n < 7:
                    dv(nc.vector.memset(vns, 0.0))
                if n >= 4:
                    b = po.take(nc.vector)
                    for d in range(2):
                        t, c = chunk_of(n, d)
                        r = slice(c * CH, (c + 1) * CH)
                        dst = qtok[r, t - CTX_TILES, heads].rearrange("p (h c) -> p h c", h=2)
                        src = b[r, :].rearrange("p (h d c) -> p h d c", h=2, d=2)[:, :, d, :]
                        if n < 6:
                            ins = nc.vector.tensor_copy(dst, src)
                        else:
                            ins = nc.vector.tensor_tensor(dst, dst, src, ALU.add)
                        dv(ins) if d == 0 else po.release(ins)
                    nc.vector.wait_ge(po.free, po.left)
                yield

        def dve_dn_out(dv):
            for t in range(2):
                dv(nc.vector.tensor_tensor(sqb[:, 0:D], qtok[:, t, :], qtok[:, t, :], ALU.mult))
                dv(nc.vector.tensor_reduce(stat[:, 0, t * 8:t * 8 + 8], sqb[:, 0:D].rearrange("p (h c) -> p h c", h=8), AX.X, ALU.add))
            var_ready.give(nc.vector.tensor_scalar(stat[:, 1, 0:16], stat[:, 0, 0:16], 1.0 / P, EPS, ALU.mult, ALU.add))
            dve_rstd(dv, 16)
            for t in range(2):
                v = qtok[:, t, :].rearrange("p (h c) -> p h c", h=8)
                dv(nc.vector.tensor_tensor(v, v, stat[:, 2, t * 8:t * 8 + 8].unsqueeze(2).to_broadcast([P, 8, P]), ALU.mult))
                dv(nc.vector.tensor_tensor(v, v, sm("onorm").unsqueeze(1).to_broadcast([P, 8, P]), ALU.mult))
                o_ready.give(nc.vector.tensor_tensor(qtok[:, t, :], qtok[:, t, :], zgs[:, t, :], ALU.mult))

        def pe_dn():
            pe_dn_project()
            norm_ready.take(nc.tensor)
            dn_groups(pe_dn_inverse, pe_dn_scan)
            mark["dn_done"] = (ps.full, ps.closed)
            for t in range(2):
                o_ready.take(nc.tensor)
                for half in range(2):
                    b = pa.open(nc.tensor)
                    for q in range(4):
                        kk = half * 4 + q
                        last = nc.tensor.transpose(b[:, q * P:(q + 1) * P], qtok[:, t, kk * P:(kk + 1) * P], ident)
                    pa.close(last)
            pa.drain(nc.tensor)

        def act_dn(ac):
            act_dn_project(ac)
            dn_groups(act_dn_inverse, act_dn_scan)
            act_sqrt(16)

        def dve_dn(dv):
            dve_dn_project(dv)
            dn_groups(lambda gp: dve_dn_inverse(dv, gp), lambda gp: dve_dn_scan(dv, gp))
            dve_dn_out(dv)

        AT = range(NT)
        block = es.enter_context(nc.Block())

        @block.tensor
        def _(pe):
            pe.wait_ge(p_ld, 16 * N_PARAM)
            for c in range(ADA_C):
                pe_ada(0, c)
            pa.drain(pe)
            pe_turn(xn, AT, xn_ready)
            pe_lin(W_EVIN, (512, 512, 512, 416), hT, AT, pa)
            pe_heads()
            pe_attn()
            pe_turn(o_tok, AT, o_ready)
            pe_lin(W_EVOUT, (512, 512), oT, AT, pv)
            if stop >= 2:
                pe_turn(htok, AT, xn_ready)
                pe_query(0)
                pv.drain(pe)
                pe_peer(0)
            if stop >= 3:
                pe_turn(xn, AT, xn_ready)
                pe_dn()
                pe_lin(W_DNOUT, (512, 512), oT, XT, pv)
            if stop >= 4:
                pe_turn(htok, XT, xn_ready)
                pe_query(1)
                pv.drain(pe)
                pe_peer(1)

        @block.scalar
        def _(act):
            ac = Chain(act, act_sem)
            act_silu(ac)
            act_ada()
            act.wait_ge(ctx_ld, 32)
            act_norm(ac, 0, 0, AT)
            act_z()
            act_heads()
            act_attn()
            act_sqrt(4 * NT)
            act_turn(oT, AT)
            if stop >= 2:
                act_norm(ac, 0, 1, AT)
                act_query(0)
                act_peer(0)
            if stop >= 3:
                act_norm(ac, 1, 0, AT)
                act_dn(ac)
                act_turn(oT, XT)
            if stop >= 4:
                act_norm(ac, 1, 1, XT)
                act_query(1)
                act_peer(1)

        @block.vector
        def _(dve):
            dv = Chain(dve, dve_sem)
            dve.wait_ge(p_ld, 16 * N_PARAM)
            dve_silu(dv)
            for c in range(ADA_C):
                dve_ada(0, c)
            dve_norm(dv, 0, 0, AT)
            dve_heads(dv)
            dve_attn(dv)
            dve_residual(dv, 0, AT, tmpv[:, 0:512])
            vec_free.give(dve.tensor_copy(negs[:, 1:2], ident[:, 0:1]))
            if stop >= 2:
                dve.wait_ge(bc_ld, 16 * BC_COUNT[0, 1])
                dve_norm(dv, 0, 1, AT)
                dve_peer(dv, 0)
            if stop >= 3:
                vec_free.give(dve.tensor_copy(negs[:, 1:2], ident[:, 0:1]))
                dve_norm(dv, 1, 0, AT)
                dve_dn(dv)
                dve_residual(dv, 1, XT, junk[:, 0:512])
            if stop >= 4:
                dve.wait_ge(bc_ld, 16 * BC_COUNT[1, 1])
                dve_norm(dv, 1, 1, XT)
                dve_peer(dv, 1)

        @block.gpsimd
        def _(pool):
            pool_ada(0)
            pool_vectors(0, 0)
            pool_ada(1)
            if stop >= 2:
                pool_vectors(0, 1)
                pool_peer(0)
            if stop >= 3:
                pool_vectors(1, 0)
            if stop >= 4:
                pool_vectors(1, 1)
            if stop >= 4:
                pool_peer(1)

        @block.sync
        def _(sp):
            for dst, src in ((cs[:, 0, :], cT), (cst[:], consts), (smallp[:], small),
                             (keys[:], keysT), (convw[:], conv_w), (wab[:], w_ab)):
                sp.dma_start(dst, src).then_inc(p_ld, 16)
            for w in range(W_END if stop >= 4 else (W_WQ0, W_DNIN, W_WQ1)[stop - 1]):
                if w >= 2:
                    sp.wait_ge(*w_done[w - 2]) if w - 2 in w_done else None
                if w == 2:
                    sp.dma_start(R[:, 0:CTX_TILES, :], ctx_in[0].rearrange("(t p) d -> p t d", p=P)).then_inc(ctx_ld, 16)
                    sp.dma_start(R[:, CTX_TILES:NT, :], x[0].rearrange("(t p) d -> p t d", p=P)).then_inc(ctx_ld, 16)
                if w == W_ADA1:
                    for r in range(2):
                        sp.wait_ge(row_st[r], 16 * ADA_C // 2)
                    sp.dma_start(wuq_sb, w_uq).then_inc(mla_ld, 16)
                    sp.dma_start(wukv_sb, w_ukv).then_inc(mla_ld, 16)
                if w == W_DNOUT:
                    sp.wait_ge(*mark["dn_done"])
                if w in (W_DNIN, W_DNIN + 1):
                    sp.wait_ge(v_read, NT * HEADS * TOPK)
                sp.dma_start(wbuf[:, w % 2], wstream[w]).then_inc(w_ld[w % 2], 16)
            sp.wait_ge(r_ready.sem, r_ready.made)
            if stop >= 4:
                sp.dma_start(out[0].rearrange("(t p) d -> p t d", p=P), R[:, CTX_TILES:NT, :]).then_inc(out_st, 16)
            else:
                sp.dma_start(out.rearrange("t p d -> p t d"), R[:, :, :]).then_inc(out_st, 16)
            sp.wait_ge(out_st, 16)


STOP = 9


def _shape_constants():
    import numpy as np
    c = {}
    i = np.arange(P)[:, None]
    j = np.arange(P)[None, :]
    same = (i // 64) == (j // 64)
    c["ident"] = (i == j)
    c["ones"] = np.ones((P, P))
    c["blk"] = same
    c["incl"] = np.concatenate([same & (i >= j), same & (i <= j)], 1)
    c["strict"] = np.concatenate([same & (i > j), same & (i < j)], 1)
    lv = []
    for m in LEVELS:
        f = (i // m % 2 == 1) & (j // m == i // m - 1)
        lv += [f, f.T, f]
    c["lvl"] = np.concatenate(lv, 1)
    c["iota"] = np.broadcast_to(np.arange(16), (P, 16))
    tok = np.arange(256)
    for name, rot in (("A", 64), ("B", 32)):
        nf = rot // 4
        inv = (np.float32(10000.0) ** (-np.arange(nf, dtype=np.float32) / np.float32(nf))).astype(np.float32)
        ang = np.concatenate([(tok // 64)[:, None].astype(np.float32) * inv,
                              (tok % 64)[:, None].astype(np.float32) * inv], 1)
        for f, n in ((np.cos, "cos"), (np.sin, "sin")):
            c[n + name] = f(ang).reshape(2, P, rot // 2).transpose(1, 0, 2).reshape(P, -1)
    return np.ascontiguousarray(np.concatenate([c[n].astype(np.float32) for n in CONST], 1))


def kernel(x, c, ctx, c_ctx, ada_w, ada_b, ev_w_in, ev_w_out, diff_q_norm, diff_k_norm,
           diff_lam_q1, diff_lam_k1, diff_lam_q2, diff_lam_k2, diff_subln, mla_cq_norm, mla_ckv_norm,
           mla_w_uq, mla_w_ukv, mla_q_norm, mla_k_norm, dn_w_in, dn_conv, dn_a_log, dn_dt_bias,
           dn_o_norm, dn_w_out, peer_wq, peer_k1, peer_k2, peer_u, peer_v):
    import numpy as np
    import concourse.bacc as _bacc
    from concourse import mybir as _mybir
    from concourse.bass_utils import run_bass_kernel_spmd as _run

    cc = np.ascontiguousarray

    def chunks(w):
        n = -(-w.shape[1] // WCH)
        full = np.zeros((D, n * WCH), w.dtype)
        full[:, :w.shape[1]] = w
        return full.reshape(KD, P, n, WCH).transpose(2, 1, 0, 3)

    c2 = np.stack([np.asarray(c_ctx), np.asarray(c)[0]], 0)
    rows = [np.asarray(v).reshape(-1) for v in (
        diff_q_norm, diff_k_norm, diff_subln, mla_cq_norm, mla_ckv_norm, mla_q_norm, mla_k_norm, dn_o_norm,
        diff_lam_q1, diff_lam_k1, diff_lam_q2, diff_lam_k2, dn_a_log, dn_dt_bias)]
    keysT = np.stack([np.asarray(peer_k1), np.asarray(peer_k2)], 1)
    dn = np.asarray(dn_w_in)[0]
    wq = np.asarray(peer_wq)
    aw = np.asarray(ada_w)
    arrays = {
        "x": cc(x), "ctx_in": cc(ctx),
        "cT": cc(c2.reshape(2, KD, P).transpose(2, 1, 0).reshape(P, 2 * KD)),
        "ada_b": cc(ada_b),
        "wstream": cc(np.concatenate([chunks(aw[0]), chunks(np.asarray(ev_w_in)[0]), chunks(aw[1]), chunks(np.asarray(ev_w_out)[0]), chunks(wq[0]),
                                      chunks(dn[:, :4096]), chunks(np.asarray(dn_w_out)[0]), chunks(wq[1])], 0)),
        "small": cc(np.broadcast_to(np.concatenate(rows)[None, :], (P, SMALL_W))),
        "consts": _shape_constants(),
        "keysT": cc(keysT.transpose(3, 0, 1, 2)),
        "w_uq": cc(np.asarray(mla_w_uq)[0].reshape(2, P, 384).transpose(1, 0, 2).reshape(P, 768)),
        "w_ukv": cc(np.asarray(mla_w_ukv)[0]),
        "conv_w": cc(np.asarray(dn_conv)[0].reshape(5, 24, P).transpose(2, 1, 0)),
        "w_ab": cc(dn[:, 4096:].reshape(KD, P, 32).transpose(1, 0, 2)),
        "peer_u0": np.asarray(peer_u)[0], "peer_v0": np.asarray(peer_v)[0],
        "peer_u1": np.asarray(peer_u)[1], "peer_v1": np.asarray(peer_v)[1],
    }
    nc = _bacc.Bacc("TRN2", target_bir_lowering=False, num_devices=1)
    args = {n: nc.dram_tensor(f"in_{n}_dram", a.shape, _mybir.dt.from_np(a.dtype), kind="ExternalInput").ap()
            for n, a in arrays.items()}
    shape = (1, 256, D) if STOP >= 4 else (NT, P, D)
    out = nc.dram_tensor("out_0_dram", shape, _mybir.dt.float32, kind="ExternalOutput").ap()
    build(nc, out=out, stop=STOP, **args)
    r = _run(nc, [{f"in_{n}_dram": a for n, a in arrays.items()}], core_ids=[0])
    return r.results[0]["out_0_dram"]
```

```python
from contextlib import ExitStack

import concourse.bass as bass
from concourse import mybir

F32 = mybir.dt.float32
U32 = mybir.dt.uint32
ALU = mybir.AluOpType
ACT = mybir.ActivationFunctionType
AX = mybir.AxisListType

P = 128
D = 1024
KD = D // P
NT = 4
CTX_TILES = 2
TOK = NT * P
EPS = 1e-6
LAM_INIT = 0.2
DH = 4
MH = 4
ZW = 1952
QK96 = 96
HEADS = 8
NK = 128
TOPK = 16
RING = 8
NEG = -3.0e38
WCH = 512
ADA_C = 12
N_PARAM = 6
XT = range(CTX_TILES, NT)

SMALL = {}
_at = 0
for _n, _w in (("qn", 64), ("kn", 64), ("subln", 128), ("cqn", 256), ("ckvn", 128), ("mqn", 96), ("mkn", 96),
               ("onorm", 128), ("lq1", 64), ("lk1", 64), ("lq2", 64), ("lk2", 64), ("alog", 16), ("dtb", 16)):
    SMALL[_n] = (_at, _w)
    _at += _w
SMALL_W = _at
LEVELS = (1, 2, 4, 8, 16, 32)
CONST = {}
_at = 0
for _n, _w in (("ident", 128), ("ones", 128), ("blk", 128), ("incl", 384), ("strict", 256),
               ("lvl", 2 * 128 * len(LEVELS)), ("iota", 16), ("cosA", 64), ("sinA", 64), ("cosB", 32), ("sinB", 32)):
    CONST[_n] = (_at, _w)
    _at += _w
CONST_W = _at

W_ADA0, W_EVIN, W_ADA1, W_EVOUT, W_WQ0, W_DNIN, W_DNOUT, W_WQ1, W_END = 0, 12, 16, 28, 30, 34, 42, 44, 48


class Signal:

    def __init__(self, sem):
        self.sem, self.made, self.taken = sem, 0, 0

    def give(self, ins):
        self.made += 1
        ins.then_inc(self.sem, 1)

    def take(self, eng):
        self.taken += 1
        eng.wait_ge(self.sem, self.taken)


class Chain:

    def __init__(self, eng, sem):
        self.eng, self.sem, self.n, self.base = eng, sem, 0, 0

    def __call__(self, ins):
        self.n += 1
        ins.then_inc(self.sem, 1)
        self.eng.wait_ge(self.sem, self.base + self.n)

    def alone(self, mark):
        if not isinstance(self.base, int):
            self.eng.sem_inc(mark, 1)


class Pipe:

    def __init__(self, banks, full, free):
        self.banks, self.full, self.free = banks, full, free
        self.opened = self.closed = self.read = self.left = 0

    def open(self, pe):
        if self.opened >= 2:
            pe.wait_ge(self.free, self.opened - 1)
        self.opened += 1
        return self.banks[(self.opened - 1) % 2]

    def close(self, ins):
        self.closed += 1
        ins.then_inc(self.full, 1)

    def drain(self, pe):
        pe.wait_ge(self.free, self.opened)

    def take(self, eng):
        self.read += 1
        eng.wait_ge(self.full, self.read)
        return self.banks[(self.read - 1) % 2]

    def release(self, ins):
        self.left += 1
        ins.then_inc(self.free, 1)


def build(nc, x, ctx_in, cT, ada_b, wstream, small, consts, keysT, w_uq, w_ukv, conv_w, w_ab,
          peer_u0, peer_v0, peer_u1, peer_v1, out, stop=9):
    with ExitStack() as es:
        def sb(name, shape, dt=F32):
            return es.enter_context(nc.sbuf_tensor(name, shape, dt))

        def sem(name):
            return es.enter_context(nc.semaphore(name))

        bank = [es.enter_context(nc.psum_tensor(f"bank{i}", [P, 512], F32)) for i in range(8)]

        R = sb("R", [P, NT, D])
        hT = sb("hT", [P, KD, TOK])
        htok = sb("htok", [P, NT, D])
        wbuf = sb("wbuf", [P, 2, KD, WCH])
        bc = sb("bc", [P, 4, 2, D])
        cst = sb("cst", [P, CONST_W])
        smallp = sb("smallp", [P, SMALL_W])
        keys = sb("keys", [P, 2, 2, NK])
        convw = sb("convw", [P, 24, 5])
        wab = sb("wab", [P, KD, 32])
        cs = sb("cs", [P, 3, KD * 2])
        modT = sb("modT", [P, 2, 16, 2])
        stat = sb("stat", [P, 3, 80])
        lamt = sb("lamt", [P, 72])
        negs = sb("negs", [P, 8])
        SCR = 18432
        scr = sb("scr", [P, SCR])

        def k(name):
            o, w = CONST[name]
            return cst[:, o:o + w]

        def sm(name):
            o, w = SMALL[name]
            return smallp[:, o:o + w]

        ident, ones = k("ident"), k("ones")

        c_ld, p_ld, ctx_ld = sem("consts_landed"), sem("params_landed"), sem("streams_landed")
        ab_ld = [sem(f"ada_bias_landed{i}") for i in range(2)]
        row_ready = Signal(sem("mod_row_ready"))
        row_st = [sem(f"mod_row_stored{i}") for i in range(2)]
        bc_ld = sem("mod_vectors_landed")
        vec_free = Signal(sem("mod_vectors_free"))
        w_ld = [sem(f"w_landed{i}") for i in range(2)]
        out_st = sem("out_stored")
        dve_sem, act_sem, pool_sem = sem("vector_step"), sem("scalar_step"), sem("pool_step")
        vec_mark = sem("vector_mark")
        pa = Pipe(bank[0:2], sem("pa_full"), sem("pa_free"))
        pv = Pipe(bank[2:4], sem("pv_full"), sem("pv_free"))
        ps = Pipe(bank[4:6], sem("scores_full"), sem("scores_free"))
        po = Pipe(bank[6:8], sem("po_full"), sem("po_free"))
        silu_in, silu_ready = Signal(sem("silu_exp")), Signal(sem("silu_ready"))
        mods_ready = Signal(sem("mods_ready"))
        r_ready = Signal(sem("residual_ready"))
        ss_ready, var_ready, std_ready = Signal(sem("sumsq_ready")), Signal(sem("var_ready")), Signal(sem("std_ready"))
        xn_ready = Signal(sem("xn_ready"))
        z_ready = Signal(sem("z_ready"))
        heads_ready = Signal(sem("heads_ready"))
        lam_in, lam_ready = Signal(sem("lam_in")), Signal(sem("lam_exp"))
        nmax_ready = Signal(sem("nmax_ready"))
        o_ready = Signal(sem("o_ready"))
        mla_ld = sem("mla_weights_landed")
        u_land = [sem(f"u_landed{i}") for i in range(RING)]
        v_land = [sem(f"v_landed{i}") for i in range(RING)]
        u_read, v_read = sem("u_read"), sem("v_read")
        q_staged, sc_done, idx_ready, top_ready = sem("q_staged"), sem("keyscores_done"), sem("idx_ready"), sem("top_ready")
        exp_done, gelu_done, w_ready, diag_done, y_free = (sem("exp_done"), sem("gelu_done"), sem("w_ready"),
                                                          sem("diag_done"), sem("y_free"))
        q_ready = Signal(sem("q_ready"))
        y_zero = Signal(sem("y_zero"))

        mark = {}
        mods = nc.dram_tensor("mods_scratch", (2, 2, 6 * D), F32, kind="Internal").ap()

        xn = scr[:, 4096:8192].rearrange("p (t d) -> p t d", t=NT)
        junk = scr[:, 8192:9216]

        class Region:
            def __init__(self, whole):
                self.whole, self.at = whole, 0

            def get(self, n):
                a = self.at
                self.at += n
                assert self.at <= self.whole.shape[1], self.at
                return self.whole[:, a:a + n]

        g = Region(scr)
        z = g.get(NT * ZW).rearrange("p (t c) -> p t c", t=NT)
        qkb = g.get(NT * 8 * QK96).rearrange("p (t g c) -> p t g c", t=NT, g=8)
        kvb = g.get(NT * 768).rearrange("p (t c) -> p t c", t=NT)
        bcx = bc[:, 1:3].rearrange("p v s d -> p (v s d)")
        qbT = bcx[:, 0:2048].rearrange("p (h t) -> p h t", h=MH)
        kbT = bcx[:, 2048:4096].rearrange("p (h t) -> p h t", h=MH)
        tmpv = g.get(2048)
        modbuf = scr[:, g.at:g.at + 2048].rearrange("p (s r c) -> p s r c", s=2, r=2)
        mrow, mbias = modbuf[:, 0], modbuf[:, 1]
        wuq_sb = g.get(768).rearrange("p (k c) -> p k c", k=2)
        wukv_sb = g.get(768)
        cT3 = tmpv[:, 0:3 * TOK].rearrange("p (b t) -> p b t", b=3)
        prob = tmpv[:, 0:1024].rearrange("p (s n) -> p s n", s=2)
        probT = tmpv[:, 1024:2048].rearrange("p (s n) -> p s n", s=2)
        qaT = htok[:, 0:2, :].rearrange("p a (b t) -> p (a b) t", b=2)
        kaT = htok[:, 2:4, :].rearrange("p a (b t) -> p (a b) t", b=2)
        o_tok = hT.rearrange("p k t -> p (k t)").rearrange("p (t d) -> p t d", t=NT)
        oT = htok.rearrange("p t d -> p (t d)").rearrange("p (k t) -> p k t", k=KD)
        rsum = lamt[:, 0:48]
        g = Region(scr)
        qT = g.get(NT * HEADS * 2 * P).rearrange("p (s c) -> p s c", c=2 * P)
        uring = g.get(RING * D).rearrange("p (s d) -> p s d", s=RING)
        g = Region(bcx)
        qst = g.get(2 * 256).rearrange("p (s c) -> p s c", s=2)
        sw = g.get(256)
        cand = g.get(256)
        candw = g.get(256)
        v16 = g.get(32)
        i16 = g.get(32).bitcast(U32)
        sc16 = g.get(32).rearrange("p (s c) -> p s c", s=2)
        j16 = g.get(16).bitcast(U32)
        ab16 = g.get(32).bitcast(U32)
        onehot = g.get(512)
        sel = g.get(32)
        idx = g.get(32).bitcast(U32).rearrange("p (s c) -> p s c", s=2)
        e16 = g.get(32).rearrange("p (s c) -> p s c", s=2)
        act16 = g.get(32).rearrange("p (s c) -> p s c", s=2)
        gel16 = g.get(32).rearrange("p (s c) -> p s c", s=2)
        w16 = g.get(32).rearrange("p (s c) -> p s c", s=2)
        nb = g.get(2)
        zs = g.get(4)
        diag = g.get(4 * 128).rearrange("p (s c) -> p s c", s=4)
        vring = wbuf.rearrange("p s k c -> p (s k c)").rearrange("p (s d) -> p s d", s=RING)
        Y = hT.rearrange("p k t -> p (k t)").rearrange("p (t d) -> p t d", t=NT)
        ybank = [(bank[0], bank[1]), (bank[2], bank[3])]
        scbank = bank[4:6]

        def peer_tiles(l):
            return range(NT) if l == 0 else range(CTX_TILES, NT)

        def act_silu(ac):
            nc.scalar.wait_ge(p_ld, 16 * N_PARAM)
            silu_in.give(nc.scalar.activation(cs[:, 1, :], cs[:, 0, :], ACT.Exp, scale=-1.0))

        def dve_silu(dv):
            silu_in.take(nc.vector)
            dv(nc.vector.tensor_scalar_add(cs[:, 1, :], cs[:, 1, :], 1.0))
            dv(nc.vector.reciprocal(cs[:, 2, :], cs[:, 1, :]))
            nc.vector.wait_ge(p_ld, 16 * N_PARAM)
            silu_ready.give(nc.vector.tensor_tensor(cs[:, 2, :], cs[:, 2, :], cs[:, 0, :], ALU.mult))

        def pe_ada(l, c):
            if (l, c) == (0, 0):
                silu_ready.take(nc.tensor)
            w = (W_ADA0, W_ADA1)[l] + c
            nc.tensor.wait_ge(w_ld[w % 2], 16 * (w // 2 + 1))
            b = pa.open(nc.tensor)
            sc = cs[:, 2, :].rearrange("p (k s) -> p k s", k=KD)
            for kk in range(KD):
                last = nc.tensor.matmul(b[0:2, :], sc[:, kk, :], wbuf[:, w % 2, kk, :], start=(kk == 0), stop=(kk == KD - 1))
            pa.close(last)
            used_chunk(w, pa)
            mark["ada", l, c] = pa.closed
            if c < 4:
                b = pa.open(nc.tensor)
                nc.tensor.wait_ge(pa.free, pa.opened - 1)
                for q in range(4):
                    last = nc.tensor.transpose(b[:, 2 * q:2 * q + 2], mrow[0:2, c % 2, q * P:(q + 1) * P], ident[0:2, 0:2])
                pa.close(last)

        def dve_ada(l, c):
            n = l * ADA_C + c
            nc.vector.wait_ge(ab_ld[n % 2], 16 * (n // 2 + 1))
            if n >= 2:
                nc.vector.wait_ge(row_st[n % 2], 16 * (n // 2))
            nc.vector.wait_ge(pa.full, mark["ada", l, c])
            one = 1.0 if c in (2, 3, 8, 9) else 0.0
            nc.vector.scalar_tensor_tensor(out=mrow[0:2, n % 2, :], in0=bank[(mark["ada", l, c] - 1) % 2][0:2, :], scalar=one,
                                           in1=mbias[0:2, n % 2, :], op0=ALU.add, op1=ALU.add).then_inc(pa.free, 1)
            nc.vector.wait_ge(pa.free, mark["ada", l, c])
            row_ready.give(nc.vector.tensor_copy(negs[0:2, 6 + n % 2:7 + n % 2], mrow[0:2, n % 2, 0:1]))
            if c < 4:
                nc.vector.wait_ge(pa.full, mark["ada", l, c] + 1)
                nc.vector.tensor_copy(modT[:, l, 4 * c:4 * c + 4, :],
                                      bank[mark["ada", l, c] % 2][:, 0:8].rearrange("p (q s) -> p q s", q=4)).then_inc(pa.free, 1)
            if c == 3:
                nc.vector.wait_ge(pa.free, mark["ada", l, c] + 1)
                mods_ready.give(nc.vector.tensor_copy(lamt[:, 54 + l:55 + l], modT[:, l, 0, 0:1]))

        def act_ada():
            pa.read += ADA_C + 4
            pa.left += ADA_C + 4

        def pool_ada(l):
            for n in range(l * ADA_C, (l + 1) * ADA_C + 2):
                if n < (l + 1) * ADA_C:
                    if l == 1 and n == ADA_C:
                        nc.gpsimd.wait_ge(pa.full, mark["heads"])
                    if n >= 2:
                        nc.gpsimd.wait_ge(row_ready.sem, n - 1)
                    o = (n % ADA_C) * 512
                    nc.gpsimd.dma_start(mbias[0:2, n % 2, :], ada_b[l:l + 1, o:o + 512].to_broadcast([2, 512]))\
                        .then_inc(ab_ld[n % 2], 16)
                m = n - 2
                if m >= l * ADA_C:
                    nc.gpsimd.wait_ge(row_ready.sem, m + 1)
                    o = (m % ADA_C) * 512
                    nc.gpsimd.dma_start(mods[l, :, o:o + 512], mrow[0:2, m % 2, :]).then_inc(row_st[m % 2], 16)

        def pool_vectors(l, part):
            if part == 0:
                for r in range(2):
                    nc.gpsimd.wait_ge(row_st[r], 16 * (l + 1) * ADA_C // 2)
            if (l, part) != (0, 0):
                vec_free.take(nc.gpsimd)
            for v, at in (((0, 2), (3, 5)) if part == 0 else ((1, 3), (2, 4))):
                for s in ((0, 1) if l == 0 else (1,)):
                    nc.gpsimd.dma_start(bc[:, v, s, :], mods[l, s:s + 1, at * D:(at + 1) * D].to_broadcast([P, D]))\
                        .then_inc(bc_ld, 16)

        BC_COUNT = {(0, 0): 4, (0, 1): 8, (1, 0): 10, (1, 1): 12}

        def act_norm(ac, l, sub, tiles):
            if (l, sub) != (0, 0):
                r_ready.take(nc.scalar)
            for t in tiles:
                ac(nc.scalar.activation(junk, R[:, t, :], ACT.Square, accum_out=stat[:, 0, t:t + 1]))
            ss_ready.give(nc.scalar.activation(stat[:, 1, 0:NT], stat[:, 0, 0:NT], ACT.Copy))
            var_ready.take(nc.scalar)
            std_ready.give(nc.scalar.activation(stat[:, 0, 0:NT], stat[:, 1, 0:NT], ACT.Sqrt))
            if sub == 0:
                mods_ready.take(nc.scalar)
                for t in tiles:
                    s = 0 if t < CTX_TILES else 1
                    for half in range(2):
                        b = pa.take(nc.scalar)
                        for q in range(4):
                            kk = half * 4 + q
                            ins = nc.scalar.activation(hT[:, kk, t * P:(t + 1) * P], b[:, q * P:(q + 1) * P],
                                                       ACT.Identity, scale=modT[:, l, 8 + kk, s:s + 1],
                                                       bias=modT[:, l, kk, s:s + 1])
                        pa.release(ins)
            else:
                act_hT(tiles)

        def act_hT(tiles):
            for t in tiles:
                for half in range(2):
                    b = pa.take(nc.scalar)
                    pa.release(nc.scalar.activation(
                        hT[:, half * 4:half * 4 + 4, t * P:(t + 1) * P],
                        b[:, :].rearrange("p (q t) -> p q t", q=4), ACT.Copy))

        def dve_norm(dv, l, sub, tiles):
            t0, t1 = tiles[0], tiles[-1] + 1
            ss_ready.take(nc.vector)
            var_ready.give(nc.vector.tensor_scalar(stat[:, 1, 0:NT], stat[:, 1, 0:NT], 1.0 / D, EPS, ALU.mult, ALU.add))
            std_ready.take(nc.vector)
            dv(nc.vector.reciprocal(stat[:, 2, t0:t1], stat[:, 0, t0:t1]))
            for t in tiles:
                s = 0 if t < CTX_TILES else 1
                if sub == 0:
                    xn_ready.give(nc.vector.tensor_scalar(xn[:, t, :], R[:, t, :], stat[:, 2, t:t + 1], None, ALU.mult))
                else:
                    dv(nc.vector.scalar_tensor_tensor(out=htok[:, t, :], in0=R[:, t, :], scalar=stat[:, 2, t:t + 1],
                                                      in1=bc[:, 2, s, :], op0=ALU.mult, op1=ALU.mult))
                    xn_ready.give(nc.vector.tensor_tensor(htok[:, t, :], htok[:, t, :], bc[:, 1, s, :], ALU.add))

        def pe_turn(src, tiles, ready):
            for t in tiles:
                ready.take(nc.tensor)
                for half in range(2):
                    b = pa.open(nc.tensor)
                    for q in range(4):
                        kk = half * 4 + q
                        last = nc.tensor.transpose(b[:, q * P:(q + 1) * P], src[:, t, kk * P:(kk + 1) * P], ident)
                    pa.close(last)
            pa.drain(nc.tensor)

        def pe_lin(first, widths, lhs, tiles, pipe):
            for c, n in enumerate(widths):
                w = first + c
                nc.tensor.wait_ge(w_ld[w % 2], 16 * (w // 2 + 1))
                for t in tiles:
                    b = pipe.open(nc.tensor)
                    for kk in range(KD):
                        last = nc.tensor.matmul(b[:, 0:n], lhs[:, kk, t * P:(t + 1) * P], wbuf[:, w % 2, kk, 0:n],
                                                start=(kk == 0), stop=(kk == KD - 1))
                    pipe.close(last)
                used_chunk(w, pipe)

        def used_chunk(w, pipe):
            w_done[w] = (pipe.full, pipe.closed)

        w_done = {}
        def act_z():
            act_lambda()
            for c, n in ((3, 416), (0, 512), (1, 512), (2, 512)):
                for t in range(NT):
                    b = pa.take(nc.scalar)
                    pa.release(nc.scalar.activation(z[:, t, c * 512:c * 512 + n], b[:, 0:n], ACT.Copy))
                    mark["z", c, t] = pa.left
                    if (c, t) == (3, 3):
                        act_sqrt_of(16, 18)
                    elif (c, t) == (1, 1):
                        act_sqrt(32)
                    elif (c, t) == (2, 1):
                        act_sqrt_of(0, 16)
                if c == 0:
                    act_latents()

        def act_sqrt_of(a, b):
            var_ready.take(nc.scalar)
            st = [stat[:, i, 0:72].rearrange("p (t c) -> p t c", t=NT) for i in range(2)]
            std_ready.give(nc.scalar.activation(st[0][:, :, a:b], st[1][:, :, a:b], ACT.Sqrt))

        def act_sqrt(n):
            var_ready.take(nc.scalar)
            std_ready.give(nc.scalar.activation(stat[:, 0, 0:n], stat[:, 1, 0:n], ACT.Sqrt))

        def dve_rstd(dv, n):
            std_ready.take(nc.vector)
            dv(nc.vector.reciprocal(stat[:, 2, 0:n], stat[:, 0, 0:n]))

        def dve_rope(dv, v, groups, half, cos, sin, tmp):
            n = groups * half
            x1, x2 = v[:, :, 0:half], v[:, :, half:2 * half]
            c = cos.unsqueeze(1).to_broadcast([P, groups, half])
            s = sin.unsqueeze(1).to_broadcast([P, groups, half])
            t1, t2, t3 = (tmp[:, i * n:(i + 1) * n].rearrange("p (g c) -> p g c", g=groups) for i in range(3))
            dv(nc.vector.tensor_tensor(t1, x1, c, ALU.mult))
            dv(nc.vector.tensor_tensor(t2, x2, s, ALU.mult))
            dv(nc.vector.tensor_tensor(t3, x1, s, ALU.mult))
            dv(nc.vector.tensor_tensor(x1, t1, t2, ALU.subtract))
            dv(nc.vector.tensor_tensor(t1, x2, c, ALU.mult))
            return nc.vector.tensor_tensor(x2, t3, t1, ALU.add)

        def dve_lambda(dv):
            nc.vector.wait_ge(p_ld, 16 * N_PARAM)
            for i, (a, b) in enumerate((("lq1", "lk1"), ("lq2", "lk2"))):
                dv(nc.vector.tensor_tensor(tmpv[:, 0:64], sm(a), sm(b), ALU.mult))
                ins = nc.vector.tensor_reduce(lamt[:, 48 + i:49 + i], tmpv[:, 0:64], AX.X, ALU.add)
                dv(ins) if i == 0 else lam_in.give(ins)
            lam_ready.take(nc.vector)
            dv(nc.vector.tensor_tensor(lamt[:, 52:53], lamt[:, 51:52], lamt[:, 50:51], ALU.subtract))
            dv(nc.vector.tensor_scalar_add(lamt[:, 52:53], lamt[:, 52:53], -LAM_INIT))

        def act_lambda():
            lam_in.take(nc.scalar)
            lam_ready.give(nc.scalar.activation(lamt[:, 50:52], lamt[:, 48:50], ACT.Exp))

        def dve_heads(dv):
            dve_lambda(dv)
            st = [stat[:, i, 0:72].rearrange("p (t c) -> p t c", t=NT) for i in range(3)]
            for t in range(NT):
                nc.vector.wait_ge(pa.free, mark["z", 3, t])
                zc = z[:, t, 1536:1920]
                dv(nc.vector.tensor_tensor(tmpv[:, 0:384], zc, zc, ALU.mult))
                dv(nc.vector.tensor_reduce(st[0][:, t, 16:17], tmpv[:, 0:256], AX.X, ALU.add))
                dv(nc.vector.tensor_reduce(st[0][:, t, 17:18], tmpv[:, 256:384], AX.X, ALU.add))
            dv(nc.vector.tensor_scalar(st[1][:, :, 16:17], st[0][:, :, 16:17], 1.0 / 256, EPS, ALU.mult, ALU.add))
            var_ready.give(nc.vector.tensor_scalar(st[1][:, :, 17:18], st[0][:, :, 17:18], 1.0 / 128, EPS, ALU.mult, ALU.add))
            std_ready.take(nc.vector)
            dv(nc.vector.reciprocal(st[2][:, :, 16:18], st[0][:, :, 16:18]))
            for t in range(NT):
                for a, n, c, name in ((1536, 256, 16, "cqn"), (1792, 128, 17, "ckvn")):
                    v = z[:, t, a:a + n]
                    ins = nc.vector.scalar_tensor_tensor(out=v, in0=v, scalar=st[2][:, t, c:c + 1], in1=sm(name),
                                                         op0=ALU.mult, op1=ALU.mult)
                    dv(ins) if c == 16 else heads_ready.give(ins)
            nc.vector.wait_ge(pa.free, mark["mla"])
            for t in range(NT):
                dv(nc.vector.tensor_copy(qkb[:, t, 4:8, 0:64], kvb[:, t, :].rearrange("p (h c) -> p h c", h=MH)[:, :, 0:64]))
                dv(nc.vector.tensor_copy(qkb[:, t, 4:8, 64:96], z[:, t, 1920:1952].unsqueeze(1).to_broadcast([P, 4, 32])))
                v = qkb[:, t, :, :].rearrange("p g c -> p (g c)")
                dv(nc.vector.tensor_tensor(tmpv[:, 0:768], v, v, ALU.mult))
                dv(nc.vector.tensor_reduce(stat[:, 0, t * 8:t * 8 + 8], tmpv[:, 0:768].rearrange("p (g c) -> p g c", g=8), AX.X, ALU.add))
            var_ready.give(nc.vector.tensor_scalar(stat[:, 1, 0:32], stat[:, 0, 0:32], 1.0 / QK96, EPS, ALU.mult, ALU.add))
            dve_rstd(dv, 32)
            for t in range(NT):
                v = qkb[:, t, :, :]
                dv(nc.vector.tensor_tensor(v, v, stat[:, 2, t * 8:t * 8 + 8].unsqueeze(2).to_broadcast([P, 8, QK96]), ALU.mult))
                dv(nc.vector.tensor_tensor(v[:, 0:4], v[:, 0:4], sm("mqn").unsqueeze(1).to_broadcast([P, 4, QK96]), ALU.mult))
                ins = nc.vector.tensor_tensor(v[:, 4:8], v[:, 4:8], sm("mkn").unsqueeze(1).to_broadcast([P, 4, QK96]), ALU.mult)
                if t >= CTX_TILES:
                    dv(ins)
                    o = (t - CTX_TILES) * 16
                    ins = dve_rope(dv, v[:, :, 64:96], 8, 16, k("cosB")[:, o:o + 16], k("sinB")[:, o:o + 16], tmpv)
                heads_ready.give(ins)
            nc.vector.wait_ge(heads_ready.sem, heads_ready.made)
            for t in range(NT):
                nc.vector.wait_ge(pa.free, mark["z", 1, t])
                zq = z[:, t, 0:1024]
                dv(nc.vector.tensor_tensor(tmpv[:, 0:1024], zq, zq, ALU.mult))
                dv(nc.vector.tensor_reduce(st[0][:, t, 0:16], tmpv[:, 0:1024].rearrange("p (g c) -> p g c", g=16), AX.X, ALU.add))
            var_ready.give(nc.vector.tensor_scalar(st[1][:, :, 0:16], st[0][:, :, 0:16], 1.0 / 64, EPS, ALU.mult, ALU.add))
            std_ready.take(nc.vector)
            dv(nc.vector.reciprocal(st[2][:, :, 0:16], st[0][:, :, 0:16]))
            for t in range(NT):
                zq = z[:, t, 0:1024].rearrange("p (g c) -> p g c", g=16)
                dv(nc.vector.tensor_tensor(zq, zq, st[2][:, t, 0:16].unsqueeze(2).to_broadcast([P, 16, 64]), ALU.mult))
                for a, name in ((0, "qn"), (8, "kn")):
                    v = zq[:, a:a + 8, :]
                    if a == 0 or t >= CTX_TILES:
                        dv(nc.vector.tensor_tensor(v, v, sm(name).unsqueeze(1).to_broadcast([P, 8, 64]), ALU.mult))
                    else:
                        heads_ready.give(nc.vector.tensor_tensor(v, v, sm(name).unsqueeze(1).to_broadcast([P, 8, 64]), ALU.mult))
                if t >= CTX_TILES:
                    o = (t - CTX_TILES) * 32
                    heads_ready.give(dve_rope(dv, zq, 16, 32, k("cosA")[:, o:o + 32], k("sinA")[:, o:o + 32], tmpv))

        def pe_latents():
            for t in range(NT):
                heads_ready.take(nc.tensor)
                b = pa.open(nc.tensor)
                for q in range(3):
                    last = nc.tensor.transpose(b[:, q * P:(q + 1) * P], z[:, t, 1536 + q * P:1536 + (q + 1) * P], ident)
                pa.close(last)
            pa.drain(nc.tensor)
            nc.tensor.wait_ge(mla_ld, 32)
            for t in range(NT):
                tt = slice(t * P, (t + 1) * P)
                b = pa.open(nc.tensor)
                nc.tensor.matmul(b[:, 0:384], cT3[:, 0, tt], wuq_sb[:, 0, :], start=True, stop=False)
                pa.close(nc.tensor.matmul(b[:, 0:384], cT3[:, 1, tt], wuq_sb[:, 1, :], start=False, stop=True))
                for half in range(2):
                    b = pa.open(nc.tensor)
                    pa.close(nc.tensor.matmul(b[:, 0:384], cT3[:, 2, tt], wukv_sb[:, half * 384:(half + 1) * 384],
                                              start=True, stop=True))

        def pe_heads():
            for t in range(NT):
                heads_ready.take(nc.tensor)
                for base in (0, 4):
                    b = pa.open(nc.tensor)
                    for h in range(MH):
                        last = nc.tensor.transpose(b[0:QK96, h * P:(h + 1) * P], qkb[:, t, base + h, :], ident)
                    pa.close(last)
            for t in range(NT):
                heads_ready.take(nc.tensor)
                for base in (0, 512):
                    b = pa.open(nc.tensor)
                    for h in range(DH):
                        last = nc.tensor.transpose(b[:, h * P:(h + 1) * P], z[:, t, base + h * P:base + (h + 1) * P], ident)
                    pa.close(last)
            pa.drain(nc.tensor)
            mark["heads"] = pa.closed

        def act_latents():
            for t in range(NT):
                b = pa.take(nc.scalar)
                pa.release(nc.scalar.activation(cT3[:, :, t * P:(t + 1) * P], b[:, 0:3 * P].rearrange("p (h t) -> p h t", h=3), ACT.Copy))
            for t in range(NT):
                b = pa.take(nc.scalar)
                pa.release(nc.scalar.activation(qkb[:, t, 0:4, :], b[:, 0:384].rearrange("p (h c) -> p h c", h=4), ACT.Copy))
                for half in range(2):
                    b = pa.take(nc.scalar)
                    pa.release(nc.scalar.activation(kvb[:, t, half * 384:(half + 1) * 384], b[:, 0:384], ACT.Copy))
            mark["mla"] = pa.left

        def act_heads():
            for t in range(NT):
                for dst in (qbT, kbT):
                    b = pa.take(nc.scalar)
                    pa.release(nc.scalar.activation(dst[0:QK96, :, t * P:(t + 1) * P],
                                                    b[0:QK96, :].rearrange("p (h t) -> p h t", h=MH), ACT.Copy))
            for t in range(NT):
                for dst in (qaT, kaT):
                    b = pa.take(nc.scalar)
                    pa.release(nc.scalar.activation(dst[:, :, t * P:(t + 1) * P], b[:, :].rearrange("p (h t) -> p h t", h=4), ACT.Copy))

        UNITS = [(t, m) for t in range(NT) for m in range(12)]

        def unit(u):
            t, m = UNITS[u]
            return t, m, (CTX_TILES if t < CTX_TILES else NT), (64 ** -0.5 if m < 8 else QK96 ** -0.5)

        def pe_attn():
            def scores(u):
                t, m, nk, _ = unit(u)
                b = ps.open(nc.tensor)
                if m < 8:
                    r = slice((m % 2) * 64, (m % 2) * 64 + 64)
                    q, kt = qaT[r, m // 2, t * P:(t + 1) * P], kaT[r, m // 2, 0:nk * P]
                else:
                    q, kt = qbT[0:QK96, m - 8, t * P:(t + 1) * P], kbT[0:QK96, m - 8, 0:nk * P]
                ps.close(nc.tensor.matmul(b[:, 0:nk * P], q, kt, start=True, stop=True))

            def turn(u):
                nk = unit(u)[2]
                b = pv.open(nc.tensor)
                nc.tensor.wait_ge(ps.free, u + 1)
                for c in range(nk):
                    last = nc.tensor.transpose(b[:, c * P:(c + 1) * P], prob[:, u % 2, c * P:(c + 1) * P], ident)
                pv.close(last)
                turned[u] = pv.opened

            def values(u):
                t, m, nk, _ = unit(u)
                b = po.open(nc.tensor)
                nc.tensor.wait_ge(pv.free, turned[u])
                for c in range(nk):
                    v = z[:, c, 1024 + (m // 2) * P:1024 + (m // 2 + 1) * P] if m < 8 else \
                        kvb[:, c, (m - 8) * 192 + 64:(m - 8) * 192 + 192]
                    last = nc.tensor.matmul(b[:, 0:P], probT[:, u % 2, c * P:(c + 1) * P], v, start=(c == 0), stop=(c == nk - 1))
                po.close(last)
                if u % 4 == 3:
                    pe_ada(1, u // 4)

            turned = {}
            scores(0)
            for u in range(len(UNITS)):
                if u + 1 < len(UNITS):
                    scores(u + 1)
                turn(u)
                if u:
                    values(u - 1)
            values(len(UNITS) - 1)
            pa.drain(nc.tensor)

        def act_attn():
            act_ada()
            for u in range(len(UNITS)):
                _, _, nk, scale = unit(u)
                nmax_ready.take(nc.scalar)
                ps.release(nc.scalar.activation(prob[:, u % 2, 0:nk * P], ps.banks[u % 2][:, 0:nk * P], ACT.Exp,
                                                bias=negs[:, 2 + u % 2:3 + u % 2], scale=scale, accum_out=rsum[:, u:u + 1]))

        def dve_attn(dv):
            def nmax(u):
                _, _, nk, scale = unit(u)
                b = ps.take(nc.vector)
                dv(nc.vector.tensor_reduce(negs[:, u % 2:u % 2 + 1], b[:, 0:nk * P], AX.X, ALU.max))
                nmax_ready.give(nc.vector.tensor_scalar(negs[:, 2 + u % 2:3 + u % 2], negs[:, u % 2:u % 2 + 1],
                                                        -scale, None, ALU.mult))

            def turned(u):
                nk = unit(u)[2]
                b = pv.take(nc.vector)
                pv.release(nc.vector.tensor_copy(probT[:, u % 2, 0:nk * P], b[:, 0:nk * P]))
                if u >= 2:
                    nc.vector.wait_ge(po.free, po.left)
                ins = nc.vector.reciprocal(negs[:, 4 + u % 2:5 + u % 2], rsum[:, u:u + 1])
                lam = unit(u)[1] < 8 and u % 2
                dv(ins)
                if lam:
                    dv(nc.vector.tensor_tensor(negs[:, 4 + u % 2:5 + u % 2], negs[:, 4 + u % 2:5 + u % 2], lamt[:, 52:53], ALU.mult))

            def values(u):
                t, m, nk, _ = unit(u)
                b = po.take(nc.vector)
                nc.vector.wait_ge(po.free, po.left)
                if m < 8:
                    dst = o_tok[:, t, (m // 2) * P:(m // 2 + 1) * P]
                else:
                    dst = o_tok[:, t, (m - 4) * P:(m - 3) * P]
                if m < 8 and m % 2:
                    po.release(nc.vector.scalar_tensor_tensor(out=dst, in0=b[:, 0:P], scalar=negs[:, 4 + u % 2:5 + u % 2], in1=dst,
                                                              op0=ALU.mult, op1=ALU.add))
                else:
                    po.release(nc.vector.tensor_scalar(dst, b[:, 0:P], negs[:, 4 + u % 2:5 + u % 2], None, ALU.mult))
                if u % 4 == 3:
                    dve_ada(1, u // 4)

            nmax(0)
            for u in range(len(UNITS)):
                if u + 1 < len(UNITS):
                    nmax(u + 1)
                turned(u)
                if u:
                    values(u - 1)
            values(len(UNITS) - 1)
            nc.vector.wait_ge(po.free, po.left)
            for t in range(NT):
                v = o_tok[:, t, 0:512]
                dv(nc.vector.tensor_tensor(tmpv[:, 0:512], v, v, ALU.mult))
                dv(nc.vector.tensor_reduce(stat[:, 0, t * 4:t * 4 + 4], tmpv[:, 0:512].rearrange("p (g c) -> p g c", g=4), AX.X, ALU.add))
            var_ready.give(nc.vector.tensor_scalar(stat[:, 1, 0:16], stat[:, 0, 0:16], 1.0 / P, EPS, ALU.mult, ALU.add))
            dve_rstd(dv, 16)
            for t in range(NT):
                v = o_tok[:, t, 0:512].rearrange("p (g c) -> p g c", g=4)
                dv(nc.vector.tensor_tensor(v, v, stat[:, 2, t * 4:t * 4 + 4].unsqueeze(2).to_broadcast([P, 4, P]), ALU.mult))
                o_ready.give(nc.vector.scalar_tensor_tensor(out=v, in0=v, scalar=1.0 - LAM_INIT,
                                                            in1=sm("subln").unsqueeze(1).to_broadcast([P, 4, P]),
                                                            op0=ALU.mult, op1=ALU.mult))

        def act_turn(dst, tiles):
            for t in tiles:
                for half in range(2):
                    b = pa.take(nc.scalar)
                    pa.release(nc.scalar.activation(dst[:, half * 4:half * 4 + 4, t * P:(t + 1) * P],
                                                    b[:, :].rearrange("p (q t) -> p q t", q=4), ACT.Copy))

        def dve_residual(dv, l, tiles, tmp):
            n = 0
            nc.vector.wait_ge(bc_ld, 16 * BC_COUNT[l, 0])
            for c in range(2):
                for t in tiles:
                    n += 1
                    s = 0 if t < CTX_TILES else 1
                    b = pv.take(nc.vector)
                    cc = slice(c * 512, (c + 1) * 512)
                    pv.release(nc.vector.tensor_tensor(tmp, b[:, :], bc[:, 0, s, cc], ALU.mult))
                    nc.vector.wait_ge(pv.free, pv.left)
                    ins = nc.vector.tensor_tensor(R[:, t, cc], R[:, t, cc], tmp, ALU.add)
                    r_ready.give(ins) if n == 2 * len(tiles) else dv(ins)
            nc.vector.wait_ge(r_ready.sem, r_ready.made)
            if l == 1:
                vec_free.give(nc.vector.tensor_copy(negs[:, 0:1], ident[:, 0:1]))

        qT4 = qT.rearrange("p (t h) c -> p t h c", h=HEADS)
        qTf = qT.rearrange("p s c -> p (s c)")
        htf = htok.rearrange("p t d -> p (t d)")
        Yf = Y.rearrange("p t d -> p (t d)")

        def stage(s, gs, par):
            if not (isinstance(gs, int) and gs < 2):
                nc.scalar.wait_ge(sc_done, gs - 1)
            nc.scalar.activation(qst[:, par, :], qTf[:, bass.ds(s * 256, 256)], ACT.Copy).then_inc(q_staged, 1)

        def keyscores(l, gs, par):
            nc.tensor.wait_ge(q_staged, gs + 1)
            if not (isinstance(gs, int) and gs < 2):
                nc.tensor.wait_ge(idx_ready, gs - 1)
            nc.tensor.matmul(scbank[par][:, 0:NK], qst[:, par, 0:P], keys[:, l, 0, :], start=True, stop=True)
            nc.tensor.matmul(scbank[par][:, NK:2 * NK], qst[:, par, P:2 * P], keys[:, l, 1, :],
                             start=True, stop=True).then_inc(sc_done, 1)

        def pe_query(l):
            base = 0 if l == 0 else NT * HEADS
            tiles = peer_tiles(l)
            a, n = tiles[0] * P, len(tiles) * P
            for c in range(4):
                w = (W_WQ0 if l == 0 else W_WQ1) + c
                nc.tensor.wait_ge(w_ld[w % 2], 16 * (w // 2 + 1))
                for cb in range(4):
                    b = pa.open(nc.tensor)
                    for kk in range(KD):
                        last = nc.tensor.matmul(b[:, 0:n], wbuf[:, w % 2, kk, cb * P:(cb + 1) * P], hT[:, kk, a:a + n],
                                                start=(kk == 0), stop=(kk == KD - 1))
                    pa.close(last)
                    if (c, cb) == (1, 0):
                        keyscores(l, base, 0)
                        keyscores(l, base + 1, 1)
                used_chunk(w, pa)
            mark[f"q{l}"] = pa.closed
            pa.drain(nc.tensor)

        def act_query(l):
            nt = len(peer_tiles(l))
            base = 0 if l == 0 else NT * HEADS
            for c in range(4):
                if c == 1:
                    nc.scalar.wait_ge(pa.free, pa.left)
                    stage(0, base, 0)
                    stage(1, base + 1, 1)
                for cb in range(4):
                    b = pa.take(nc.scalar)
                    pa.release(nc.scalar.activation(qT4[:, 0:nt, 2 * c + cb // 2, (cb % 2) * P:(cb % 2 + 1) * P],
                                                    b[:, 0:nt * P].rearrange("p (t c) -> p t c", t=nt), ACT.Copy))
            nc.scalar.wait_ge(pa.free, pa.left)

        def steps(eng, l, body, chain=None):
            n = len(peer_tiles(l)) * HEADS
            base = 0 if l == 0 else NT * HEADS
            start = chain.n if chain else 0
            for p in range(2):
                body(p, base + p, p, 0, True, n)
            per = chain.n - start if chain else 0
            start += per
            with eng.Fori(1, n // 2 - 1) as i:
                if chain:
                    chain.base, chain.n = (i - 1) * per + start, 0
                for p in range(2):
                    body(i * 2 + p, i * 2 + (base + p), p, i, False, n)
                if chain:
                    assert chain.n == per, (chain.n, per)
            if chain:
                chain.base, chain.n = 0, start + per * (n // 2 - 2)
            for p in range(2):
                body(n - 2 + p, base + n - 2 + p, p, None, False, n)

        def tab(l, which):
            return ((peer_u0, peer_v0), (peer_u1, peer_v1))[l][which]

        def pool_peer(l):
            def body(s, gs, par, i, first, n):
                dyn = not isinstance(s, int)

                def hold(sm_, v):
                    if isinstance(v, int) and v <= 0:
                        return
                    nc.gpsimd.wait_ge(sm_, v)
                    if dyn:
                        nc.gpsimd.sem_inc(pool_sem, 1)

                hold(idx_ready, gs + 1)
                for which, ring, land, read in ((0, uring, u_land, u_read), (1, vring, v_land, v_read)):
                    if first and par == 0 and which == 1:
                        nc.gpsimd.wait_ge(pa.full, mark[f"q{l}"])
                    for kk in range(TOPK):
                        hold(read, gs * 16 + (kk - RING + 1))
                        nc.gpsimd.indirect_dma_start(
                            ring[:, kk % RING, :], None, tab(l, which),
                            bass.IndirectOffsetOnAxis(idx[:, par, kk:kk + 1], 0)).then_inc(land[kk % RING], 16)
            steps(nc.gpsimd, l, body)

        def dve_route(dv, s, gs, par):
            b = scbank[par]
            nc.vector.wait_ge(sc_done, gs + 1)
            for half in range(2):
                src = b[:, half * NK:(half + 1) * NK]
                o = half * TOPK
                dv.alone(vec_mark)
                dv(nc.vector.max(v16[:, o:o + 8], src))
                dv.alone(vec_mark)
                dv(nc.vector.max_index(i16[:, o:o + 8], v16[:, o:o + 8], src))
                dv.alone(vec_mark)
                dv(nc.vector.match_replace(sw[:, 0:NK], v16[:, o:o + 8], src, NEG))
                dv.alone(vec_mark)
                dv(nc.vector.max(v16[:, o + 8:o + 16], sw[:, 0:NK]))
                dv.alone(vec_mark)
                dv(nc.vector.max_index(i16[:, o + 8:o + 16], v16[:, o + 8:o + 16], sw[:, 0:NK]))
            c2 = cand.rearrange("p (a b) -> p a b", a=TOPK)
            dv(nc.vector.tensor_tensor(c2, v16[:, 0:16].unsqueeze(2).to_broadcast([P, TOPK, TOPK]),
                                       v16[:, 16:32].unsqueeze(1).to_broadcast([P, TOPK, TOPK]), ALU.add))
            dv.alone(vec_mark)
            dv(nc.vector.max(sc16[:, par, 0:8], cand))
            dv.alone(vec_mark)
            dv(nc.vector.max_index(j16[:, 0:8], sc16[:, par, 0:8], cand))
            dv.alone(vec_mark)
            dv(nc.vector.match_replace(candw, sc16[:, par, 0:8], cand, NEG))
            dv.alone(vec_mark)
            dv(nc.vector.max(sc16[:, par, 8:16], candw))
            dv.alone(vec_mark)
            dv(nc.vector.max_index(j16[:, 8:16], sc16[:, par, 8:16], candw))
            nc.vector.tensor_scalar(nb[:, par:par + 1], sc16[:, par, 0:1], -1.0, None, ALU.mult).then_inc(top_ready, 1)
            dv(nc.vector.tensor_scalar(ab16[:, 0:16], j16, 4, None, ALU.logical_shift_right))
            dv(nc.vector.tensor_scalar(ab16[:, 16:32], j16, 15, None, ALU.bitwise_and))
            oh = onehot.rearrange("p (k i) -> p k i", k=32)
            dv(nc.vector.tensor_tensor(oh, ab16.unsqueeze(2).to_broadcast([P, 32, TOPK]),
                                       k("iota").unsqueeze(1).to_broadcast([P, 32, TOPK]), ALU.is_equal))
            for half in range(2):
                o = half * TOPK
                dv(nc.vector.tensor_tensor(oh[:, o:o + 16, :], oh[:, o:o + 16, :],
                                           i16[:, o:o + 16].unsqueeze(1).to_broadcast([P, TOPK, TOPK]), ALU.mult))
            dv(nc.vector.tensor_reduce(sel, oh, AX.X, ALU.add))
            nc.vector.scalar_tensor_tensor(out=idx[:, par, :], in0=sel[:, 0:16], scalar=float(NK), in1=sel[:, 16:32],
                                           op0=ALU.mult, op1=ALU.add).then_inc(idx_ready, 1)

        def tile_of(s, par, i, t0, back=0):
            if isinstance(s, int):
                return t0 + (s - back) // HEADS
            return (i - 1) // 4 + t0 if (back and par == 0) else i // 4 + t0

        def dve_peer(dv, l):
            t0 = peer_tiles(l)[0]

            def yacc(s, gs, par, t):
                nc.vector.wait_ge(v_read, gs * 16 + 16)
                nc.vector.wait_ge(y_free, gs * 2) if not (isinstance(gs, int) and gs == 0) else None
                for half in range(2):
                    dst = Yf[:, bass.ds(t * D + half * 512, 512)]
                    nc.vector.tensor_tensor(dst, dst, ybank[par][half][:, :], ALU.add).then_inc(y_free, 1)

            def residual(tiles):
                for t in tiles:
                    s = 0 if t < CTX_TILES else 1
                    dv(nc.vector.tensor_tensor(Y[:, t, :], Y[:, t, :], bc[:, 3, s, :], ALU.mult))
                    ins = nc.vector.tensor_tensor(R[:, t, :], R[:, t, :], Y[:, t, :], ALU.add)
                    dv(ins) if t < NT - 1 else r_ready.give(ins)

            def body(s, gs, par, i, first, n):
                if isinstance(s, int) and s == n - 2:
                    nc.vector.wait_ge(y_free, gs * 2 - 2)
                    residual(range(t0, NT - 1))
                t = tile_of(s, par, i, t0)
                for kk in range(TOPK):
                    nc.vector.wait_ge(u_land[kk % RING], gs * 32 + 16 * (kk // RING + 1))
                    nc.vector.scalar_tensor_tensor(out=uring[:, kk % RING, :], in0=uring[:, kk % RING, :], scalar=1.0,
                                                   in1=htf[:, bass.ds(t * D, D)], op0=ALU.mult, op1=ALU.mult,
                                                   accum_out=act16[:, par, kk:kk + 1]).then_inc(u_read, 1)
                if first and par == 0:
                    dve_route(dv, s, gs + 1, 1 - par)
                nc.vector.wait_ge(exp_done, gs + 1)
                dv(nc.vector.reciprocal(zs[:, 2 + par:3 + par], zs[:, par:par + 1]))
                nc.vector.wait_ge(gelu_done, gs + 1)
                nc.vector.scalar_tensor_tensor(out=w16[:, par, :], in0=gel16[:, par, :], scalar=zs[:, 2 + par:3 + par],
                                               in1=e16[:, par, :], op0=ALU.mult, op1=ALU.mult).then_inc(w_ready, 1)
                if first and par == 1:
                    nc.vector.wait_ge(pa.full, mark[f"q{l}"])
                    y_zero.give(nc.vector.memset(Yf, 0.0))
                    nc.vector.wait_ge(y_zero.sem, y_zero.made)
                if not (first and par == 0):
                    yacc(None, gs - 1, 1 - par, tile_of(s, par, i, t0, 1))
                if not (first and par == 0) and not (isinstance(s, int) and s == n - 1):
                    dve_route(dv, s, gs + 1, 1 - par)
                if isinstance(s, int) and s == n - 1:
                    yacc(None, gs, par, tile_of(s, par, i, t0))

            base = 0 if l == 0 else NT * HEADS
            dve_route(dv, 0, base, 0)
            steps(nc.vector, l, body, dv)
            end = base + len(peer_tiles(l)) * HEADS
            nc.vector.wait_ge(y_free, 2 * end)
            residual((NT - 1,))
            nc.vector.wait_ge(r_ready.sem, r_ready.made)

        def act_peer(l):
            base = 0 if l == 0 else NT * HEADS

            def softmax(gs, par):
                nc.scalar.wait_ge(top_ready, gs + 1)
                nc.scalar.activation(e16[:, par, :], sc16[:, par, :], ACT.Exp, bias=nb[:, par:par + 1],
                                     accum_out=zs[:, par:par + 1]).then_inc(exp_done, 1)

            def body(s, gs, par, i, first, n):
                last = isinstance(s, int) and s == n - 1
                if not last and not (first and par == 0):
                    stage(s + 1, gs + 1, 1 - par)
                nc.scalar.wait_ge(u_read, gs * 16 + 16)
                nc.scalar.activation(gel16[:, par, :], act16[:, par, :], ACT.Gelu).then_inc(gelu_done, 1)
                nc.scalar.wait_ge(w_ready, gs + 1)
                for kk in range(TOPK):
                    if not (isinstance(gs, int) and gs * 16 + kk < 4):
                        nc.scalar.wait_ge(v_read, gs * 16 + (kk - 3))
                    nc.scalar.activation(diag[:, kk % 4, :], ident, ACT.Copy, scale=w16[:, par, kk:kk + 1]).then_inc(diag_done, 1)
                if not last:
                    softmax(gs + 1, 1 - par)

            softmax(base, 0)
            steps(nc.scalar, l, body)

        def pe_peer(l):
            base = 0 if l == 0 else NT * HEADS

            def body(s, gs, par, i, first, n):
                if not (first and par == 0) and not (isinstance(s, int) and s == n - 1):
                    keyscores(l, gs + 1, 1 - par)
                if not (isinstance(gs, int) and gs < 2):
                    nc.tensor.wait_ge(y_free, gs * 2 - 2)
                for kk in range(TOPK):
                    nc.tensor.wait_ge(v_land[kk % RING], gs * 32 + 16 * (kk // RING + 1))
                    nc.tensor.wait_ge(diag_done, gs * 16 + (kk + 1))
                    for half in range(2):
                        ins = nc.tensor.matmul(ybank[par][half][:, :], diag[:, kk % 4, :],
                                               vring[:, kk % RING, half * 512:(half + 1) * 512],
                                               start=(kk == 0), stop=(kk == TOPK - 1))
                    ins.then_inc(v_read, 1)

            steps(nc.tensor, l, body)
            nc.tensor.wait_ge(y_free, 2 * (base + len(peer_tiles(l)) * HEADS))
        NG, CH, CONV, XW = 4, 64, 5, 256
        g = Region(scr)
        ktok = g.get(NT * D).rearrange("p (t d) -> p t d", t=NT)
        vtok = g.get(NT * D).rearrange("p (t d) -> p t d", t=NT)
        qtok = g.get(2 * D).rearrange("p (t d) -> p t d", t=2)
        zgs = g.get(2 * D).rearrange("p (t d) -> p t d", t=2)
        kTg = g.get(2 * TOK).rearrange("p (h t) -> p h t", h=2)
        qTg = g.get(2 * XW).rearrange("p (h t) -> p h t", h=2)
        vns = [g.get(512).rearrange("p (u c) -> p u c", u=4)]
        g2, g3 = Region(htok.rearrange("p t d -> p (t d)")), Region(wbuf[:, 0].rearrange("p k c -> p (k c)"))
        ug, wTg, ATg, qdTg = [], [], [], []
        for r1, r2, r3 in ((g, g, g2), (g2, g3, g3)):
            ug.append(r1.get(NT * 512).rearrange("p (t u c) -> p t u c", t=NT, u=4))
            wTg.append(r2.get(NT * 512).rearrange("p (t u c) -> p t u c", t=NT, u=4))
            ATg.append(r3.get(2 * 512).rearrange("p (t u c) -> p t u c", t=2, u=4))
            qdTg.append(r3.get(2 * 512).rearrange("p (t u c) -> p t u c", t=2, u=4))
        g = Region(bcx)
        cpad = g.get(2 * 2 * (XW + CONV - 1)).rearrange("p (r s c) -> p r s c", r=2, s=2)
        cout = g.get(2 * TOK).rearrange("p (r c) -> p r c", r=2)
        csil = g.get(2 * TOK).rearrange("p (r c) -> p r c", r=2)
        g = Region(bcx)
        Xm, XTm, LTm, Pm = (g.get(1024).rearrange("p (r u c) -> p r u c", r=2, u=4) for _ in range(4))
        g = Region(hT.rearrange("p k t -> p (k t)"))
        S = g.get(512).rearrange("p (u c) -> p u c", u=4)
        vn = g.get(512).rearrange("p (u c) -> p u c", u=4)
        dec, CTm = (g.get(1024).rearrange("p (r u c) -> p r u c", r=2, u=4) for _ in range(2))
        dgc = g.get(1024).rearrange("p (r u c) -> p r u c", r=2, u=4)
        g = Region(wbuf[:, 1].rearrange("p k c -> p (k c)"))
        vb0, kb0, Lm, qem = (g.get(1024).rearrange("p (r u c) -> p r u c", r=2, u=4) for _ in range(4))
        g = Region(R[:, 0:CTX_TILES, :].rearrange("p t d -> p (t d)"))
        vb1, kb1 = (g.get(1024).rearrange("p (r u c) -> p r u c", r=2, u=4) for _ in range(2))
        vbm, kbm = (vb0, vb1), (kb0, kb1)
        Am = CTm
        LCm = Pm
        Xcm, XTom = Lm, dgc
        XTu = (dec, dgc)
        sqb = wTg[0].rearrange("p t u c -> p (t u c)")
        g = Region(bc[:, 0, 0, :])
        abt = g.get(128).rearrange("p (t c) -> p t c", t=NT)
        ga, gm, gn, gg, beta, eg, ed, bek = (g.get(64) for _ in range(8))
        gct = g.get(256)
        g = Region(bc[:, 3, 0, :])
        glb = g.get(128)
        ealog = g.get(16)
        vns.append(g.get(512).rearrange("p (u c) -> p u c", u=4))

        pad_ready = Signal(sem("conv_padding_ready"))
        conv_ready, csil_ready = Signal(sem("conv_ready")), Signal(sem("conv_silu_ready"))
        gate_in, gate_out = Signal(sem("gate_in")), Signal(sem("gate_exp"))
        g_ready = Signal(sem("log_decay_ready"))
        norm_ready = Signal(sem("qk_normed"))
        operand_ready = Signal(sem("dn_operand_ready"))
        block_ready, rhs_ready = Signal(sem("dn_level_block_ready")), Signal(sem("dn_rhs_ready"))
        level_ready, turned_ready = Signal(sem("dn_level_ready")), Signal(sem("dn_level_turned_ready"))
        dec_in, dec_exp = Signal(sem("decay_in")), Signal(sem("decay_exp"))
        vn_ready = Signal(sem("vnew_ready"))
        DT = [(0, 1), (2, 3)]

        def dth(v):
            return v.rearrange("p (d t h) -> p d t h", d=2, t=NT)

        def unit_scalars(v, gp, t):
            s = dth(v)[:, :, t, 2 * gp:2 * gp + 2].rearrange("p d h -> p h d")
            return s.unsqueeze(3).to_broadcast([P, 2, 2, P])

        def u4(v):
            return v.rearrange("p (h d) c -> p h d c", h=2)

        def over_dirs(v):
            return v.unsqueeze(2).to_broadcast([P, 2, 2, P])

        def over_heads(v):
            return v.unsqueeze(1).to_broadcast([P, 2, 2, P])

        incl = k("incl").rearrange("p (d c) -> p d c", d=3)
        strict = k("strict").rearrange("p (d c) -> p d c", d=2)
        lvl = k("lvl").rearrange("p (l d c) -> p l d c", l=len(LEVELS), d=2)
        identu = ident.unsqueeze(1).to_broadcast([P, 4, P])

        def pe_dn_project():
            def log_decay_sums():
                g_ready.take(nc.tensor)
                b = pv.open(nc.tensor)
                gd = dth(gg).rearrange("p d t h -> p d (t h)")
                for d, m in ((0, k("incl")[:, P:2 * P]), (1, k("incl")[:, 0:P])):
                    nc.tensor.matmul(b[:, d * 32:(d + 1) * 32], m, gd[:, d], start=True, stop=True)
                    nc.tensor.matmul(b[:, 64 + d * 32:96 + d * 32], k("blk"), gd[:, d], start=True, stop=True)
                for c in range(2):
                    rows_c = k("blk")[:, c * CH:c * CH + 1].to_broadcast([P, P])
                    for d in range(2):
                        o = 128 + c * 64 + d * 32
                        last = nc.tensor.matmul(b[:, o:o + 32], rows_c, gd[:, d], start=True, stop=True)
                pv.close(last)

            def turn(i):
                csil_ready.take(nc.tensor)
                b = pa.open(nc.tensor)
                for t in (XT if i < 8 else AT):
                    last = nc.tensor.transpose(b[:, t * P:(t + 1) * P], csil[:, i % 2, t * P:(t + 1) * P], ident)
                pa.close(last)

            b = pa.open(nc.tensor)
            for t in AT:
                for kk in range(KD):
                    last = nc.tensor.matmul(b[:, t * 32:(t + 1) * 32], hT[:, kk, t * P:(t + 1) * P], wab[:, kk, :],
                                            start=(kk == 0), stop=(kk == KD - 1))
            pa.close(last)
            for i in range(26):
                if i == 9:
                    log_decay_sums()
                if i < 24:
                    w, cb = W_DNIN + i // 4, i % 4
                    if cb == 0:
                        nc.tensor.wait_ge(w_ld[w % 2], 16 * (w // 2 + 1))
                    a = XW if i < 8 else 0
                    b = pa.open(nc.tensor)
                    for kk in range(KD):
                        last = nc.tensor.matmul(b[:, a:TOK], wbuf[:, w % 2, kk, cb * P:(cb + 1) * P], hT[:, kk, a:TOK],
                                                start=(kk == 0), stop=(kk == KD - 1))
                    pa.close(last)
                    if cb == 3:
                        used_chunk(w, pa)
                if i >= 2:
                    turn(i - 2)
            pe_lin(W_DNIN + 6, (512, 512), hT, XT, pa)
            mark["dn_hT"] = pa.closed

        def act_dn_project(ac):
            def silu(i):
                conv_ready.take(nc.scalar)
                a = XW if i < 8 else 0
                csil_ready.give(nc.scalar.activation(csil[:, i % 2, a:TOK], cout[:, i % 2, a:TOK], ACT.Silu))

            def turned(i):
                b = pa.take(nc.scalar)
                o = (i % 8) * P
                dst, a, n = ((qtok, XW, 2), (ktok, 0, NT), (vtok, 0, NT))[i // 8]
                pa.release(nc.scalar.activation(dst[:, 0:n, o:o + P], b[:, a:TOK].rearrange("p (t c) -> p t c", t=n), ACT.Copy))

            b = pa.take(nc.scalar)
            pa.release(nc.scalar.activation(abt, b[:, 0:128].rearrange("p (t c) -> p t c", t=NT), ACT.Copy))
            mark["ab"] = pa.left
            pad_ready.take(nc.scalar)
            for i in range(26):
                if i == 0:
                    gate_in.take(nc.scalar)
                    ac(nc.scalar.activation(gn, gn, ACT.Exp))
                    ac(nc.scalar.activation(beta, beta, ACT.Exp))
                    gate_out.give(nc.scalar.activation(ealog, sm("alog"), ACT.Exp))
                elif i == 4:
                    gate_in.take(nc.scalar)
                    gate_out.give(nc.scalar.activation(gn, gn, ACT.Ln))
                elif i == 14:
                    gate_in.take(nc.scalar)
                    ac(nc.scalar.activation(eg, gct[:, 0:64], ACT.Exp))
                    ac(nc.scalar.activation(ed, ed, ACT.Exp))
                    gate_out.give(nc.scalar.activation(glb, gct[:, 128:256], ACT.Exp))
                elif i == 24:
                    act_sqrt(48)
                if i < 24:
                    b = pa.take(nc.scalar)
                    s = 1 if i < 8 else 0
                    pa.release(nc.scalar.activation(cpad[:, i % 2, s:2, 2:2 + XW],
                                                    b[:, s * XW:TOK].rearrange("p (s c) -> p s c", s=2 - s), ACT.Copy))
                    mark["cv", i] = pa.left
                if 1 <= i < 25:
                    silu(i - 1)
                if i >= 2:
                    turned(i - 2)
                    mark["turned", i - 2] = pa.left
            for c in range(2):
                for t in range(2):
                    b = pa.take(nc.scalar)
                    pa.release(nc.scalar.activation(zgs[:, t, c * 512:(c + 1) * 512], b[:, :], ACT.Silu))
            mark["zg"] = pa.left

        def dve_dn_project(dv):
            rows = [(ktok, t) for t in range(NT)] + [(qtok, t) for t in range(2)]

            def conv(i):
                nc.vector.wait_ge(pa.free, mark["cv", i])
                s = 1 if i < 8 else 0
                o = cout[:, i % 2, s * XW:TOK].rearrange("p (s c) -> p s c", s=2 - s)
                for j in range(CONV):
                    v = cpad[:, i % 2, s:2, j:j + XW]
                    if j == 0:
                        dv(nc.vector.tensor_scalar(o, v, convw[:, i, 0:1], None, ALU.mult))
                    else:
                        ins = nc.vector.scalar_tensor_tensor(out=o, in0=v, scalar=convw[:, i, j:j + 1], in1=o,
                                                             op0=ALU.mult, op1=ALU.add)
                        conv_ready.give(ins) if j == CONV - 1 else dv(ins)

            def gates(step):
                if step == 0:
                    nc.vector.wait_ge(pa.free, mark["ab"])
                    a_in = abt[:, :, 0:16].rearrange("p t (d h) -> p t d h", d=2)
                    b_in = abt[:, :, 16:32].rearrange("p t (d h) -> p t d h", d=2)
                    tdh = lambda v: dth(v).rearrange("p d t h -> p t d h")
                    dtb = sm("dtb").rearrange("p (d h) -> p d h", d=2).unsqueeze(1).to_broadcast([P, NT, 2, 8])
                    dv(nc.vector.tensor_tensor(tdh(ga), a_in, dtb, ALU.add))
                    dv(nc.vector.tensor_scalar(gn, ga, -1.0, None, ALU.mult))
                    dv(nc.vector.tensor_tensor(gn, gn, ga, ALU.min))
                    dv(nc.vector.tensor_scalar(gm, ga, 0.0, None, ALU.max))
                    gate_in.give(nc.vector.tensor_scalar(tdh(beta), b_in, -1.0, None, ALU.mult))
                elif step == 1:
                    gate_out.take(nc.vector)
                    dv(nc.vector.tensor_scalar_add(beta, beta, 1.0))
                    dv(nc.vector.reciprocal(beta, beta))
                    gate_in.give(nc.vector.tensor_scalar_add(gn, gn, 1.0))
                elif step == 2:
                    gate_out.take(nc.vector)
                    dv(nc.vector.tensor_tensor(gm, gm, gn, ALU.add))
                    ea = ealog.rearrange("p (d h) -> p d h", d=2).unsqueeze(2).to_broadcast([P, 2, NT, 8])
                    g_ready.give(nc.vector.tensor_tensor(dth(gg), dth(gm), ea, ALU.mult))
                elif step == 3:
                    b = pv.take(nc.vector)
                    pv.release(nc.vector.tensor_scalar(gct, b[:, 0:256], -1.0, None, ALU.mult))
                    nc.vector.wait_ge(pv.free, pv.left)
                    gate_in.give(nc.vector.tensor_tensor(ed, gct[:, 64:128], gct[:, 0:64], ALU.subtract))
                else:
                    gate_out.take(nc.vector)
                    dv(nc.vector.tensor_tensor(bek, beta, eg, ALU.mult))

            def squares(n):
                v, t = rows[n]
                dv(nc.vector.tensor_tensor(sqb[:, 0:D], v[:, t, :], v[:, t, :], ALU.mult))
                dv(nc.vector.tensor_reduce(stat[:, 0, n * 8:n * 8 + 8], sqb[:, 0:D].rearrange("p (h c) -> p h c", h=8), AX.X, ALU.add))

            pad_ready.give(nc.vector.memset(cpad, 0.0))
            step_before = {0: 0, 2: 1, 6: 2, 11: 3, 16: 4}
            for i in range(24):
                if i in step_before:
                    gates(step_before[i])
                if i == 19:
                    nc.vector.wait_ge(pa.free, mark["turned", 15])
                if 19 <= i < 22:
                    squares(2 * (i - 19))
                    squares(2 * (i - 19) + 1)
                if i == 22:
                    var_ready.give(nc.vector.tensor_scalar(stat[:, 1, 0:48], stat[:, 0, 0:48], EPS, None, ALU.add))
                conv(i)
            dve_rstd(dv, 48)
            dv(nc.vector.tensor_scalar(stat[:, 2, 32:48], stat[:, 2, 32:48], float(P) ** -0.5, None, ALU.mult))
            for n, (v, t) in enumerate(rows):
                w = v[:, t, :].rearrange("p (h c) -> p h c", h=8)
                ins = nc.vector.tensor_tensor(w, w, stat[:, 2, n * 8:n * 8 + 8].unsqueeze(2).to_broadcast([P, 8, P]), ALU.mult)
                norm_ready.give(ins) if n == len(rows) - 1 else dv(ins)
            nc.vector.wait_ge(norm_ready.sem, norm_ready.made)
            nc.vector.wait_ge(pa.full, mark["dn_hT"])
            nc.vector.wait_ge(pa.free, mark["turned", 23])
            dv(nc.vector.memset(vn, 0.0))
            dv(nc.vector.memset(vns[0], 0.0))
            dv(nc.vector.memset(vns[1], 0.0))

        def pe_dn_inverse(gp):
            for hh in range(2):
                b = pa.open(nc.tensor)
                for t in AT:
                    o = (2 * gp + hh) * P
                    last = nc.tensor.transpose(b[:, t * P:(t + 1) * P], ktok[:, t, o:o + P], ident)
                pa.close(last)
            b = pa.open(nc.tensor)
            for hh in range(2):
                for t in range(2):
                    o = (2 * gp + hh) * P
                    last = nc.tensor.transpose(b[:, (hh * 2 + t) * P:(hh * 2 + t + 1) * P], qtok[:, t, o:o + P], ident)
            pa.close(last)
            pa.drain(nc.tensor)
            for i, pair in enumerate(DT):
                x_pair = pair[0] >= CTX_TILES
                for r, t in enumerate(pair):
                    tt = slice(t * P, (t + 1) * P)
                    b = pv.open(nc.tensor)
                    operand_ready.take(nc.tensor)
                    pv.close(nc.tensor.matmul(b[:, :], ones, dgc[:, r].rearrange("p u c -> p (u c)"), start=True, stop=True))
                    b = ps.open(nc.tensor)
                    for hh in range(2):
                        last = nc.tensor.matmul(b[:, hh * P:(hh + 1) * P], kTg[:, hh, tt], kTg[:, hh, tt], start=True, stop=True)
                        if x_pair:
                            a = (t - CTX_TILES) * P
                            last = nc.tensor.matmul(b[:, 256 + hh * P:256 + (hh + 1) * P], qTg[:, hh, a:a + P], kTg[:, hh, tt],
                                                    start=True, stop=True)
                    ps.close(last)
                yield
                b = pa.open(nc.tensor)
                operand_ready.take(nc.tensor)
                for v in range(4):
                    last = nc.tensor.transpose(b[:, v * P:(v + 1) * P], LCm[:, i, v, :], ident)
                pa.close(last)
                if x_pair:
                    for r in range(2):
                        b = pa.open(nc.tensor)
                        for u in range(4):
                            last = nc.tensor.transpose(b[:, u * P:(u + 1) * P], Am[:, r, u, :], ident)
                        pa.close(last)
                yield

            def reach(i, li):
                level_ready.take(nc.tensor)
                block_ready.take(nc.tensor)
                b = pa.open(nc.tensor)
                for v in range(4):
                    last = nc.tensor.matmul(b[:, v * P:(v + 1) * P], CTm[:, i, v, :], Xcm[:, i, v, :], start=True, stop=True)
                pa.close(last)
                level_job[i] = pa.opened
                mark["reach", gp, i, li] = pa.closed

            def correct(i, li):
                turned_ready.take(nc.tensor)
                nc.tensor.wait_ge(pa.free, level_job[i])
                if li < len(LEVELS) - 1:
                    b = ps.open(nc.tensor)
                    for v in range(4):
                        last = nc.tensor.matmul(b[:, v * P:(v + 1) * P], XTom[:, i, v, :], Pm[:, i, v, :], start=True, stop=True)
                    ps.close(last)
                b = pv.open(nc.tensor)
                for v in range(4):
                    last = nc.tensor.matmul(b[:, v * P:(v + 1) * P], Pm[:, i, v, :], XTom[:, i, v, :], start=True, stop=True)
                pv.close(last)

            for li in range(1, len(LEVELS)):
                reach(0, li)
                if li > 1:
                    correct(1, li - 1)
                yield
                correct(0, li)
                reach(1, li)
                yield
            correct(1, len(LEVELS) - 1)
            for i, pair in enumerate(DT):
                x_pair = pair[0] >= CTX_TILES
                for r, t in enumerate(pair):
                    b = pa.open(nc.tensor)
                    operand_ready.take(nc.tensor)
                    rhs_ready.take(nc.tensor)
                    for u in range(4):
                        last = nc.tensor.matmul(b[:, u * P:(u + 1) * P], XTu[i][:, r, u, :], vbm[i][:, r, u, :], start=True, stop=True)
                    pa.close(last)
                    b = pa.open(nc.tensor)
                    for u in range(4):
                        last = nc.tensor.matmul(b[:, u * P:(u + 1) * P], kbm[i][:, r, u, :], XTu[i][:, r, u, :], start=True, stop=True)
                    pa.close(last)
                    if x_pair:
                        b = pa.open(nc.tensor)
                        for u in range(4):
                            last = nc.tensor.transpose(b[:, u * P:(u + 1) * P], qem[:, r, u, :], ident)
                        pa.close(last)
                mark["rhs_read", gp, i] = pa.closed
                mark["rhs", gp] = pa.opened
                yield

        def pe_dn_scan(gp):
            s2 = gp % 2
            nc.tensor.wait_ge(pa.free, mark["rhs", gp])
            for n in range(8):
                b = pv.open(nc.tensor)
                if n == 0:
                    operand_ready.take(nc.tensor)
                else:
                    nc.tensor.wait_ge(ps.free, state_job)
                for u in range(4):
                    t, c = chunk_of(n, u % 2)
                    r = slice(c * CH, (c + 1) * CH)
                    last = nc.tensor.matmul(b[r, u * P:(u + 1) * P], wTg[s2][:, t, u, r], S[:, u, :], start=True, stop=True)
                pv.close(last)
                yield
                if n >= 4:
                    b = po.open(nc.tensor)
                    vn_ready.take(nc.tensor)
                    for u in range(4):
                        t, c = chunk_of(n, u % 2)
                        r = slice(c * CH, (c + 1) * CH)
                        nc.tensor.matmul(b[r, u * P:(u + 1) * P], qdTg[s2][:, t - CTX_TILES, u, r], S[:, u, :], start=True, stop=False)
                        last = nc.tensor.matmul(b[r, u * P:(u + 1) * P], ATg[s2][:, t - CTX_TILES, u, r], vn[:, u, :],
                                                start=False, stop=True)
                    po.close(last)
                else:
                    vn_ready.take(nc.tensor)
                b = ps.open(nc.tensor)
                for u in range(4):
                    t, c = chunk_of(n, u % 2)
                    o = (2 * gp + u // 2) * P
                    last = nc.tensor.matmul(b[:, u * P:(u + 1) * P], ktok[:, t, o:o + P], vns[n % 2][:, u, :], start=True, stop=True)
                ps.close(last)
                state_job = ps.opened
                yield

        def beside(first, second):
            for _ in range(16):
                next(first)
                next(second)

        def dn_groups(inverse, scan):
            for _ in inverse(0):
                pass
            for gp in range(NG - 1):
                beside(inverse(gp + 1), scan(gp))
            for _ in scan(NG - 1):
                pass

        level_job = [0, 0]

        def chunk_of(n, d):
            c = n if d == 0 else (3 - n if n < 4 else 11 - n)
            return c // 2, c % 2

        def act_dn_inverse(gp):
            s2 = gp % 2

            def copy4(dst):
                b = pa.take(nc.scalar)
                pa.release(nc.scalar.activation(dst, b[:, :].rearrange("p (u c) -> p u c", u=4), ACT.Copy))

            for hh in range(2):
                b = pa.take(nc.scalar)
                pa.release(nc.scalar.activation(kTg[:, hh, :], b[:, :], ACT.Copy))
            b = pa.take(nc.scalar)
            pa.release(nc.scalar.activation(qTg, b[:, :].rearrange("p (h t) -> p h t", h=2), ACT.Copy))
            for i, pair in enumerate(DT):
                x_pair = pair[0] >= CTX_TILES
                for r, t in enumerate(pair):
                    dec_in.take(nc.scalar)
                    dec_exp.give(nc.scalar.activation(dec[:, r], dec[:, r], ACT.Exp, scale=-1.0))
                yield
                copy4(LTm[:, i])
                mark["lt", gp, i] = pa.left
                if x_pair:
                    for r in range(2):
                        copy4(ATg[s2][:, r])
                    mark["at", gp] = pa.left
                yield
            for half in range(2 * (len(LEVELS) - 1)):
                copy4(Pm[:, half % 2])
                yield
            for i, pair in enumerate(DT):
                x_pair = pair[0] >= CTX_TILES
                for r, t in enumerate(pair):
                    copy4(ug[s2][:, t])
                    copy4(wTg[s2][:, t])
                    if x_pair:
                        copy4(qdTg[s2][:, r])
                mark["pre", gp] = pa.left
                yield

        def act_dn_scan(gp):
            for n in range(16):
                yield

        def dve_dn_inverse(dv, gp):
            heads = slice(2 * gp * P, 2 * (gp + 1) * P)
            over_units = lambda m: m.unsqueeze(1).to_broadcast([P, 4, P])

            def by_direction(i, r):
                return nc.vector.tensor_tensor(u4(XTu[i][:, r]), over_dirs(XTm[:, i, 2 * r:2 * r + 2]), over_heads(incl[:, 1:3]), ALU.mult)

            if gp:
                nc.vector.wait_ge(pa.full, mark["rhs_read", gp - 1, 1])
            for i, pair in enumerate(DT):
                x_pair = pair[0] >= CTX_TILES
                for r, t in enumerate(pair):
                    operand_ready.give(nc.vector.tensor_tensor(u4(dgc[:, r]), u4(identu), unit_scalars(gct[:, 0:64], gp, t), ALU.mult))
                for r, t in enumerate(pair):
                    b = pv.take(nc.vector)
                    pv.release(nc.vector.tensor_tensor(u4(dec[:, r]), b[:, :].rearrange("p (h d c) -> p h d c", h=2, d=2),
                                                       unit_scalars(gct[:, 0:64], gp, t), ALU.subtract))
                    nc.vector.wait_ge(pv.free, pv.left)
                    dec_in.give(nc.vector.tensor_scalar(dec[:, r], dec[:, r], 0.0, None, ALU.max))
                yield
                for r, t in enumerate(pair):
                    dec_exp.take(nc.vector)
                    b = ps.take(nc.vector)
                    ins = nc.vector.tensor_tensor(u4(Lm[:, r]), u4(dec[:, r]),
                                                  over_dirs(b[:, 0:256].rearrange("p (h c) -> p h c", h=2)), ALU.mult)
                    if x_pair:
                        ins = nc.vector.tensor_tensor(u4(Am[:, r]), u4(dec[:, r]),
                                                      over_dirs(b[:, 256:512].rearrange("p (h c) -> p h c", h=2)), ALU.mult)
                    ps.release(ins)
                for r, t in enumerate(pair):
                    nc.vector.wait_ge(ps.free, ps.left - 1 + r)
                    ins = nc.vector.tensor_tensor(u4(Lm[:, r]), u4(Lm[:, r]), unit_scalars(beta, gp, t), ALU.mult)
                dv(ins)
                for r in range(2):
                    ins = nc.vector.tensor_tensor(u4(Lm[:, r]), u4(Lm[:, r]), over_heads(strict), ALU.mult)
                    if x_pair:
                        ins = nc.vector.tensor_tensor(u4(Am[:, r]), u4(Am[:, r]), over_heads(incl[:, 0:2]), ALU.mult)
                dv(ins)
                lo, up = (Lm.rearrange("p a (h d) c -> p a h d c", h=2)[:, :, :, d, :] for d in range(2))
                operand_ready.give(nc.vector.tensor_tensor(LCm[:, i].rearrange("p (a h) c -> p a h c", a=2), lo, up, ALU.add))
                nc.vector.wait_ge(operand_ready.sem, operand_ready.made)
                dv(nc.vector.tensor_tensor(Xm[:, i], LCm[:, i], over_units(lvl[:, 0, 0]), ALU.mult))
                dv(nc.vector.tensor_tensor(Xm[:, i], identu, Xm[:, i], ALU.subtract))
                nc.vector.wait_ge(pa.free, mark["lt", gp, i])
                dv(nc.vector.tensor_tensor(XTm[:, i], LTm[:, i], over_units(lvl[:, 0, 0]), ALU.mult))
                dv(nc.vector.tensor_tensor(XTm[:, i], identu, XTm[:, i], ALU.subtract))
                if i == 1:
                    for j in range(2):
                        dve_level_operands(j, 1)
                yield
            for li in range(1, len(LEVELS)):
                if li > 1:
                    dve_level_result(1, li - 1)
                    dve_level_operands(1, li)
                yield
                dve_level_result(0, li)
                if li < len(LEVELS) - 1:
                    dve_level_operands(0, li + 1)
                yield
            for i, pair in enumerate(DT):
                if i == 0:
                    for r in range(2):
                        operand_ready.give(by_direction(0, r))
                    dve_level_result(1, len(LEVELS) - 1)
                else:
                    for r in range(2):
                        operand_ready.give(by_direction(1, r))
                yield

        def dve_level_operands(i, li):
            mask = lvl[:, li, 1].unsqueeze(1).to_broadcast([P, 4, P])
            level_ready.give(nc.vector.tensor_tensor(Xcm[:, i], Xm[:, i], mask, ALU.mult))
            turned_ready.give(nc.vector.tensor_tensor(XTom[:, i], XTm[:, i], mask, ALU.mult))

        def pool_dn():
            nc.gpsimd.wait_ge(norm_ready.sem, norm_ready.made)
            for gp in range(NG):
                heads = slice(2 * gp * P, 2 * (gp + 1) * P)
                for li in range(1, len(LEVELS)):
                    for i in range(2):
                        if li == 1:
                            nc.gpsimd.wait_ge(pa.free, mark["at", gp])
                        else:
                            nc.gpsimd.wait_ge(pa.full, mark["reach", gp, i, li - 1])
                        block_ready.give(nc.gpsimd.tensor_tensor(CTm[:, i], LTm[:, i],
                                                                 lvl[:, li, 0].unsqueeze(1).to_broadcast([P, 4, P]), ALU.mult))
                    if li < len(LEVELS) - 1:
                        t = li - 1
                        i, r = t // 2, t % 2
                        if gp and r == 0:
                            nc.gpsimd.wait_ge(pa.full, mark["rhs_read", gp - 1, i])
                        kh = over_dirs(ktok[:, t, heads].rearrange("p (h c) -> p h c", h=2))
                        vh = over_dirs(vtok[:, t, heads].rearrange("p (h c) -> p h c", h=2))
                        nc.gpsimd.tensor_tensor(u4(vbm[i][:, r]), vh, unit_scalars(beta, gp, t), ALU.mult)
                        if t >= CTX_TILES:
                            qh = over_dirs(qtok[:, t - CTX_TILES, heads].rearrange("p (h c) -> p h c", h=2))
                            nc.gpsimd.tensor_tensor(u4(qem[:, r]), qh, unit_scalars(eg, gp, t), ALU.mult)
                        rhs_ready.give(nc.gpsimd.tensor_tensor(u4(kbm[i][:, r]), kh, unit_scalars(bek, gp, t), ALU.mult))

        def dve_level_result(i, li):
            if li < len(LEVELS) - 1:
                b = ps.take(nc.vector)
                ps.release(nc.vector.tensor_tensor(Xm[:, i], Xm[:, i], b[:, :].rearrange("p (u c) -> p u c", u=4), ALU.subtract))
            b = pv.take(nc.vector)
            pv.release(nc.vector.tensor_tensor(XTm[:, i], XTm[:, i], b[:, :].rearrange("p (u c) -> p u c", u=4), ALU.subtract))
            nc.vector.wait_ge(pv.free, pv.left)

        def dve_dn_scan(dv, gp):
            s2 = gp % 2
            heads = slice(2 * gp * P, 2 * (gp + 1) * P)
            nc.vector.wait_ge(pa.free, mark["pre", gp])
            operand_ready.give(nc.vector.memset(S, 0.0))
            nc.vector.wait_ge(operand_ready.sem, operand_ready.made)
            for n in range(8):
                b = pv.take(nc.vector)
                for d in range(2):
                    t, c = chunk_of(n, d)
                    r = slice(c * CH, (c + 1) * CH)
                    by_dir = lambda v: v.rearrange("p (h d) c -> p h d c", h=2)[r, :, d, :]
                    ins = nc.vector.tensor_tensor(by_dir(vn), by_dir(ug[s2][:, t]),
                                                  by_dir(b[:, :].rearrange("p (u c) -> p u c", u=4)), ALU.subtract)
                pv.release(ins)
                nc.vector.wait_ge(pv.free, pv.left)
                for d in range(2):
                    t, c = chunk_of(n, d)
                    r = slice(c * CH, (c + 1) * CH)
                    by_dir = lambda v: v.rearrange("p (h d) c -> p h d c", h=2)[r, :, d, :]
                    last_decay = dth(ed)[r, d, t, 2 * gp:2 * gp + 2].unsqueeze(2).to_broadcast([CH, 2, P])
                    ins = nc.vector.tensor_tensor(by_dir(vns[n % 2]), by_dir(vn), last_decay, ALU.mult)
                vn_ready.give(ins)
                yield
                b = ps.take(nc.vector)
                for u in range(4):
                    t, c = chunk_of(n, u % 2)
                    o = (c * 2 + u % 2) * 32 + t * 8 + 2 * gp + u // 2
                    ins = nc.vector.scalar_tensor_tensor(out=S[:, u, :], in0=S[:, u, :], scalar=glb[:, o:o + 1],
                                                         in1=b[:, u * P:(u + 1) * P], op0=ALU.mult, op1=ALU.add)
                ps.release(ins)
                nc.vector.wait_ge(ps.free, ps.left)
                if n >= 4:
                    b = po.take(nc.vector)
                    for d in range(2):
                        t, c = chunk_of(n, d)
                        r = slice(c * CH, (c + 1) * CH)
                        dst = qtok[r, t - CTX_TILES, heads].rearrange("p (h c) -> p h c", h=2)
                        src = b[r, :].rearrange("p (h d c) -> p h d c", h=2, d=2)[:, :, d, :]
                        if n < 6:
                            ins = nc.vector.tensor_copy(dst, src)
                        else:
                            ins = nc.vector.tensor_tensor(dst, dst, src, ALU.add)
                    po.release(ins)
                    nc.vector.wait_ge(po.free, po.left)
                yield

        def dve_dn_out(dv):
            nc.vector.wait_ge(pa.free, mark["zg"])
            for t in range(2):
                dv(nc.vector.tensor_tensor(sqb[:, 0:D], qtok[:, t, :], qtok[:, t, :], ALU.mult))
                dv(nc.vector.tensor_reduce(stat[:, 0, t * 8:t * 8 + 8], sqb[:, 0:D].rearrange("p (h c) -> p h c", h=8), AX.X, ALU.add))
            var_ready.give(nc.vector.tensor_scalar(stat[:, 1, 0:16], stat[:, 0, 0:16], 1.0 / P, EPS, ALU.mult, ALU.add))
            dve_rstd(dv, 16)
            for t in range(2):
                v = qtok[:, t, :].rearrange("p (h c) -> p h c", h=8)
                dv(nc.vector.tensor_tensor(v, v, stat[:, 2, t * 8:t * 8 + 8].unsqueeze(2).to_broadcast([P, 8, P]), ALU.mult))
                dv(nc.vector.tensor_tensor(v, v, sm("onorm").unsqueeze(1).to_broadcast([P, 8, P]), ALU.mult))
                o_ready.give(nc.vector.tensor_tensor(qtok[:, t, :], qtok[:, t, :], zgs[:, t, :], ALU.mult))

        def pe_dn():
            pe_dn_project()
            norm_ready.take(nc.tensor)
            dn_groups(pe_dn_inverse, pe_dn_scan)
            mark["dn_done"] = (ps.full, ps.closed)
            for t in range(2):
                o_ready.take(nc.tensor)
                for half in range(2):
                    b = pa.open(nc.tensor)
                    for q in range(4):
                        kk = half * 4 + q
                        last = nc.tensor.transpose(b[:, q * P:(q + 1) * P], qtok[:, t, kk * P:(kk + 1) * P], ident)
                    pa.close(last)
            pa.drain(nc.tensor)

        def act_dn(ac):
            act_dn_project(ac)
            dn_groups(act_dn_inverse, act_dn_scan)
            act_sqrt(16)

        def dve_dn(dv):
            dve_dn_project(dv)
            dn_groups(lambda gp: dve_dn_inverse(dv, gp), lambda gp: dve_dn_scan(dv, gp))
            dve_dn_out(dv)

        AT = range(NT)
        block = es.enter_context(nc.Block())

        @block.tensor
        def _(pe):
            pe.wait_ge(p_ld, 16 * N_PARAM)
            for c in range(ADA_C):
                pe_ada(0, c)
            pa.drain(pe)
            pe_turn(xn, AT, xn_ready)
            pe_lin(W_EVIN, (416, 512), hT, AT, pa)
            pe_latents()
            pe_lin(W_EVIN + 2, (512, 512), hT, AT, pa)
            pe_heads()
            pe_attn()
            pe_turn(o_tok, AT, o_ready)
            pe_lin(W_EVOUT, (512, 512), oT, AT, pv)
            if stop >= 2:
                pe_turn(htok, AT, xn_ready)
                pe_query(0)
                pv.drain(pe)
                pe_peer(0)
            if stop >= 3:
                pe_turn(xn, AT, xn_ready)
                pe_dn()
                pe_lin(W_DNOUT, (512, 512), oT, XT, pv)
            if stop >= 4:
                pe_turn(htok, XT, xn_ready)
                pe_query(1)
                pv.drain(pe)
                pe_peer(1)

        @block.scalar
        def _(act):
            ac = Chain(act, act_sem)
            act_silu(ac)
            act_ada()
            act.wait_ge(ctx_ld, 32)
            act_norm(ac, 0, 0, AT)
            act_z()
            act_heads()
            act_attn()
            act_sqrt(4 * NT)
            act_turn(oT, AT)
            if stop >= 2:
                act_norm(ac, 0, 1, AT)
                act_query(0)
                act_peer(0)
            if stop >= 3:
                act_norm(ac, 1, 0, AT)
                act_dn(ac)
                act_turn(oT, XT)
            if stop >= 4:
                act_norm(ac, 1, 1, XT)
                act_query(1)
                act_peer(1)

        @block.vector
        def _(dve):
            dv = Chain(dve, dve_sem)
            dve.wait_ge(p_ld, 16 * N_PARAM)
            dve_silu(dv)
            for c in range(ADA_C):
                dve_ada(0, c)
            dve_norm(dv, 0, 0, AT)
            dve_heads(dv)
            dve_attn(dv)
            dve_residual(dv, 0, AT, tmpv[:, 0:512])
            vec_free.give(dve.tensor_copy(negs[:, 1:2], ident[:, 0:1]))
            if stop >= 2:
                dve.wait_ge(bc_ld, 16 * BC_COUNT[0, 1])
                dve_norm(dv, 0, 1, AT)
                dve_peer(dv, 0)
            if stop >= 3:
                vec_free.give(dve.tensor_copy(negs[:, 1:2], ident[:, 0:1]))
                dve_norm(dv, 1, 0, AT)
                dve_dn(dv)
                dve_residual(dv, 1, XT, junk[:, 0:512])
            if stop >= 4:
                dve.wait_ge(bc_ld, 16 * BC_COUNT[1, 1])
                dve_norm(dv, 1, 1, XT)
                dve_peer(dv, 1)

        @block.gpsimd
        def _(pool):
            pool_ada(0)
            pool_vectors(0, 0)
            pool_ada(1)
            if stop >= 2:
                pool_vectors(0, 1)
                pool_peer(0)
            if stop >= 3:
                pool_vectors(1, 0)
                pool_dn()
            if stop >= 4:
                pool_vectors(1, 1)
            if stop >= 4:
                pool_peer(1)

        @block.sync
        def _(sp):
            for dst, src in ((cs[:, 0, :], cT), (cst[:], consts), (smallp[:], small),
                             (keys[:], keysT), (convw[:], conv_w), (wab[:], w_ab)):
                sp.dma_start(dst, src).then_inc(p_ld, 16)
            for w in range(W_END if stop >= 4 else (W_WQ0, W_DNIN, W_WQ1)[stop - 1]):
                if w >= 2:
                    sp.wait_ge(*w_done[w - 2]) if w - 2 in w_done else None
                if w == 2:
                    sp.dma_start(R[:, 0:CTX_TILES, :], ctx_in[0].rearrange("(t p) d -> p t d", p=P)).then_inc(ctx_ld, 16)
                    sp.dma_start(R[:, CTX_TILES:NT, :], x[0].rearrange("(t p) d -> p t d", p=P)).then_inc(ctx_ld, 16)
                if w == W_EVIN + 2:
                    for r in range(2):
                        sp.wait_ge(row_st[r], 16 * ADA_C // 2)
                    sp.dma_start(wuq_sb, w_uq).then_inc(mla_ld, 16)
                    sp.dma_start(wukv_sb, w_ukv).then_inc(mla_ld, 16)
                if w == W_DNOUT:
                    sp.wait_ge(*mark["dn_done"])
                if w in (W_DNIN, W_DNIN + 1):
                    sp.wait_ge(v_read, NT * HEADS * TOPK)
                sp.dma_start(wbuf[:, w % 2], wstream[w]).then_inc(w_ld[w % 2], 16)
            sp.wait_ge(r_ready.sem, r_ready.made)
            if stop >= 4:
                sp.dma_start(out[0].rearrange("(t p) d -> p t d", p=P), R[:, CTX_TILES:NT, :]).then_inc(out_st, 16)
            else:
                sp.dma_start(out.rearrange("t p d -> p t d"), R[:, :, :]).then_inc(out_st, 16)
            sp.wait_ge(out_st, 16)


STOP = 9


def _shape_constants():
    import numpy as np
    c = {}
    i = np.arange(P)[:, None]
    j = np.arange(P)[None, :]
    same = (i // 64) == (j // 64)
    c["ident"] = (i == j)
    c["ones"] = np.ones((P, P))
    c["blk"] = same
    c["incl"] = np.concatenate([same & (i >= j), same & (i <= j), same & (i >= j)], 1)
    c["strict"] = np.concatenate([same & (i > j), same & (i < j)], 1)
    lv = []
    for m in LEVELS:
        f = (i // m % 2 == 1) & (j // m == i // m - 1)
        block = (i // m) == (j // m)
        lv += [f | f.T, block & np.where(i // m % 2 == 0, i >= j, i <= j)]
    c["lvl"] = np.concatenate(lv, 1)
    c["iota"] = np.broadcast_to(np.arange(16), (P, 16))
    tok = np.arange(256)
    for name, rot in (("A", 64), ("B", 32)):
        nf = rot // 4
        inv = (np.float32(10000.0) ** (-np.arange(nf, dtype=np.float32) / np.float32(nf))).astype(np.float32)
        ang = np.concatenate([(tok // 64)[:, None].astype(np.float32) * inv,
                              (tok % 64)[:, None].astype(np.float32) * inv], 1)
        for f, n in ((np.cos, "cos"), (np.sin, "sin")):
            c[n + name] = f(ang).reshape(2, P, rot // 2).transpose(1, 0, 2).reshape(P, -1)
    return np.ascontiguousarray(np.concatenate([c[n].astype(np.float32) for n in CONST], 1))


def kernel(x, c, ctx, c_ctx, ada_w, ada_b, ev_w_in, ev_w_out, diff_q_norm, diff_k_norm,
           diff_lam_q1, diff_lam_k1, diff_lam_q2, diff_lam_k2, diff_subln, mla_cq_norm, mla_ckv_norm,
           mla_w_uq, mla_w_ukv, mla_q_norm, mla_k_norm, dn_w_in, dn_conv, dn_a_log, dn_dt_bias,
           dn_o_norm, dn_w_out, peer_wq, peer_k1, peer_k2, peer_u, peer_v):
    import numpy as np
    import concourse.bacc as _bacc
    from concourse import mybir as _mybir
    from concourse.bass_utils import run_bass_kernel_spmd as _run

    cc = np.ascontiguousarray

    def chunks(w):
        n = -(-w.shape[1] // WCH)
        full = np.zeros((D, n * WCH), w.dtype)
        full[:, :w.shape[1]] = w
        return full.reshape(KD, P, n, WCH).transpose(2, 1, 0, 3)

    c2 = np.stack([np.asarray(c_ctx), np.asarray(c)[0]], 0)
    rows = [np.asarray(v).reshape(-1) for v in (
        diff_q_norm, diff_k_norm, diff_subln, mla_cq_norm, mla_ckv_norm, mla_q_norm, mla_k_norm, dn_o_norm,
        diff_lam_q1, diff_lam_k1, diff_lam_q2, diff_lam_k2, dn_a_log, dn_dt_bias)]
    keysT = np.stack([np.asarray(peer_k1), np.asarray(peer_k2)], 1)
    dn = np.asarray(dn_w_in)[0]
    wq = np.asarray(peer_wq)
    aw = np.asarray(ada_w)
    arrays = {
        "x": cc(x), "ctx_in": cc(ctx),
        "cT": cc(c2.reshape(2, KD, P).transpose(2, 1, 0).reshape(P, 2 * KD)),
        "ada_b": cc(ada_b),
        "wstream": cc(np.concatenate([chunks(aw[0]), chunks(np.asarray(ev_w_in)[0])[[3, 0, 1, 2]], chunks(aw[1]), chunks(np.asarray(ev_w_out)[0]), chunks(wq[0]),
                                      chunks(dn[:, :4096]), chunks(np.asarray(dn_w_out)[0]), chunks(wq[1])], 0)),
        "small": cc(np.broadcast_to(np.concatenate(rows)[None, :], (P, SMALL_W))),
        "consts": _shape_constants(),
        "keysT": cc(keysT.transpose(3, 0, 1, 2)),
        "w_uq": cc(np.asarray(mla_w_uq)[0].reshape(2, P, 384).transpose(1, 0, 2).reshape(P, 768)),
        "w_ukv": cc(np.asarray(mla_w_ukv)[0]),
        "conv_w": cc(np.asarray(dn_conv)[0].reshape(5, 24, P).transpose(2, 1, 0)),
        "w_ab": cc(dn[:, 4096:].reshape(KD, P, 32).transpose(1, 0, 2)),
        "peer_u0": np.asarray(peer_u)[0], "peer_v0": np.asarray(peer_v)[0],
        "peer_u1": np.asarray(peer_u)[1], "peer_v1": np.asarray(peer_v)[1],
    }
    nc = _bacc.Bacc("TRN2", target_bir_lowering=False, num_devices=1)
    args = {n: nc.dram_tensor(f"in_{n}_dram", a.shape, _mybir.dt.from_np(a.dtype), kind="ExternalInput").ap()
            for n, a in arrays.items()}
    shape = (1, 256, D) if STOP >= 4 else (NT, P, D)
    out = nc.dram_tensor("out_0_dram", shape, _mybir.dt.float32, kind="ExternalOutput").ap()
    build(nc, out=out, stop=STOP, **args)
    r = _run(nc, [{f"in_{n}_dram": a for n, a in arrays.items()}], core_ids=[0])
    return r.results[0]["out_0_dram"]
```
